# Optimizing a Trainium2 kernel written in Bass

```python
import math
import jax, jax.numpy as jnp
from jax import lax
import numpy as np

D_MODEL = 1024
BATCH = 1
SEQ = 512
DEPTH = 1

LRU_HEADS = 8
LRU_BLOCK = D_MODEL // 8
D_LRU = LRU_HEADS * LRU_BLOCK
CONV_GROUPS = 4
D_CONV = CONV_GROUPS * (D_MODEL // 8)
D_MIX = D_LRU + D_CONV
D_IN = 2 * D_LRU + 3 * D_CONV
IN_SPLITS = (D_LRU, 2 * D_LRU, 2 * D_LRU + D_CONV, 2 * D_LRU + 2 * D_CONV)
LRU_CONV_W = 4
LRU_PADS = ((LRU_CONV_W - 1, 0), (0, LRU_CONV_W - 1))
LRU_C = 8.0
SHORT_CONV_W = 3

PEER_HEADS = 8
PEER_QDIM = 256
PEER_HALF = PEER_QDIM // 2
N_KEYS = 128
N_EXPERTS = N_KEYS * N_KEYS
PEER_TOPK = 16
PEER_CHUNK = 128

LN_EPS = 1e-5
RMS_EPS = 1e-6
ALPHA = (2.0 * DEPTH) ** 0.25
BETA = (8.0 * DEPTH) ** -0.25

kernel_name = "hymba_griffin_shortconv_peer_encoder_block"

def layer_norm(x, g, b):
    xf = x.astype(jnp.float32)
    mu = jnp.mean(xf, axis=-1, keepdims=True)
    var = jnp.mean(jnp.square(xf - mu), axis=-1, keepdims=True)
    y = (xf - mu) * lax.rsqrt(var + LN_EPS) * g.astype(jnp.float32) + b.astype(jnp.float32)
    return y.astype(x.dtype)

def rms_norm(x, g):
    xf = x.astype(jnp.float32)
    y = xf * lax.rsqrt(jnp.mean(jnp.square(xf), axis=-1, keepdims=True) + RMS_EPS) * g.astype(jnp.float32)
    return y.astype(x.dtype)

def depthwise_conv(x, w, pad):
    c = x.shape[-1]
    return lax.conv_general_dilated(
        x, w[:, None, :].astype(x.dtype), window_strides=(1,), padding=[pad],
        dimension_numbers=("NWC", "WIO", "NWC"), feature_group_count=c)

def block_diag_linear(x, w, b):
    bsz, s, d = x.shape
    xh = x.reshape(bsz, s, LRU_HEADS, LRU_BLOCK)
    y = jnp.einsum("bshi,hij->bshj", xh, w.astype(x.dtype)).reshape(bsz, s, d)
    return y + b.astype(x.dtype)

def _linear_recurrence_combine(left, right):
    a_l, b_l = left
    a_r, b_r = right
    return a_l * a_r, a_r * b_l + b_r

def rg_lru(xc, w_a, b_a, w_x, b_x, lam, reverse):
    r = jax.nn.sigmoid(block_diag_linear(xc, w_a, b_a).astype(jnp.float32))
    i = jax.nn.sigmoid(block_diag_linear(xc, w_x, b_x).astype(jnp.float32))
    log_a = -LRU_C * r * jax.nn.softplus(-lam.astype(jnp.float32))
    a = jnp.exp(log_a)
    u = jnp.sqrt(-jnp.expm1(2.0 * log_a)) * (i * xc.astype(jnp.float32))
    if reverse:
        a = jnp.flip(a, axis=1)
        u = jnp.flip(u, axis=1)
    _, h = lax.associative_scan(_linear_recurrence_combine, (a, u), axis=1)
    if reverse:
        h = jnp.flip(h, axis=1)
    return h.astype(xc.dtype)

def peer(x, w_q, k1, k2, u_tab, v_tab):
    bsz, s, d = x.shape
    t = bsz * s
    xt = x.reshape(t, d)
    q = (xt @ w_q.astype(x.dtype)).reshape(t, PEER_HEADS, 2, PEER_HALF)
    s1 = jnp.einsum("thd,kd->thk", q[:, :, 0], k1.astype(x.dtype)).astype(jnp.float32)
    s2 = jnp.einsum("thd,kd->thk", q[:, :, 1], k2.astype(x.dtype)).astype(jnp.float32)
    v1, i1 = lax.top_k(s1, PEER_TOPK)
    v2, i2 = lax.top_k(s2, PEER_TOPK)
    cand_s = (v1[..., :, None] + v2[..., None, :]).reshape(t, PEER_HEADS, PEER_TOPK * PEER_TOPK)
    cand_i = (i1[..., :, None] * N_KEYS + i2[..., None, :]).reshape(t, PEER_HEADS, PEER_TOPK * PEER_TOPK)
    top_s, pos = lax.top_k(cand_s, PEER_TOPK)
    idx = jnp.take_along_axis(cand_i, pos, axis=-1)
    g = jax.nn.softmax(top_s, axis=-1)

    n_blocks = t // PEER_CHUNK
    e_per_tok = PEER_HEADS * PEER_TOPK
    xb_all = xt.reshape(n_blocks, PEER_CHUNK, d)
    ib_all = idx.reshape(n_blocks, PEER_CHUNK, e_per_tok)
    gb_all = g.reshape(n_blocks, PEER_CHUNK, e_per_tok).astype(x.dtype)

    def expert_block(args):
        xb, ib, gb = args
        u = u_tab[ib].astype(x.dtype)
        act = jax.nn.gelu(jnp.einsum("cd,ced->ce", xb, u), approximate=False)
        v = v_tab[ib].astype(x.dtype)
        return jnp.einsum("ce,ced->cd", gb * act, v)

    y = lax.map(expert_block, (xb_all, ib_all, gb_all))
    return y.reshape(bsz, s, d)

def setup_inputs(seed: int = 0) -> dict:
    key = jax.random.key(seed)
    ks = jax.random.split(key, 28)
    f32 = jnp.float32
    L = DEPTH

    def nrm(k, shape, scale):
        return jax.random.normal(k, shape, f32) * scale

    a0 = jax.random.uniform(ks[10], (L, 2, D_LRU), f32, minval=0.9, maxval=0.999)
    p = a0 ** (1.0 / LRU_C)
    lam = jnp.log(p) - jnp.log1p(-p)

    return {
        "x": nrm(ks[0], (BATCH, SEQ, D_MODEL), 1.0),
        "ln_emb_g": 1.0 + nrm(ks[1], (D_MODEL,), 0.02),
        "ln_emb_b": nrm(ks[2], (D_MODEL,), 0.02),
        "w_in": nrm(ks[3], (L, D_MODEL, D_IN), D_MODEL ** -0.5),
        "lru_conv_w": nrm(ks[4], (L, 2, LRU_CONV_W, D_LRU), LRU_CONV_W ** -0.5),
        "lru_conv_b": nrm(ks[5], (L, 2, D_LRU), 0.01),
        "lru_wa": nrm(ks[6], (L, 2, LRU_HEADS, LRU_BLOCK, LRU_BLOCK), LRU_BLOCK ** -0.5),
        "lru_ba": nrm(ks[7], (L, 2, D_LRU), 0.01),
        "lru_wx": nrm(ks[8], (L, 2, LRU_HEADS, LRU_BLOCK, LRU_BLOCK), LRU_BLOCK ** -0.5),
        "lru_bx": nrm(ks[9], (L, 2, D_LRU), 0.01),
        "lru_lambda": lam,
        "conv_w": nrm(ks[11], (L, SHORT_CONV_W, D_CONV), SHORT_CONV_W ** -0.5),
        "norm_lru_g": 1.0 + nrm(ks[12], (L, D_LRU), 0.02),
        "norm_conv_g": 1.0 + nrm(ks[13], (L, D_CONV), 0.02),
        "w_out": nrm(ks[14], (L, D_MIX, D_MODEL), BETA * D_MIX ** -0.5),
        "ln1_g": 1.0 + nrm(ks[15], (L, D_MODEL), 0.02),
        "ln1_b": nrm(ks[16], (L, D_MODEL), 0.02),
        "peer_wq": nrm(ks[17], (L, D_MODEL, PEER_HEADS * PEER_QDIM), D_MODEL ** -0.5),
        "peer_k1": nrm(ks[18], (L, N_KEYS, PEER_HALF), PEER_HALF ** -0.5),
        "peer_k2": nrm(ks[19], (L, N_KEYS, PEER_HALF), PEER_HALF ** -0.5),
        "peer_u": nrm(ks[20], (L, N_EXPERTS, D_MODEL), D_MODEL ** -0.5),
        "peer_v": nrm(ks[21], (L, N_EXPERTS, D_MODEL), BETA),
        "ln2_g": 1.0 + nrm(ks[22], (L, D_MODEL), 0.02),
        "ln2_b": nrm(ks[23], (L, D_MODEL), 0.02),
    }

def reference(x, ln_emb_g, ln_emb_b, w_in, lru_conv_w, lru_conv_b, lru_wa, lru_ba, lru_wx, lru_bx,
              lru_lambda, conv_w, norm_lru_g, norm_conv_g, w_out, ln1_g, ln1_b,
              peer_wq, peer_k1, peer_k2, peer_u, peer_v, ln2_g, ln2_b):
    h = layer_norm(x, ln_emb_g, ln_emb_b)
    for l in range(DEPTH):
        z = h @ w_in[l].astype(h.dtype)
        xr, gate, cb, cc, cx = jnp.split(z, IN_SPLITS, axis=-1)
        lru = None
        for d, pad in enumerate(LRU_PADS):
            xc = depthwise_conv(xr, lru_conv_w[l, d], pad) + lru_conv_b[l, d].astype(xr.dtype)
            hd = rg_lru(xc, lru_wa[l, d], lru_ba[l, d], lru_wx[l, d], lru_bx[l, d],
                        lru_lambda[l, d], reverse=(d == 1))
            lru = hd if lru is None else lru + hd
        y_lru = jax.nn.gelu(gate) * lru
        y_conv = cb * depthwise_conv(cc * cx, conv_w[l], (1, 1))
        mix = jnp.concatenate([rms_norm(y_lru, norm_lru_g[l]),
                               rms_norm(y_conv, norm_conv_g[l])], axis=-1)
        h = layer_norm(ALPHA * h + mix @ w_out[l].astype(h.dtype), ln1_g[l], ln1_b[l])
        f = peer(h, peer_wq[l], peer_k1[l], peer_k2[l], peer_u[l], peer_v[l])
        h = layer_norm(ALPHA * h + f, ln2_g[l], ln2_b[l])
    return h


_drawn_inputs = setup_inputs


def setup_inputs(seed=0):
    import zlib

    import numpy as np

    out = dict(_drawn_inputs(seed))
    spreads = {}
    factors = {'lru_ba': 20.279, 'lru_bx': 6.741, 'norm_conv_g': 2.694, 'ln2_g': 7.967, 'ln2_b': 8.217}
    for name, (base, spread) in spreads.items():
        noise = np.random.default_rng([zlib.crc32(name.encode()), seed]).standard_normal(out[name].shape)
        drawn = base * np.exp(spread * noise) if base else spread * noise
        out[name] = __import__('jax').numpy.asarray(drawn.astype(out[name].dtype))
    for name, factor in factors.items():
        out[name] = (out[name] * factor).astype(out[name].dtype)
    return out
```

```python
from contextlib import ExitStack

import numpy as np
import concourse.bass as bass
from concourse import mybir

F32 = mybir.dt.float32
F32R = mybir.dt.float32r
BF16 = mybir.dt.bfloat16
U32 = mybir.dt.uint32
ALU = mybir.AluOpType
ACT = mybir.ActivationFunctionType
AX = mybir.AxisListType

P = 128
T, D = 512, 1024
TB, KD = T // P, D // P
HALF_D = D // 2
HEADS = 8
CONV = 4
MIX = HEADS + CONV
D_IN = 2 * D + 3 * CONV * P
LRU_W, SHORT_W = 4, 3
PAD = LRU_W - 1
LRU_C = 8.0
QH, TOPK = 8, 16
KEYS = 128
SLOTS = QH * TOPK
LN_EPS, RMS_EPS = 1e-5, 1e-6
ALPHA = 2.0 ** 0.25
NEG = -3.0e38

PC_CONVW, PC_CONVB, PC_BA, PC_BX, PC_LAM = 0, 64, 80, 96, 112
PC_SHORT, PC_GLRU, PC_GCONV = 0, 12, 20

COL_X, COL_GATE, COL_CB, COL_CC, COL_CX = 0, HEADS, 2 * HEADS, 2 * HEADS + CONV, 2 * HEADS + 2 * CONV


class Chain:

    def __init__(self, eng, sem):
        self.eng, self.sem, self.n = eng, sem, 0

    def __call__(self, ins):
        self.n += 1
        ins.then_inc(self.sem, 1)
        self.eng.wait_ge(self.sem, self.n)


def after(eng, sem, count):
    if not isinstance(count, int) or count > 0:
        eng.wait_ge(sem, count)


def build(nc, a, out, gates_dram):
    ctx = ExitStack()
    with ctx:
        sem = lambda name: ctx.enter_context(nc.semaphore(name))
        sb = lambda name, shape, dt=F32: ctx.enter_context(nc.sbuf_tensor(name, shape, dt))
        bank = [ctx.enter_context(nc.psum_tensor(f"bank{i}", [P, 512], F32)) for i in range(8)]
        h = sb("h", [P, TB, D])
        ident = sb("ident", [P, P])
        ones = sb("ones", [P, P])
        iota = sb("iota", [P, KEYS])
        small = sb("small", [P, 8])
        mixer(nc, a, sem, bank, h, ident, ones, iota, small)
        xhi = sb("xhi", [P, KD, T], F32R)
        xlo = sb("xlo", [P, KD, T], F32R)
        with ExitStack() as rs:
            rb = lambda name, shape, dt=F32: rs.enter_context(nc.sbuf_tensor(name, shape, dt))
            top = rb("top", [P, TB, QH, TOPK])
            pos = rb("pos", [P, TB, QH, TOPK], U32)
            key = rb("key", [P, TB, QH, 2, TOPK], U32)
            queries(nc, a, sem, bank, h, ident, xhi, xlo, top, pos, key)
            gates(nc, sem, bank, ident, iota, top, pos, key, gates_dram)
        experts(nc, a, sem, bank, h, ident, small, xhi, xlo, gates_dram, out)


def mixer(nc, a, sem, bank, h, ident, ones, iota, small):
    V, S, G = nc.vector, nc.scalar, nc.gpsimd
    with ExitStack() as st:
        sb = lambda name, shape, dt=F32: st.enter_context(nc.sbuf_tensor(name, shape, dt))
        hT = sb("hT", [P, KD, T])
        NW = 4
        wbuf = [sb(f"w_in{i}", [P, KD, P]) for i in range(NW)]
        wa = sb("wa", [P, 2 * HEADS, P])
        wx = sb("wx", [P, 2 * HEADS, P])
        wo = sb("wo", [P, MIX, D])
        y = sb("y", [P, MIX, T])
        ln = sb("ln", [P, 4, D])
        prow = sb("prow", [P, 2, P])
        pA = sb("pA", [P, P])
        pB = sb("pB", [P, 24])
        hb = sb("hb", [P, 32])
        sp = sb("sp", [P, 2, 16])
        t16 = sb("t16", [P, 8, 16])
        xp = sb("xp", [P, 2, T + 2 * PAD])
        xc = sb("xc", [P, 2, 2, T])
        th = sb("th", [P, 2, 2, T])
        da = sb("da", [P, 2, T])
        dw = sb("dw", [P, 2, T])
        dq = sb("dq", [P, 2, T])
        dr = sb("dr", [P, T])
        hd = sb("hd", [P, 2, T])
        sq = sb("sq", [P, 2, T])
        rstd = sb("rstd", [P, 2, T])
        bn = sb("bn", [P, TB, 2, 6])
        mv = sb("mv", [P, TB, 2])
        rs = sb("rs", [P, TB, 1])

        x_loaded = [sem(f"x_loaded{i}") for i in range(TB)]
        w_loaded = [sem(f"w_loaded{i}") for i in range(NW)]
        wo_loaded, ln_loaded, p_loaded, g_loaded = (sem(n) for n in (
            "wo_loaded", "ln_loaded", "params_loaded", "gate_weights_loaded"))
        consts_ready, pT_ready, p_ready, sp_ready, exp_lam = (sem(n) for n in (
            "consts_ready", "params_transposed", "params_ready", "softplus_ready", "exp_lambda"))
        var_ready, rstd_ready, norm_ready, h_ready = (sem(n) for n in (
            "var_ready", "rstd_ready", "norm_ready", "h_ready"))
        ht_done, ht_ready = sem("h_transposed"), sem("hT_ready")
        z_done, z_used_act, z_used_dve = sem("z_done"), sem("z_used_act"), sem("z_used_dve")
        xp_ready, xc_ready, gates_done, tanh_ready = (sem(n) for n in (
            "xp_ready", "xc_ready", "gates_done", "tanh_ready"))
        decay_ready, q_ready, root_ready, y_ready, sq_ready, sums_done = (sem(n) for n in (
            "decay_ready", "q_ready", "root_ready", "y_ready", "squares_ready", "sums_done"))
        cc_ready, rms_root, mix_ready, o_done = (sem(n) for n in (
            "cc_ready", "rms_root_ready", "mix_ready", "out_projection_done"))
        xp_zero, o_used = sem("xp_zero"), sem("out_projection_used")
        dve_chain, pool_chain, act_chain = sem("dve_chain"), sem("pool_chain"), sem("act_chain")

        order = [COL_GATE + i for i in range(HEADS)] + [COL_X + i for i in range(HEADS)]
        for j in range(CONV):
            order += [COL_CC + j, COL_CX + j, COL_CB + j]
        HX, HC = HEADS, 2 * HEADS
        by_dve = [n >= HC and (n - HC) % 3 > 0 for n in range(len(order))]
        n_act = lambda n: sum(not b for b in by_dve[:n + 1])
        n_dve = lambda n: sum(by_dve[:n + 1])

        with nc.Block() as block:
            @block.sync
            def _(sp_eng):
                eng = sp_eng
                for tb in range(TB):
                    eng.dma_start(h[:, tb, :], a["x"][0, tb * P:(tb + 1) * P, :]).then_inc(x_loaded[tb], 16)
                for n, c in enumerate(order):
                    if n >= NW:
                        eng.wait_ge(z_done, n - NW + 1)
                    eng.dma_start(wbuf[n % NW][:, :, :],
                                  a["w_in"][0, :, c * P:(c + 1) * P].rearrange("(k p) c -> p k c", p=P)
                                  ).then_inc(w_loaded[n % NW], 16)
                    if n == 12:
                        eng.dma_start(wo[:, :, :], a["w_out"][0].rearrange("(k p) n -> p k n", p=P)
                                      ).then_inc(wo_loaded, 16)

            @block.gpsimd
            def _(eng):
                link = Chain(eng, pool_chain)
                G.memset(ones[:, :], 1.0)
                link(G.memset(ident[:, :], 0.0))
                link(G.affine_select(out=ident[:, :], in_=ident[:, :], compare_op=ALU.not_equal, fill=1.0,
                                     base=0, pattern=[[-1, P]], channel_multiplier=1))
                G.iota(iota[:, :], [[1, KEYS]], base=0, channel_multiplier=0,
                       allow_small_or_imprecise_dtypes=True)
                G.memset(small[:, 0:1], -0.5)
                G.memset(small[:, 1:2], RMS_EPS)
                G.memset(small[:, 2:3], LN_EPS).then_inc(consts_ready, 1)
                eng.wait_ge(consts_ready, 1)
                G.memset(xp[:, :, :], 0.0).then_inc(xp_zero, 1)
                for half in range(2):
                    for tb in range(TB):
                        eng.wait_ge(var_ready, half * TB + tb + 1)
                        link(G.tensor_tensor(out=rs[:, tb, :], in0=mv[:, tb, 1:2], in1=small[:, 2:3], op=ALU.add))
                        G.tensor_tensor(out=rs[:, tb, :], in0=rs[:, tb, :], in1=small[:, 0:1],
                                        op=ALU.pow).then_inc(rstd_ready, 1)
                        eng.wait_ge(norm_ready, half * TB + tb + 1)
                        if tb == 0 and half == 0:
                            eng.wait_ge(ln_loaded, 64)
                        link(G.tensor_tensor(out=h[:, tb, :], in0=h[:, tb, :], in1=ln[:, 2 * half, :], op=ALU.mult))
                        G.tensor_tensor(out=h[:, tb, :], in0=h[:, tb, :], in1=ln[:, 2 * half + 1, :],
                                        op=ALU.add).then_inc(h_ready, 1)

            @block.scalar
            def _(eng):
                rows = lambda r0, n, src: eng.dma_start(prow[r0 % P:r0 % P + n, r0 // P, :], src).then_inc(p_loaded, 16)
                rows(PC_CONVW, 64, a["lru_conv_w"][0].rearrange("d k (h p) -> (d k h) p", p=P))
                rows(PC_CONVB, 16, a["lru_conv_b"][0].rearrange("d (h p) -> (d h) p", p=P))
                rows(PC_BA, 16, a["lru_ba"][0].rearrange("d (h p) -> (d h) p", p=P))
                rows(PC_BX, 16, a["lru_bx"][0].rearrange("d (h p) -> (d h) p", p=P))
                rows(PC_LAM, 16, a["lru_lambda"][0].rearrange("d (h p) -> (d h) p", p=P))
                rows(P + PC_SHORT, 12, a["conv_w"][0].rearrange("k (h p) -> (k h) p", p=P))
                rows(P + PC_GLRU, 8, a["norm_lru_g"][0].rearrange("(h p) -> h p", p=P))
                rows(P + PC_GCONV, 4, a["norm_conv_g"][0].rearrange("(h p) -> h p", p=P))
                for i, name in enumerate(("ln_emb_g", "ln_emb_b", "ln1_g", "ln1_b")):
                    v = a[name] if i < 2 else a[name][0]
                    eng.dma_start(ln[:, i, :], v.partition_broadcast(P)).then_inc(ln_loaded, 16)
                eng.dma_start(wa[:, :, :], a["lru_wa"][0].rearrange("d h i j -> i (d h) j")).then_inc(g_loaded, 16)
                eng.dma_start(wx[:, :, :], a["lru_wx"][0].rearrange("d h i j -> i (d h) j")).then_inc(g_loaded, 16)
                link = Chain(eng, act_chain)
                eng.wait_ge(pT_ready, 1)
                S.activation(pA[:, :], bank[4][:, 0:P], ACT.Copy)
                S.activation(pB[:, :], bank[4][:, P:P + 24], ACT.Copy).then_inc(p_ready, 1)
                eng.wait_ge(exp_lam, 1)
                S.activation(t16[:, 2, :], t16[:, 1, :], ACT.Exp, scale=-1.0).then_inc(exp_lam, 1)
                for i in range(2 * TB):
                    tb, half = i // 2, i % 2
                    eng.wait_ge(ht_done, i + 1)
                    S.activation(hT[:, 4 * half:4 * half + 4, tb * P:(tb + 1) * P],
                                 bank[i % 2].rearrange("p (k t) -> p k t", k=4), ACT.Copy).then_inc(ht_ready, 1)
                for n in range(HEADS):
                    eng.wait_ge(z_done, n + 1)
                    S.activation(y[:, n, :], bank[n % 2][:, :], ACT.Gelu_apprx_tanh).then_inc(z_used_act, 1)

                def squares(i):
                    eng.wait_ge(y_ready, i + 1)
                    after(eng, sums_done, i - 1)
                    S.activation(sq[:, i % 2, :], y[:, i, :], ACT.Square).then_inc(sq_ready, 1)

                for hd_i in range(HEADS + 1):
                    if hd_i < HEADS:
                        eng.wait_ge(z_done, HX + hd_i + 1)
                        if hd_i == 0:
                            eng.wait_ge(xp_zero, 1)
                        after(eng, xc_ready, 2 * (hd_i - 1))
                        S.activation(xp[:, hd_i % 2, PAD:PAD + T], bank[(HX + hd_i) % 2][:, :],
                                     ACT.Copy).then_inc(z_used_act, 1)
                    if hd_i == 0:
                        eng.wait_ge(sp_ready, 1)
                        continue
                    g = hd_i - 1
                    for d in range(2):
                        c = d * HEADS + g
                        eng.wait_ge(gates_done, 2 * g + d + 1)
                        after(eng, y_ready, g)
                        S.activation(th[:, d, 0, :], bank[4 + 2 * d][:, :], ACT.Tanh, scale=0.5, bias=hb[:, c:c + 1])
                        link(S.activation(th[:, d, 1, :], bank[5 + 2 * d][:, :], ACT.Tanh, scale=0.5,
                                          bias=hb[:, 16 + c:17 + c]))
                        S.activation(dw[:, d, :], th[:, d, 0, :], ACT.Tanh, scale=sp[:, 0, c:c + 1],
                                     bias=sp[:, 0, c:c + 1]).then_inc(tanh_ready, 1)
                        S.activation(da[:, d, :], th[:, d, 0, :], ACT.Exp, scale=sp[:, 1, c:c + 1],
                                     bias=sp[:, 1, c:c + 1]).then_inc(decay_ready, 1)
                    for d in range(2):
                        eng.wait_ge(q_ready, 2 * g + d + 1)
                        S.activation(dq[:, d, :], dq[:, d, :], ACT.Sqrt, scale=0.5).then_inc(root_ready, 1)
                    if g > 0:
                        squares(g - 1)
                squares(HEADS - 1)
                for j in range(CONV):
                    n = HC + 3 * j
                    eng.wait_ge(z_done, n + 1)
                    after(eng, y_ready, HEADS + j)
                    S.activation(dr[:, :], bank[n % 2][:, :], ACT.Copy).then_inc(z_used_act, 1)
                    squares(HEADS + j)
                for i in range(2):
                    eng.wait_ge(sums_done, MIX)
                    S.activation(rstd[:, i, :], bank[2 + i][:, :], ACT.Sqrt, scale=1.0 / (P * (HEADS, CONV)[i]),
                                 bias=small[:, 1:2]).then_inc(rms_root, 1)

            @block.vector
            def _(eng):
                link = Chain(eng, dve_chain)

                def stats(tb):
                    for i in range(2):
                        ins = V.bn_stats(bn[:, tb, i, :], h[:, tb, i * HALF_D:(i + 1) * HALF_D])
                    link(ins)
                    V.bn_aggr(mv[:, tb, :], bn[:, tb, :, :].rearrange("p a b -> p (a b)")).then_inc(var_ready, 1)

                def normalise(n, tb):
                    eng.wait_ge(rstd_ready, n)
                    V.tensor_scalar(out=h[:, tb, :], in0=h[:, tb, :], scalar1=mv[:, tb, 0:1], scalar2=rs[:, tb, :],
                                    op0=ALU.subtract, op1=ALU.mult).then_inc(norm_ready, 1)

                eng.wait_ge(consts_ready, 1)
                for tb in range(TB):
                    eng.wait_ge(x_loaded[tb], 16)
                    stats(tb)
                    if tb:
                        normalise(tb, tb - 1)
                normalise(TB, TB - 1)

                eng.wait_ge(p_ready, 1)
                neg, mag, e, s, s2, poly = (t16[:, i, :] for i in range(6))
                V.tensor_scalar(out=hb[:, :], in0=pA[:, PC_BA:PC_BA + 32], scalar1=0.5, scalar2=None, op0=ALU.mult)
                link(V.tensor_scalar(out=neg, in0=pA[:, PC_LAM:PC_LAM + 16], scalar1=-1.0, scalar2=None, op0=ALU.mult))
                V.tensor_tensor(out=mag, in0=neg, in1=pA[:, PC_LAM:PC_LAM + 16], op=ALU.max).then_inc(exp_lam, 1)
                eng.wait_ge(exp_lam, 2)
                link(V.tensor_scalar(out=s, in0=e, scalar1=2.0, scalar2=None, op0=ALU.add))
                link(V.reciprocal(s, s))
                link(V.tensor_tensor(out=s, in0=s, in1=e, op=ALU.mult))
                link(V.tensor_tensor(out=s2, in0=s, in1=s, op=ALU.mult))
                link(V.tensor_scalar(out=poly, in0=s2, scalar1=1.0 / 15, scalar2=1.0 / 13, op0=ALU.mult, op1=ALU.add))
                for k in (11, 9, 7, 5, 3, 1):
                    link(V.tensor_tensor(out=poly, in0=poly, in1=s2, op=ALU.mult))
                    link(V.tensor_scalar(out=poly, in0=poly, scalar1=1.0 / k, scalar2=None, op0=ALU.add))
                link(V.tensor_tensor(out=poly, in0=poly, in1=s, op=ALU.mult))
                link(V.tensor_scalar(out=neg, in0=neg, scalar1=0.0, scalar2=LRU_C / 2, op0=ALU.max, op1=ALU.mult))
                link(V.scalar_tensor_tensor(out=sp[:, 0, :], in0=poly, scalar=LRU_C, in1=neg, op0=ALU.mult, op1=ALU.add))
                V.tensor_scalar(out=sp[:, 1, :], in0=sp[:, 0, :], scalar1=-1.0, scalar2=None,
                                op0=ALU.mult).then_inc(sp_ready, 1)

                for hd_i in range(HEADS + 1):
                    if hd_i < HEADS:
                        eng.wait_ge(z_used_act, n_act(HX + hd_i))
                        x0 = xp[:, hd_i % 2, :]
                        after(eng, gates_done, 2 * (hd_i - 1))
                        for k in range(LRU_W):
                            for d in range(2):
                                c = d * HEADS + hd_i
                                w = pA[:, PC_CONVW + (d * LRU_W + k) * HEADS + hd_i:][:, 0:1]
                                o, src = xc[:, hd_i % 2, d, :], x0[:, d * PAD + k:d * PAD + k + T]
                                if k == 0:
                                    ins = V.tensor_scalar(out=o, in0=src, scalar1=w,
                                                          scalar2=pA[:, PC_CONVB + c:PC_CONVB + c + 1],
                                                          op0=ALU.mult, op1=ALU.add)
                                else:
                                    ins = V.scalar_tensor_tensor(out=o, in0=src, scalar=w, in1=o,
                                                                 op0=ALU.mult, op1=ALU.add)
                                if k == LRU_W - 1:
                                    ins.then_inc(xc_ready, 1)
                            if k < LRU_W - 1:
                                link(ins)
                    if hd_i == 0:
                        continue
                    g = hd_i - 1
                    for d in range(2):
                        eng.wait_ge(tanh_ready, 2 * g + d + 1)
                        link(V.tensor_scalar(out=dq[:, d, :], in0=dw[:, d, :], scalar1=1.0, scalar2=None, op0=ALU.add))
                        link(V.reciprocal(dq[:, d, :], dq[:, d, :]))
                        V.tensor_tensor(out=dq[:, d, :], in0=dq[:, d, :], in1=dw[:, d, :],
                                        op=ALU.mult).then_inc(q_ready, 1)
                        link(V.scalar_tensor_tensor(out=th[:, d, 1, :], in0=th[:, d, 1, :], scalar=1.0,
                                                    in1=xc[:, g % 2, d, :], op0=ALU.add, op1=ALU.mult))
                    for d in range(2):
                        eng.wait_ge(root_ready, 2 * g + d + 1)
                        eng.wait_ge(decay_ready, 2 * g + d + 1)
                        link(V.tensor_tensor(out=dq[:, d, :], in0=dq[:, d, :], in1=th[:, d, 1, :], op=ALU.mult))
                        along = slice(None) if d == 0 else slice(None, None, -1)
                        ins = V.tensor_tensor_scan(out=hd[:, d, along], data0=da[:, d, along],
                                                   data1=dq[:, d, along], initial=0.0, op0=ALU.mult, op1=ALU.add)
                    link(ins)
                    link(V.tensor_tensor(out=hd[:, 0, :], in0=hd[:, 0, :], in1=hd[:, 1, :], op=ALU.add))
                    V.tensor_tensor(out=y[:, g, :], in0=y[:, g, :], in1=hd[:, 0, :], op=ALU.mult).then_inc(y_ready, 1)
                for j in range(CONV):
                    n = HC + 3 * j
                    prod, acc = xp[:, 0, PAD:PAD + T], hd[:, 0, :]
                    eng.wait_ge(z_used_act, n_act(n))
                    eng.wait_ge(z_done, n + 2)
                    ins = V.tensor_tensor(out=prod, in0=dr[:, :], in1=bank[(n + 1) % 2][:, :], op=ALU.mult)
                    link(ins)
                    V.sem_inc(z_used_dve, 1)
                    for k in range(SHORT_W):
                        w = pB[:, PC_SHORT + k * CONV + j:][:, 0:1]
                        src = xp[:, 0, PAD - 1 + k:PAD - 1 + k + T]
                        if k == 0:
                            link(V.tensor_scalar(out=acc, in0=src, scalar1=w, scalar2=None, op0=ALU.mult))
                        else:
                            link(V.scalar_tensor_tensor(out=acc, in0=src, scalar=w, in1=acc, op0=ALU.mult, op1=ALU.add))
                    eng.wait_ge(z_done, n + 3)
                    link(V.tensor_tensor(out=y[:, HEADS + j, :], in0=acc, in1=bank[(n + 2) % 2][:, :], op=ALU.mult))
                    V.sem_inc(z_used_dve, 1)
                    V.sem_inc(y_ready, 1)
                for i in range(2):
                    eng.wait_ge(rms_root, i + 1)
                    link(V.reciprocal(rstd[:, i, :], rstd[:, i, :]))
                for c in range(MIX):
                    gain = pB[:, PC_GLRU + c:PC_GLRU + c + 1]
                    V.scalar_tensor_tensor(out=y[:, c, :], in0=y[:, c, :], scalar=gain, in1=rstd[:, int(c >= HEADS), :],
                                           op0=ALU.mult, op1=ALU.mult).then_inc(mix_ready, 1)
                eng.wait_ge(h_ready, TB)
                for tb in range(TB):
                    eng.wait_ge(o_done, tb + 1)
                    for i in range(2):
                        blk = h[:, tb, i * HALF_D:(i + 1) * HALF_D]
                        ins = V.scalar_tensor_tensor(out=blk, in0=blk, scalar=ALPHA, in1=bank[4 + 2 * (tb % 2) + i][:, :],
                                                     op0=ALU.mult, op1=ALU.add)
                    link(ins)
                    V.sem_inc(o_used, 1)
                    stats(tb)
                    if tb:
                        normalise(TB + tb, tb - 1)
                normalise(2 * TB, TB - 1)

            @block.tensor
            def _(eng):
                mm = nc.tensor.matmul
                eng.wait_ge(consts_ready, 1)
                eng.wait_ge(p_loaded, 8 * 16)
                nc.tensor.transpose(bank[4][:, 0:P], prow[:, 0, :], ident[:, :])
                nc.tensor.transpose(bank[4][:, P:P + 24], prow[0:24, 1, :], ident[0:24, 0:24]).then_inc(pT_ready, 1)
                for i in range(2 * TB):
                    tb, half = i // 2, i % 2
                    eng.wait_ge(h_ready, tb + 1)
                    after(eng, ht_ready, i - 1)
                    for k in range(4):
                        c = 4 * half + k
                        ins = nc.tensor.transpose(bank[i % 2][:, k * P:(k + 1) * P], h[:, tb, c * P:(c + 1) * P],
                                                  ident[:, :])
                    ins.then_inc(ht_done, 1)
                eng.wait_ge(ht_ready, 2 * TB)

                def z_chunk(n):
                    eng.wait_ge(w_loaded[n % NW], 16 * (n // NW + 1))
                    if n >= 2:
                        if by_dve[n - 2]:
                            eng.wait_ge(z_used_dve, n_dve(n - 2))
                        else:
                            eng.wait_ge(z_used_act, n_act(n - 2))
                    for k in range(KD):
                        ins = mm(bank[n % 2][:, :], wbuf[n % NW][:, k, :], hT[:, k, :], start=(k == 0), stop=(k == KD - 1))
                    ins.then_inc(z_done, 1)

                def head_gates(g):
                    if g == 0:
                        eng.wait_ge(g_loaded, 32)
                    eng.wait_ge(xc_ready, 2 * g + 2)
                    after(eng, decay_ready, 2 * g)
                    for d in range(2):
                        c = d * HEADS + g
                        mm(bank[4 + 2 * d][:, :], wa[:, c, :], xc[:, g % 2, d, :], start=True, stop=True)
                        mm(bank[5 + 2 * d][:, :], wx[:, c, :], xc[:, g % 2, d, :], start=True,
                           stop=True).then_inc(gates_done, 1)

                def sum_squares(i):
                    eng.wait_ge(sq_ready, i + 1)
                    first, last = i in (0, HEADS), i in (HEADS - 1, MIX - 1)
                    mm(bank[2 + int(i >= HEADS)][:, :], ones[:, :], sq[:, i % 2, :], start=first,
                       stop=last).then_inc(sums_done, 1)

                for n in range(HEADS):
                    z_chunk(n)
                for g in range(HEADS):
                    z_chunk(HX + g)
                    if g:
                        head_gates(g - 1)
                    if g > 2:
                        sum_squares(g - 3)
                z_chunk(HC)
                head_gates(HEADS - 1)
                z_chunk(HC + 1)
                sum_squares(HEADS - 3)
                z_chunk(HC + 2)
                sum_squares(HEADS - 2)
                for j in range(1, CONV):
                    for i in range(3):
                        z_chunk(HC + 3 * j + i)
                    sum_squares(HEADS - 2 + j)
                for i in range(HEADS - 2 + CONV, MIX):
                    sum_squares(i)
                eng.wait_ge(wo_loaded, 16)
                for tb in range(TB):
                    after(eng, o_used, tb - 1)
                    for c in range(MIX):
                        if tb == 0:
                            eng.wait_ge(mix_ready, c + 1)
                        for i in range(2):
                            ins = mm(bank[4 + 2 * (tb % 2) + i][:, :], y[:, c, tb * P:(tb + 1) * P],
                                     wo[:, c, i * HALF_D:(i + 1) * HALF_D], start=(c == 0), stop=(c == MIX - 1))
                    ins.then_inc(o_done, 1)


def queries(nc, a, sem, bank, h, ident, xhi, xlo, top, pos, key):
    V, S = nc.vector, nc.scalar
    QC = 2 * QH
    with ExitStack() as st:
        sb = lambda name, shape, dt=F32: st.enter_context(nc.sbuf_tensor(name, shape, dt))
        NW = 4
        x1T = sb("x1T", [P, KD, T])
        wq = [sb(f"wq{i}", [P, KD, P]) for i in range(NW)]
        keys = sb("keys", [P, 2, P])
        keysT = sb("keysT", [P, 2, P])
        qT = sb("qT", [P, 2, T])
        rep = sb("rep", [P, TB, KEYS])
        best = sb("best", [P, 2, TB, TOPK])
        cand = sb("cand", [P, TB, TOPK, TOPK])
        crep = sb("crep", [P, TB, TOPK * TOPK])

        wq_loaded = [sem(f"wq_loaded{i}") for i in range(NW)]
        keys_loaded, kt_done, kt_ready = sem("keys_loaded"), sem("keys_transposed"), sem("keysT_ready")
        t_done, x1_ready, lo_ready = (sem(n) for n in ("x1_transposed", "x1T_ready", "xlo_ready"))
        q_done, qT_ready, s_done, s_used = (sem(n) for n in ("q_done", "qT_ready", "scores_done", "scores_used"))
        chain = sem("dve_chain_queries")

        with nc.Block() as block:
            @block.sync
            def _(eng):
                eng.dma_start(keys[:, 0, :], a["peer_k1"][0]).then_inc(keys_loaded, 16)
                eng.dma_start(keys[:, 1, :], a["peer_k2"][0]).then_inc(keys_loaded, 16)
                for n in range(QC):
                    after(eng, q_done, n - NW + 1)
                    eng.dma_start(wq[n % NW][:, :, :],
                                  a["peer_wq"][0, :, n * P:(n + 1) * P].rearrange("(k p) c -> p k c", p=P)
                                  ).then_inc(wq_loaded[n % NW], 16)

            @block.scalar
            def _(eng):
                eng.wait_ge(kt_done, 1)
                S.activation(keysT[:, :, :], bank[6][:, 0:2 * P].rearrange("p (s k) -> p s k", s=2),
                             ACT.Copy).then_inc(kt_ready, 1)
                for i in range(2 * TB):
                    tb, half = i // 2, i % 2
                    eng.wait_ge(t_done, i + 1)
                    src = bank[half].rearrange("p (k t) -> p k t", k=4)
                    at = (slice(None), slice(4 * half, 4 * half + 4), slice(tb * P, (tb + 1) * P))
                    S.activation(xhi[at], src, ACT.Copy)
                    S.activation(x1T[at], src, ACT.Copy).then_inc(x1_ready, 1)
                for n in range(QC):
                    eng.wait_ge(q_done, n + 1)
                    after(eng, s_done, n - 1)
                    S.activation(qT[:, n % 2, :], bank[2 + n % 2][:, :], ACT.Copy).then_inc(qT_ready, 1)

            @block.tensor
            def _(eng):
                mm, tr = nc.tensor.matmul, nc.tensor.transpose
                eng.wait_ge(keys_loaded, 32)
                tr(bank[6][:, 0:P], keys[:, 0, :], ident[:, :])
                tr(bank[6][:, P:2 * P], keys[:, 1, :], ident[:, :]).then_inc(kt_done, 1)
                for i in range(2 * TB):
                    tb, half = i // 2, i % 2
                    after(eng, lo_ready, i - 1)
                    for k in range(4):
                        c = 4 * half + k
                        ins = tr(bank[half][:, k * P:(k + 1) * P], h[:, tb, c * P:(c + 1) * P], ident[:, :])
                    ins.then_inc(t_done, 1)
                eng.wait_ge(x1_ready, 2 * TB)
                eng.wait_ge(kt_ready, 1)

                def scores(n):
                    eng.wait_ge(qT_ready, n + 1)
                    after(eng, s_used, n - 1)
                    for tb in range(TB):
                        ins = mm(bank[4 + n % 2][:, tb * P:(tb + 1) * P], qT[:, n % 2, tb * P:(tb + 1) * P],
                                 keysT[:, n % 2, :], start=True, stop=True)
                    ins.then_inc(s_done, 1)

                for n in range(QC):
                    eng.wait_ge(wq_loaded[n % NW], 16 * (n // NW + 1))
                    after(eng, qT_ready, n - 1)
                    for k in range(KD):
                        ins = mm(bank[2 + n % 2][:, :], wq[n % NW][:, k, :], x1T[:, k, :], start=(k == 0), stop=(k == KD - 1))
                    ins.then_inc(q_done, 1)
                    if n:
                        scores(n - 1)
                scores(QC - 1)

            @block.vector
            def _(eng):
                link = Chain(eng, chain)
                for i in range(2 * TB):
                    tb, half = i // 2, i % 2
                    at = (slice(None), slice(4 * half, 4 * half + 4), slice(tb * P, (tb + 1) * P))
                    eng.wait_ge(x1_ready, i + 1)
                    V.tensor_tensor(out=xlo[at], in0=bank[half].rearrange("p (k t) -> p k t", k=4),
                                    in1=xhi[at].bitcast(F32), op=ALU.subtract).then_inc(lo_ready, 1)

                def top16(src, spare, vals, places):
                    for tb in range(TB):
                        ins = V.max(vals(tb)[:, 0:8], src(tb))
                    link(ins)
                    for tb in range(TB):
                        V.max_index(places(tb)[:, 0:8], vals(tb)[:, 0:8], src(tb))
                        ins = V.match_replace(spare(tb), vals(tb)[:, 0:8], src(tb), NEG)
                    link(ins)
                    for tb in range(TB):
                        ins = V.max(vals(tb)[:, 8:16], spare(tb))
                    link(ins)
                    for tb in range(TB):
                        ins = V.max_index(places(tb)[:, 8:16], vals(tb)[:, 8:16], spare(tb))
                    return ins

                for n in range(QC):
                    q, side = n // 2, n % 2
                    eng.wait_ge(s_done, n + 1)
                    top16(lambda tb: bank[4 + n % 2][:, tb * P:(tb + 1) * P], lambda tb: rep[:, tb, :],
                          lambda tb: best[:, side, tb, :], lambda tb: key[:, tb, q, side, :]).then_inc(s_used, 1)
                    if side == 1:
                        shape = [P, TB, TOPK, TOPK]
                        link(V.tensor_tensor(out=cand[:, :, :, :], in0=best[:, 0, :, :].unsqueeze(3).broadcast_to(shape),
                                             in1=best[:, 1, :, :].unsqueeze(2).broadcast_to(shape), op=ALU.add))
                        link(top16(lambda tb: cand[:, tb, :, :].rearrange("p a b -> p (a b)"), lambda tb: crep[:, tb, :],
                                   lambda tb: top[:, tb, q, :], lambda tb: pos[:, tb, q, :]))


def gates(nc, sem, bank, ident, iota, top, pos, key, gates_dram):
    V, S = nc.vector, nc.scalar
    NT = 4
    SETS = 2
    LOOPS = P // (NT * SETS)
    with ExitStack() as st:
        sb = lambda name, shape, dt=F32: st.enter_context(nc.sbuf_tensor(name, shape, dt))
        stage = sb("stage", [P, KEYS, P])
        place = sb("place", [P, 2, SLOTS], U32)
        placef = sb("placef", [P, 2, SLOTS], BF16)
        keyf = sb("keyf", [P, QH, 2, TOPK], BF16)
        iotab = sb("iotab", [P, TOPK], BF16)
        hit = sb("hit", [P, QH, TOPK, TOPK], BF16)
        sel = sb("sel", [P, 3, SLOTS])
        ex = sb("ex", [P, QH, TOPK])
        total = sb("total", [P, QH])
        selT = sb("selT", [P, 3, P])
        first = sb("first", [P, SETS, NT, KEYS])
        second = sb("second", [P, SETS, NT, KEYS])

        chain, less_max, exp_ready, sel_ready, selT_done, selT_ready = (sem(n) for n in (
            "dve_chain_gates", "less_max", "exp_ready", "sel_ready", "sel_transposed", "selT_ready"))
        hot_ready, g_done, g_copied, g_stored = (sem(n) for n in (
            "one_hot_ready", "g_done", "g_copied", "g_stored"))

        with nc.Block() as block:
            @block.vector
            def _(eng):
                link = Chain(eng, chain)
                link(V.tensor_copy(iotab[:, :], iota[:, 0:TOPK]))
                for tb in range(TB):
                    p_in = pos[:, tb, :, :].rearrange("p q k -> p (q k)")
                    V.tensor_scalar(out=place[:, 0, :], in0=p_in, scalar1=4, scalar2=None, op0=ALU.logical_shift_right)
                    V.tensor_scalar(out=place[:, 1, :], in0=p_in, scalar1=TOPK - 1, scalar2=None, op0=ALU.bitwise_and)
                    link(V.tensor_copy(keyf[:, :, :, :], key[:, tb, :, :, :]))
                    link(V.tensor_copy(placef[:, :, :], place[:, :, :]))
                    after(eng, selT_done, tb)
                    for side in range(2):
                        flat = hit[:, :, :, :].rearrange("p q k j -> p (q k) j")
                        shape = [P, SLOTS, TOPK]
                        link(V.tensor_tensor(out=flat, in0=placef[:, side, :].unsqueeze(2).broadcast_to(shape),
                                             in1=iotab[:, :].unsqueeze(1).broadcast_to(shape), op=ALU.is_equal))
                        link(V.tensor_tensor(out=hit[:, :, :, :], in0=hit[:, :, :, :],
                                             in1=keyf[:, :, side, :].unsqueeze(2).broadcast_to([P, QH, TOPK, TOPK]),
                                             op=ALU.mult))
                        link(V.tensor_reduce(sel[:, side, :], flat, AX.X, ALU.add))
                    shape = [P, QH, TOPK]
                    V.tensor_tensor(out=ex[:, :, :], in0=top[:, tb, :, :], in1=top[:, tb, :, 0:1].broadcast_to(shape),
                                    op=ALU.subtract).then_inc(less_max, 1)
                    eng.wait_ge(exp_ready, tb + 1)
                    link(V.tensor_reduce(total[:, :], ex[:, :, :], AX.X, ALU.add))
                    link(V.reciprocal(total[:, :], total[:, :]))
                    V.tensor_tensor(out=sel[:, 2, :].rearrange("p (q k) -> p q k", q=QH), in0=ex[:, :, :],
                                    in1=total[:, :].unsqueeze(2).broadcast_to(shape), op=ALU.mult).then_inc(sel_ready, 1)
                    eng.wait_ge(selT_ready, tb + 1)
                    with eng.Fori(0, LOOPS) as it:
                        for u in range(SETS):
                            step = tb * LOOPS * SETS + it * SETS + u
                            eng.wait_ge(g_done, step + 1)
                            for q in range(NT):
                                t = it * (SETS * NT) + (u * NT + q)
                                V.tensor_scalar(out=first[:, u, q, :], in0=iota[:, :], scalar1=selT[:, 0, bass.ds(t, 1)],
                                                scalar2=selT[:, 2, bass.ds(t, 1)], op0=ALU.is_equal, op1=ALU.mult)
                                ins = V.tensor_scalar(out=second[:, u, q, :], in0=iota[:, :],
                                                      scalar1=selT[:, 1, bass.ds(t, 1)], scalar2=None, op0=ALU.is_equal)
                            ins.then_inc(hot_ready, 1)

            @block.scalar
            def _(eng):
                eng.sem_inc(g_copied, SETS)
                for tb in range(TB):
                    eng.wait_ge(less_max, tb + 1)
                    S.activation(ex[:, :, :], ex[:, :, :], ACT.Exp).then_inc(exp_ready, 1)
                    eng.wait_ge(selT_done, tb + 1)
                    after(eng, hot_ready, tb * LOOPS * SETS)
                    S.activation(selT[:, :, :], bank[0][:, 0:3 * P].rearrange("p (a t) -> p a t", a=3),
                                 ACT.Copy).then_inc(selT_ready, 1)
                    after(eng, g_stored, 16 * tb)
                    with eng.Fori(0, LOOPS) as it:
                        for u in range(SETS):
                            step = tb * LOOPS * SETS + it * SETS + u
                            t = it * (SETS * NT) + u * NT
                            eng.wait_ge(g_done, step + SETS + 1)
                            S.activation(stage[:, :, bass.ds(t, NT)], bank[4 + u].rearrange("p (t i) -> p i t", t=NT),
                                         ACT.Copy).then_inc(g_copied, 1)

            @block.tensor
            def _(eng):
                eng.sem_inc(g_done, SETS)
                for tb in range(TB):
                    eng.wait_ge(sel_ready, tb + 1)
                    after(eng, selT_ready, tb)
                    for i in range(3):
                        ins = nc.tensor.transpose(bank[0][:, i * P:(i + 1) * P], sel[:, i, :], ident[:, :])
                    ins.then_inc(selT_done, 1)
                    with eng.Fori(0, LOOPS) as it:
                        for u in range(SETS):
                            step = tb * LOOPS * SETS + it * SETS + u
                            eng.wait_ge(hot_ready, step + 1)
                            eng.wait_ge(g_copied, step + 1)
                            for q in range(NT):
                                ins = nc.tensor.matmul(bank[4 + u][:, q * KEYS:(q + 1) * KEYS], second[:, u, q, :],
                                                       first[:, u, q, :], start=True, stop=True)
                            ins.then_inc(g_done, 1)

            @block.sync
            def _(eng):
                for tb in range(TB):
                    eng.wait_ge(g_copied, (tb + 1) * LOOPS * SETS + SETS)
                    eng.dma_start(gates_dram[:, :, tb * P:(tb + 1) * P].rearrange("i j t -> j i t"),
                                  stage[:, :, :]).then_inc(g_stored, 16)
                eng.wait_ge(g_stored, 16 * TB)


def experts(nc, a, sem, bank, h, ident, small, xhi, xlo, gates_dram, out):
    V, S, G = nc.vector, nc.scalar, nc.gpsimd
    GC = 4
    NG = KEYS // GC
    with ExitStack() as st:
        sb = lambda name, shape, dt=F32: st.enter_context(nc.sbuf_tensor(name, shape, dt))
        u_raw = [sb(f"u_raw{i}", [P, D]) for i in range(GC)]
        v_raw = [sb(f"v_raw{i}", [P, D]) for i in range(GC)]
        g_in = [sb(f"g_in{i}", [P, T]) for i in range(GC)]
        ut_hi = [sb(f"ut_hi{i}", [P, KD, P], F32R) for i in range(2)]
        ut_lo = [sb(f"ut_lo{i}", [P, KD, P], F32R) for i in range(2)]
        v_hi = [sb(f"v_hi{i}", [P, D], F32R) for i in range(GC)]
        v_lo = [sb(f"v_lo{i}", [P, D], F32R) for i in range(GC)]
        gel = sb("gel", [P, 2, T])
        w32 = sb("w32", [P, 2, T])
        w_hi = [sb(f"w_hi{i}", [P, T], F32R) for i in range(GC)]
        w_lo = [sb(f"w_lo{i}", [P, T], F32R) for i in range(GC)]
        ln = sb("ln2", [P, 2, D])
        bn = sb("bn2", [P, TB, 2, 6])
        mv = sb("mv2", [P, TB, 2])
        rs = sb("rs2", [P, TB, 1])

        u_loaded = [sem(f"u_loaded{i}") for i in range(GC)]
        v_loaded = [sem(f"v_loaded{i}") for i in range(GC)]
        g_loaded = [sem(f"g_loaded{i}") for i in range(GC)]
        u_turned, ut_hi_ready, ut_lo_ready = sem("u_transposed"), sem("ut_hi_ready"), sem("ut_lo_ready")
        act_done, gelu_ready, w_made = sem("act_done"), sem("gelu_ready"), sem("w_made")
        w_hi_ready, w_lo_ready, v_hi_ready, v_lo_ready = (sem(n) for n in (
            "w_hi_ready", "w_lo_ready", "v_hi_ready", "v_lo_ready"))
        y_done, y_added = sem("y_pair_done"), sem("y_added")
        ln2_loaded, var_ready, rstd_ready, norm_ready, out_ready, stored = (sem(n) for n in (
            "ln2_loaded", "var2_ready", "rstd2_ready", "norm2_ready", "out_ready", "out_stored"))
        chain, pool_chain = sem("dve_chain_experts"), sem("pool_chain_experts")

        def groups(eng, group):
            group(0, first=True)
            with eng.Fori(1, NG - 1) as g:
                group(g)
            group(NG - 1, last=True)

        u_rows = a["peer_u"][0]
        v_rows = a["peer_v"][0]
        g_rows = gates_dram.rearrange("i j t -> (i j) t")

        with nc.Block() as block:
            @block.sync
            def _(eng):
                def load(c, at):
                    return (lambda: eng.dma_start(u_raw[c][:, :], u_rows[at, :]).then_inc(u_loaded[c], 16),
                            lambda: eng.dma_start(v_raw[c][:, :], v_rows[at, :]).then_inc(v_loaded[c], 16),
                            lambda: eng.dma_start(g_in[c][:, :], g_rows[at, :]).then_inc(g_loaded[c], 16))

                for c in range(GC):
                    for start in load(c, slice(c * P, (c + 1) * P)):
                        start()
                eng.dma_start(ln[:, 0, :], a["ln2_g"][0].partition_broadcast(P)).then_inc(ln2_loaded, 16)
                eng.dma_start(ln[:, 1, :], a["ln2_b"][0].partition_broadcast(P)).then_inc(ln2_loaded, 16)
                with eng.Fori(0, NG - 1) as g:
                    for c in range(GC):
                        u, v, gt = load(c, bass.ds(g * (GC * P) + (GC + c) * P, P))
                        n = g * GC + c
                        eng.wait_ge(u_turned, 2 * n + 2)
                        u()
                        eng.wait_ge(v_lo_ready, n + 1)
                        v()
                        eng.wait_ge(w_made, n + 1)
                        gt()
                for tb in range(TB):
                    eng.wait_ge(out_ready, tb + 1)
                    eng.dma_start(out[0, tb * P:(tb + 1) * P, :], h[:, tb, :]).then_inc(stored, 16)
                eng.wait_ge(stored, 16 * TB)

            @block.tensor
            def _(eng):
                mm = nc.tensor.matmul

                def turn(c, m, loads):
                    eng.wait_ge(u_loaded[c], 16 * loads)
                    for half in range(2):
                        after(eng, ut_lo_ready, 2 * m + half - 1)
                        for k in range(4):
                            j = 4 * half + k
                            ins = nc.tensor.transpose(bank[half][:, k * P:(k + 1) * P], u_raw[c][:, j * P:(j + 1) * P],
                                                      ident[:, :])
                        ins.then_inc(u_turned, 1)

                def group(g, first=False, last=False):
                    for c in range(GC):
                        n = g * GC + c
                        if not (last and c == GC - 1):
                            turn((c + 1) % GC, n + 1, g + 1 + (c + 1) // GC)
                        eng.wait_ge(ut_lo_ready, 2 * n + 2)
                        after(eng, gelu_ready, n - 1)
                        i = 0
                        for k in range(KD):
                            for u, x in ((ut_hi, xhi), (ut_hi, xlo), (ut_lo, xhi)):
                                ins = mm(bank[2 + c % 2][:, :], u[c % 2][:, k, :], x[:, k, :], start=(i == 0),
                                         stop=(i == 3 * KD - 1))
                                i += 1
                        ins.then_inc(act_done, 1)
                    for tb in range(TB):
                        after(eng, y_added, g * TB + tb - 1)
                        for c in range(GC):
                            if tb == 0:
                                eng.wait_ge(v_lo_ready, g * GC + c + 1)
                                eng.wait_ge(w_lo_ready, g * GC + c + 1)
                            for w, v, begins, ends in ((w_hi, v_hi, c == 0, False), (w_hi, v_lo, False, False),
                                                       (w_lo, v_hi, False, c == GC - 1)):
                                for i in range(2):
                                    ins = mm(bank[4 + 2 * (tb % 2) + i][:, :], w[c][:, tb * P:(tb + 1) * P],
                                             v[c][:, i * HALF_D:(i + 1) * HALF_D], start=begins, stop=ends)
                        ins.then_inc(y_done, 1)

                turn(0, 0, 1)
                groups(eng, group)

            @block.scalar
            def _(eng):
                def upper(m, c):
                    after(eng, act_done, m - 1)
                    for half in range(2):
                        eng.wait_ge(u_turned, 2 * m + half + 1)
                        S.activation(ut_hi[c % 2][:, 4 * half:4 * half + 4, :],
                                     bank[half].rearrange("p (k e) -> p k e", k=4), ACT.Copy).then_inc(ut_hi_ready, 1)

                def group(g, first=False, last=False):
                    for c in range(GC):
                        n = g * GC + c
                        if not (last and c == GC - 1):
                            upper(n + 1, c + 1)
                        eng.wait_ge(v_loaded[c], 16 * (g + 1))
                        if c == 0:
                            after(eng, y_done, g * TB)
                        S.activation(v_hi[c][:, :], v_raw[c][:, :], ACT.Copy).then_inc(v_hi_ready, 1)
                        eng.wait_ge(act_done, n + 1)
                        after(eng, w_made, n - 1)
                        S.activation(gel[:, c % 2, :], bank[2 + c % 2][:, :], ACT.Gelu).then_inc(gelu_ready, 1)
                        eng.wait_ge(w_made, n + 1)
                        S.activation(w_hi[c][:, :], w32[:, c % 2, :], ACT.Copy).then_inc(w_hi_ready, 1)

                upper(0, 0)
                groups(eng, group)

            @block.gpsimd
            def _(eng):
                def group(g, first=False, last=False):
                    for c in range(GC):
                        eng.wait_ge(v_hi_ready, g * GC + c + 1)
                        G.tensor_tensor(out=v_lo[c][:, :], in0=v_raw[c][:, :], in1=v_hi[c][:, :].bitcast(F32),
                                        op=ALU.subtract).then_inc(v_lo_ready, 1)

                groups(eng, group)
                link = Chain(eng, pool_chain)
                eng.wait_ge(ln2_loaded, 32)
                for tb in range(TB):
                    eng.wait_ge(var_ready, tb + 1)
                    link(G.tensor_tensor(out=rs[:, tb, :], in0=mv[:, tb, 1:2], in1=small[:, 2:3], op=ALU.add))
                    G.tensor_tensor(out=rs[:, tb, :], in0=rs[:, tb, :], in1=small[:, 0:1],
                                    op=ALU.pow).then_inc(rstd_ready, 1)
                    eng.wait_ge(norm_ready, tb + 1)
                    link(G.tensor_tensor(out=h[:, tb, :], in0=h[:, tb, :], in1=ln[:, 0, :], op=ALU.mult))
                    G.tensor_tensor(out=h[:, tb, :], in0=h[:, tb, :], in1=ln[:, 1, :], op=ALU.add).then_inc(out_ready, 1)

            @block.vector
            def _(eng):
                def lower(m, c):
                    for half in range(2):
                        at = (slice(None), slice(4 * half, 4 * half + 4), slice(None))
                        eng.wait_ge(ut_hi_ready, 2 * m + half + 1)
                        V.tensor_tensor(out=ut_lo[c % 2][at], in0=bank[half].rearrange("p (k e) -> p k e", k=4),
                                        in1=ut_hi[c % 2][at].bitcast(F32), op=ALU.subtract).then_inc(ut_lo_ready, 1)

                def group(g, first=False, last=False):
                    for c in range(GC):
                        n = g * GC + c
                        if not (last and c == GC - 1):
                            lower(n + 1, c + 1)
                        eng.wait_ge(gelu_ready, n + 1)
                        eng.wait_ge(g_loaded[c], 16 * (g + 1))
                        V.tensor_tensor(out=w32[:, c % 2, :], in0=gel[:, c % 2, :], in1=g_in[c][:, :],
                                        op=ALU.mult).then_inc(w_made, 1)
                        eng.wait_ge(w_hi_ready, n + 1)
                        V.tensor_tensor(out=w_lo[c][:, :], in0=w32[:, c % 2, :], in1=w_hi[c][:, :].bitcast(F32),
                                        op=ALU.subtract).then_inc(w_lo_ready, 1)
                    after(eng, y_added, g * TB)
                    for tb in range(TB):
                        eng.wait_ge(y_done, g * TB + tb + 1)
                        for i in range(2):
                            blk = h[:, tb, i * HALF_D:(i + 1) * HALF_D]
                            ins = V.scalar_tensor_tensor(out=blk, in0=blk, scalar=ALPHA if first else 1.0,
                                                         in1=bank[4 + 2 * (tb % 2) + i][:, :], op0=ALU.mult, op1=ALU.add)
                        ins.then_inc(y_added, 1)

                lower(0, 0)
                groups(eng, group)
                link = Chain(eng, chain)
                eng.wait_ge(y_added, NG * TB)
                for tb in range(TB + 1):
                    if tb < TB:
                        for i in range(2):
                            ins = V.bn_stats(bn[:, tb, i, :], h[:, tb, i * HALF_D:(i + 1) * HALF_D])
                        link(ins)
                        V.bn_aggr(mv[:, tb, :], bn[:, tb, :, :].rearrange("p a b -> p (a b)")).then_inc(var_ready, 1)
                    if tb:
                        eng.wait_ge(rstd_ready, tb)
                        V.tensor_scalar(out=h[:, tb - 1, :], in0=h[:, tb - 1, :], scalar1=mv[:, tb - 1, 0:1],
                                        scalar2=rs[:, tb - 1, :], op0=ALU.subtract, op1=ALU.mult).then_inc(norm_ready, 1)


_INS = ["x", "ln_emb_g", "ln_emb_b", "w_in", "lru_conv_w", "lru_conv_b", "lru_wa", "lru_ba", "lru_wx", "lru_bx",
        "lru_lambda", "conv_w", "norm_lru_g", "norm_conv_g", "w_out", "ln1_g", "ln1_b",
        "peer_wq", "peer_k1", "peer_k2", "peer_u", "peer_v", "ln2_g", "ln2_b"]


def kernel(**inputs):
    import concourse.bacc as bacc
    from concourse.bass_utils import run_bass_kernel_spmd

    nc = bacc.Bacc("TRN2", target_bir_lowering=False, num_devices=1)
    arrays, args = {}, {}
    for name in _INS:
        v = np.ascontiguousarray(inputs[name])
        arrays[f"in_{name}"] = v
        args[name] = nc.dram_tensor(f"in_{name}", v.shape, F32, kind="ExternalInput").ap()
    out = nc.dram_tensor("out_0", (1, T, D), F32, kind="ExternalOutput").ap()
    gates_dram = nc.dram_tensor("gate_matrix", (KEYS, KEYS, T), F32, kind="Internal").ap()
    build(nc, args, out, gates_dram)
    r = run_bass_kernel_spmd(nc, [arrays], core_ids=[0])
    return r.results[0]["out_0"]
```

```python
from contextlib import ExitStack

import numpy as np
import concourse.bass as bass
from concourse import mybir

F32 = mybir.dt.float32
F32R = mybir.dt.float32r
BF16 = mybir.dt.bfloat16
U32 = mybir.dt.uint32
I32 = mybir.dt.int32
ALU = mybir.AluOpType
ACT = mybir.ActivationFunctionType
AX = mybir.AxisListType

P = 128
T, D = 512, 1024
TB, KD = T // P, D // P
HALF_D = D // 2
HEADS = 8
CONV = 4
MIX = HEADS + CONV
D_IN = 2 * D + 3 * CONV * P
LRU_W, SHORT_W = 4, 3
PAD = LRU_W - 1
LRU_C = 8.0
QH, TOPK = 8, 16
KEYS = 128
SLOTS = QH * TOPK
LN_EPS, RMS_EPS = 1e-5, 1e-6
ALPHA = 2.0 ** 0.25
NEG = -3.0e38

DT = TB - 1
DTOK = DT * P
QC = 2 * QH
EXTRA = 3
PER_TB = EXTRA + 16
CLOSING = 4
MADE = QC + EXTRA + DT * PER_TB + CLOSING
RING = 4
AHEAD = 2
GATE_TURNS = 4
BESIDE = (4, 8, 8)
U_FROM = sum(BESIDE) * GATE_TURNS

PC_CONVW, PC_CONVB, PC_BA, PC_BX, PC_LAM = 0, 64, 80, 96, 112
PC_SHORT, PC_GLRU, PC_GCONV = 0, 12, 20

COL_X, COL_GATE, COL_CB, COL_CC, COL_CX = 0, HEADS, 2 * HEADS, 2 * HEADS + CONV, 2 * HEADS + 2 * CONV


class Chain:

    def __init__(self, eng, sem):
        self.eng, self.sem, self.n = eng, sem, 0

    def __call__(self, ins):
        self.n += 1
        ins.then_inc(self.sem, 1)
        self.eng.wait_ge(self.sem, self.n)


def after(eng, sem, count):
    if not isinstance(count, int) or count > 0:
        eng.wait_ge(sem, count)


def build(nc, a, out, gates_dram, act_dram):
    ctx = ExitStack()
    with ctx:
        sem = lambda name: ctx.enter_context(nc.semaphore(name))
        sb = lambda name, shape, dt=F32: ctx.enter_context(nc.sbuf_tensor(name, shape, dt))
        bank = [ctx.enter_context(nc.psum_tensor(f"bank{i}", [P, 512], F32)) for i in range(8)]
        h = sb("h", [P, TB, D])
        ident = sb("ident", [P, P])
        ones = sb("ones", [P, P])
        iota = sb("iota", [P, KEYS])
        small = sb("small", [P, 8])
        mixer(nc, a, sem, bank, h, ident, ones, iota, small)
        xhi = sb("xhi", [P, KD, T], F32R)
        xlo = sb("xlo", [P, KD, T], F32R)
        acts = ActPipeline(nc, a, sem, sb, bank, ident, xhi, xlo)
        far = GatherPath(nc, a, sem, sb, h[:, DT, :])
        acts.whole = far.sum[0].rearrange("p (k e) -> p k e", k=KD)
        with ExitStack() as rs:
            rb = lambda name, shape, dt=F32: rs.enter_context(nc.sbuf_tensor(name, shape, dt))
            top = rb("top", [P, TB, QH, TOPK])
            pos = rb("pos", [P, TB, QH, TOPK], U32)
            key = rb("key", [P, TB, QH, 2, TOPK], U32)
            queries(nc, a, sem, bank, h, ident, xhi, xlo, acts, act_dram, top, pos, key)
            gates(nc, sem, bank, ident, iota, acts, far, act_dram, top, pos, key, gates_dram)
        experts(nc, a, sem, bank, h, small, acts, far, act_dram, gates_dram, out)


def mixer(nc, a, sem, bank, h, ident, ones, iota, small):
    V, S, G = nc.vector, nc.scalar, nc.gpsimd
    with ExitStack() as st:
        sb = lambda name, shape, dt=F32: st.enter_context(nc.sbuf_tensor(name, shape, dt))
        hT = sb("hT", [P, KD, T])
        NW = 4
        wbuf = [sb(f"w_in{i}", [P, KD, P]) for i in range(NW)]
        wa = sb("wa", [P, 2 * HEADS, P])
        wx = sb("wx", [P, 2 * HEADS, P])
        wo = sb("wo", [P, MIX, D])
        y = sb("y", [P, MIX, T])
        ln = sb("ln", [P, 4, D])
        prow = sb("prow", [P, 2, P])
        pA = sb("pA", [P, P])
        pB = sb("pB", [P, 24])
        hb = sb("hb", [P, 32])
        sp = sb("sp", [P, 2, 16])
        t16 = sb("t16", [P, 8, 16])
        xp = sb("xp", [P, 2, T + 2 * PAD])
        xc = sb("xc", [P, 2, 2, T])
        th = sb("th", [P, 2, 2, T])
        da = sb("da", [P, 2, T])
        dw = sb("dw", [P, 2, T])
        dq = sb("dq", [P, 2, T])
        dr = sb("dr", [P, T])
        hd = sb("hd", [P, 2, T])
        sq = sb("sq", [P, 2, T])
        rstd = sb("rstd", [P, 2, T])
        bn = sb("bn", [P, TB, 2, 6])
        mv = sb("mv", [P, TB, 2])
        rs = sb("rs", [P, TB, 1])

        x_loaded = [sem(f"x_loaded{i}") for i in range(TB)]
        w_loaded = [sem(f"w_loaded{i}") for i in range(NW)]
        wo_loaded, ln_loaded, p_loaded, g_loaded = (sem(n) for n in (
            "wo_loaded", "ln_loaded", "params_loaded", "gate_weights_loaded"))
        consts_ready, pT_ready, p_ready, sp_ready, exp_lam = (sem(n) for n in (
            "consts_ready", "params_transposed", "params_ready", "softplus_ready", "exp_lambda"))
        var_ready, rstd_ready, norm_ready, h_ready = (sem(n) for n in (
            "var_ready", "rstd_ready", "norm_ready", "h_ready"))
        ht_done, ht_ready = sem("h_transposed"), sem("hT_ready")
        z_done, z_used_act, z_used_dve = sem("z_done"), sem("z_used_act"), sem("z_used_dve")
        xp_ready, xc_ready, gates_done, tanh_ready = (sem(n) for n in (
            "xp_ready", "xc_ready", "gates_done", "tanh_ready"))
        decay_ready, q_ready, root_ready, y_ready, sq_ready, sums_done = (sem(n) for n in (
            "decay_ready", "q_ready", "root_ready", "y_ready", "squares_ready", "sums_done"))
        cc_ready, rms_root, mix_ready, o_done = (sem(n) for n in (
            "cc_ready", "rms_root_ready", "mix_ready", "out_projection_done"))
        xp_zero, o_used = sem("xp_zero"), sem("out_projection_used")
        dve_chain, pool_chain, act_chain = sem("dve_chain"), sem("pool_chain"), sem("act_chain")

        order = [COL_GATE + i for i in range(HEADS)] + [COL_X + i for i in range(HEADS)]
        for j in range(CONV):
            order += [COL_CC + j, COL_CX + j, COL_CB + j]
        HX, HC = HEADS, 2 * HEADS
        by_dve = [n >= HC and (n - HC) % 3 > 0 for n in range(len(order))]
        n_act = lambda n: sum(not b for b in by_dve[:n + 1])
        n_dve = lambda n: sum(by_dve[:n + 1])

        with nc.Block() as block:
            @block.sync
            def _(sp_eng):
                eng = sp_eng
                for tb in range(TB):
                    eng.dma_start(h[:, tb, :], a["x"][0, tb * P:(tb + 1) * P, :]).then_inc(x_loaded[tb], 16)
                for n, c in enumerate(order):
                    if n >= NW:
                        eng.wait_ge(z_done, n - NW + 1)
                    eng.dma_start(wbuf[n % NW][:, :, :],
                                  a["w_in"][0, :, c * P:(c + 1) * P].rearrange("(k p) c -> p k c", p=P)
                                  ).then_inc(w_loaded[n % NW], 16)
                    if n == 12:
                        eng.dma_start(wo[:, :, :], a["w_out"][0].rearrange("(k p) n -> p k n", p=P)
                                      ).then_inc(wo_loaded, 16)

            @block.gpsimd
            def _(eng):
                link = Chain(eng, pool_chain)
                G.memset(ones[:, :], 1.0)
                link(G.memset(ident[:, :], 0.0))
                link(G.affine_select(out=ident[:, :], in_=ident[:, :], compare_op=ALU.not_equal, fill=1.0,
                                     base=0, pattern=[[-1, P]], channel_multiplier=1))
                G.iota(iota[:, :], [[1, KEYS]], base=0, channel_multiplier=0,
                       allow_small_or_imprecise_dtypes=True)
                G.memset(small[:, 0:1], -0.5)
                G.memset(small[:, 1:2], RMS_EPS)
                G.memset(small[:, 2:3], LN_EPS).then_inc(consts_ready, 1)
                eng.wait_ge(consts_ready, 1)
                G.memset(xp[:, :, :], 0.0).then_inc(xp_zero, 1)
                for half in range(2):
                    for tb in range(TB):
                        eng.wait_ge(var_ready, half * TB + tb + 1)
                        link(G.tensor_tensor(out=rs[:, tb, :], in0=mv[:, tb, 1:2], in1=small[:, 2:3], op=ALU.add))
                        G.tensor_tensor(out=rs[:, tb, :], in0=rs[:, tb, :], in1=small[:, 0:1],
                                        op=ALU.pow).then_inc(rstd_ready, 1)
                        eng.wait_ge(norm_ready, half * TB + tb + 1)
                        if tb == 0 and half == 0:
                            eng.wait_ge(ln_loaded, 64)
                        link(G.tensor_tensor(out=h[:, tb, :], in0=h[:, tb, :], in1=ln[:, 2 * half, :], op=ALU.mult))
                        G.tensor_tensor(out=h[:, tb, :], in0=h[:, tb, :], in1=ln[:, 2 * half + 1, :],
                                        op=ALU.add).then_inc(h_ready, 1)

            @block.scalar
            def _(eng):
                rows = lambda r0, n, src: eng.dma_start(prow[r0 % P:r0 % P + n, r0 // P, :], src).then_inc(p_loaded, 16)
                rows(PC_CONVW, 64, a["lru_conv_w"][0].rearrange("d k (h p) -> (d k h) p", p=P))
                rows(PC_CONVB, 16, a["lru_conv_b"][0].rearrange("d (h p) -> (d h) p", p=P))
                rows(PC_BA, 16, a["lru_ba"][0].rearrange("d (h p) -> (d h) p", p=P))
                rows(PC_BX, 16, a["lru_bx"][0].rearrange("d (h p) -> (d h) p", p=P))
                rows(PC_LAM, 16, a["lru_lambda"][0].rearrange("d (h p) -> (d h) p", p=P))
                rows(P + PC_SHORT, 12, a["conv_w"][0].rearrange("k (h p) -> (k h) p", p=P))
                rows(P + PC_GLRU, 8, a["norm_lru_g"][0].rearrange("(h p) -> h p", p=P))
                rows(P + PC_GCONV, 4, a["norm_conv_g"][0].rearrange("(h p) -> h p", p=P))
                for i, name in enumerate(("ln_emb_g", "ln_emb_b", "ln1_g", "ln1_b")):
                    v = a[name] if i < 2 else a[name][0]
                    eng.dma_start(ln[:, i, :], v.partition_broadcast(P)).then_inc(ln_loaded, 16)
                eng.dma_start(wa[:, :, :], a["lru_wa"][0].rearrange("d h i j -> i (d h) j")).then_inc(g_loaded, 16)
                eng.dma_start(wx[:, :, :], a["lru_wx"][0].rearrange("d h i j -> i (d h) j")).then_inc(g_loaded, 16)
                link = Chain(eng, act_chain)
                eng.wait_ge(pT_ready, 1)
                S.activation(pA[:, :], bank[4][:, 0:P], ACT.Copy)
                S.activation(pB[:, :], bank[4][:, P:P + 24], ACT.Copy).then_inc(p_ready, 1)
                eng.wait_ge(exp_lam, 1)
                S.activation(t16[:, 2, :], t16[:, 1, :], ACT.Exp, scale=-1.0).then_inc(exp_lam, 1)
                for i in range(2 * TB):
                    tb, half = i // 2, i % 2
                    eng.wait_ge(ht_done, i + 1)
                    S.activation(hT[:, 4 * half:4 * half + 4, tb * P:(tb + 1) * P],
                                 bank[i % 2].rearrange("p (k t) -> p k t", k=4), ACT.Copy).then_inc(ht_ready, 1)
                for n in range(HEADS):
                    eng.wait_ge(z_done, n + 1)
                    S.activation(y[:, n, :], bank[n % 2][:, :], ACT.Gelu_apprx_tanh).then_inc(z_used_act, 1)

                def squares(i):
                    eng.wait_ge(y_ready, i + 1)
                    after(eng, sums_done, i - 1)
                    S.activation(sq[:, i % 2, :], y[:, i, :], ACT.Square).then_inc(sq_ready, 1)

                for hd_i in range(HEADS + 1):
                    if hd_i < HEADS:
                        eng.wait_ge(z_done, HX + hd_i + 1)
                        if hd_i == 0:
                            eng.wait_ge(xp_zero, 1)
                        after(eng, xc_ready, 2 * (hd_i - 1))
                        S.activation(xp[:, hd_i % 2, PAD:PAD + T], bank[(HX + hd_i) % 2][:, :],
                                     ACT.Copy).then_inc(z_used_act, 1)
                    if hd_i == 0:
                        eng.wait_ge(sp_ready, 1)
                        continue
                    g = hd_i - 1
                    for d in range(2):
                        c = d * HEADS + g
                        eng.wait_ge(gates_done, 2 * g + d + 1)
                        after(eng, y_ready, g)
                        S.activation(th[:, d, 0, :], bank[4 + 2 * d][:, :], ACT.Tanh, scale=0.5, bias=hb[:, c:c + 1])
                        link(S.activation(th[:, d, 1, :], bank[5 + 2 * d][:, :], ACT.Tanh, scale=0.5,
                                          bias=hb[:, 16 + c:17 + c]))
                        S.activation(dw[:, d, :], th[:, d, 0, :], ACT.Tanh, scale=sp[:, 0, c:c + 1],
                                     bias=sp[:, 0, c:c + 1]).then_inc(tanh_ready, 1)
                        S.activation(da[:, d, :], th[:, d, 0, :], ACT.Exp, scale=sp[:, 1, c:c + 1],
                                     bias=sp[:, 1, c:c + 1]).then_inc(decay_ready, 1)
                    for d in range(2):
                        eng.wait_ge(q_ready, 2 * g + d + 1)
                        S.activation(dq[:, d, :], dq[:, d, :], ACT.Sqrt, scale=0.5).then_inc(root_ready, 1)
                    if g > 0:
                        squares(g - 1)
                squares(HEADS - 1)
                for j in range(CONV):
                    n = HC + 3 * j
                    eng.wait_ge(z_done, n + 1)
                    after(eng, y_ready, HEADS + j)
                    S.activation(dr[:, :], bank[n % 2][:, :], ACT.Copy).then_inc(z_used_act, 1)
                    squares(HEADS + j)
                for i in range(2):
                    eng.wait_ge(sums_done, MIX)
                    S.activation(rstd[:, i, :], bank[2 + i][:, :], ACT.Sqrt, scale=1.0 / (P * (HEADS, CONV)[i]),
                                 bias=small[:, 1:2]).then_inc(rms_root, 1)

            @block.vector
            def _(eng):
                link = Chain(eng, dve_chain)

                def stats(tb):
                    for i in range(2):
                        ins = V.bn_stats(bn[:, tb, i, :], h[:, tb, i * HALF_D:(i + 1) * HALF_D])
                    link(ins)
                    V.bn_aggr(mv[:, tb, :], bn[:, tb, :, :].rearrange("p a b -> p (a b)")).then_inc(var_ready, 1)

                def normalise(n, tb):
                    eng.wait_ge(rstd_ready, n)
                    V.tensor_scalar(out=h[:, tb, :], in0=h[:, tb, :], scalar1=mv[:, tb, 0:1], scalar2=rs[:, tb, :],
                                    op0=ALU.subtract, op1=ALU.mult).then_inc(norm_ready, 1)

                eng.wait_ge(consts_ready, 1)
                for tb in range(TB):
                    eng.wait_ge(x_loaded[tb], 16)
                    stats(tb)
                    if tb:
                        normalise(tb, tb - 1)
                normalise(TB, TB - 1)

                eng.wait_ge(p_ready, 1)
                neg, mag, e, s, s2, poly = (t16[:, i, :] for i in range(6))
                V.tensor_scalar(out=hb[:, :], in0=pA[:, PC_BA:PC_BA + 32], scalar1=0.5, scalar2=None, op0=ALU.mult)
                link(V.tensor_scalar(out=neg, in0=pA[:, PC_LAM:PC_LAM + 16], scalar1=-1.0, scalar2=None, op0=ALU.mult))
                V.tensor_tensor(out=mag, in0=neg, in1=pA[:, PC_LAM:PC_LAM + 16], op=ALU.max).then_inc(exp_lam, 1)
                eng.wait_ge(exp_lam, 2)
                link(V.tensor_scalar(out=s, in0=e, scalar1=2.0, scalar2=None, op0=ALU.add))
                link(V.reciprocal(s, s))
                link(V.tensor_tensor(out=s, in0=s, in1=e, op=ALU.mult))
                link(V.tensor_tensor(out=s2, in0=s, in1=s, op=ALU.mult))
                link(V.tensor_scalar(out=poly, in0=s2, scalar1=1.0 / 15, scalar2=1.0 / 13, op0=ALU.mult, op1=ALU.add))
                for k in (11, 9, 7, 5, 3, 1):
                    link(V.tensor_tensor(out=poly, in0=poly, in1=s2, op=ALU.mult))
                    link(V.tensor_scalar(out=poly, in0=poly, scalar1=1.0 / k, scalar2=None, op0=ALU.add))
                link(V.tensor_tensor(out=poly, in0=poly, in1=s, op=ALU.mult))
                link(V.tensor_scalar(out=neg, in0=neg, scalar1=0.0, scalar2=LRU_C / 2, op0=ALU.max, op1=ALU.mult))
                link(V.scalar_tensor_tensor(out=sp[:, 0, :], in0=poly, scalar=LRU_C, in1=neg, op0=ALU.mult, op1=ALU.add))
                V.tensor_scalar(out=sp[:, 1, :], in0=sp[:, 0, :], scalar1=-1.0, scalar2=None,
                                op0=ALU.mult).then_inc(sp_ready, 1)

                for hd_i in range(HEADS + 1):
                    if hd_i < HEADS:
                        eng.wait_ge(z_used_act, n_act(HX + hd_i))
                        x0 = xp[:, hd_i % 2, :]
                        after(eng, gates_done, 2 * (hd_i - 1))
                        for k in range(LRU_W):
                            for d in range(2):
                                c = d * HEADS + hd_i
                                w = pA[:, PC_CONVW + (d * LRU_W + k) * HEADS + hd_i:][:, 0:1]
                                o, src = xc[:, hd_i % 2, d, :], x0[:, d * PAD + k:d * PAD + k + T]
                                if k == 0:
                                    ins = V.tensor_scalar(out=o, in0=src, scalar1=w,
                                                          scalar2=pA[:, PC_CONVB + c:PC_CONVB + c + 1],
                                                          op0=ALU.mult, op1=ALU.add)
                                else:
                                    ins = V.scalar_tensor_tensor(out=o, in0=src, scalar=w, in1=o,
                                                                 op0=ALU.mult, op1=ALU.add)
                                if k == LRU_W - 1:
                                    ins.then_inc(xc_ready, 1)
                            if k < LRU_W - 1:
                                link(ins)
                    if hd_i == 0:
                        continue
                    g = hd_i - 1
                    for d in range(2):
                        eng.wait_ge(tanh_ready, 2 * g + d + 1)
                        link(V.tensor_scalar(out=dq[:, d, :], in0=dw[:, d, :], scalar1=1.0, scalar2=None, op0=ALU.add))
                        link(V.reciprocal(dq[:, d, :], dq[:, d, :]))
                        V.tensor_tensor(out=dq[:, d, :], in0=dq[:, d, :], in1=dw[:, d, :],
                                        op=ALU.mult).then_inc(q_ready, 1)
                        link(V.scalar_tensor_tensor(out=th[:, d, 1, :], in0=th[:, d, 1, :], scalar=1.0,
                                                    in1=xc[:, g % 2, d, :], op0=ALU.add, op1=ALU.mult))
                    for d in range(2):
                        eng.wait_ge(root_ready, 2 * g + d + 1)
                        eng.wait_ge(decay_ready, 2 * g + d + 1)
                        link(V.tensor_tensor(out=dq[:, d, :], in0=dq[:, d, :], in1=th[:, d, 1, :], op=ALU.mult))
                        along = slice(None) if d == 0 else slice(None, None, -1)
                        ins = V.tensor_tensor_scan(out=hd[:, d, along], data0=da[:, d, along],
                                                   data1=dq[:, d, along], initial=0.0, op0=ALU.mult, op1=ALU.add)
                    link(ins)
                    link(V.tensor_tensor(out=hd[:, 0, :], in0=hd[:, 0, :], in1=hd[:, 1, :], op=ALU.add))
                    V.tensor_tensor(out=y[:, g, :], in0=y[:, g, :], in1=hd[:, 0, :], op=ALU.mult).then_inc(y_ready, 1)
                for j in range(CONV):
                    n = HC + 3 * j
                    prod, acc = xp[:, 0, PAD:PAD + T], hd[:, 0, :]
                    eng.wait_ge(z_used_act, n_act(n))
                    eng.wait_ge(z_done, n + 2)
                    ins = V.tensor_tensor(out=prod, in0=dr[:, :], in1=bank[(n + 1) % 2][:, :], op=ALU.mult)
                    link(ins)
                    V.sem_inc(z_used_dve, 1)
                    for k in range(SHORT_W):
                        w = pB[:, PC_SHORT + k * CONV + j:][:, 0:1]
                        src = xp[:, 0, PAD - 1 + k:PAD - 1 + k + T]
                        if k == 0:
                            link(V.tensor_scalar(out=acc, in0=src, scalar1=w, scalar2=None, op0=ALU.mult))
                        else:
                            link(V.scalar_tensor_tensor(out=acc, in0=src, scalar=w, in1=acc, op0=ALU.mult, op1=ALU.add))
                    eng.wait_ge(z_done, n + 3)
                    link(V.tensor_tensor(out=y[:, HEADS + j, :], in0=acc, in1=bank[(n + 2) % 2][:, :], op=ALU.mult))
                    V.sem_inc(z_used_dve, 1)
                    V.sem_inc(y_ready, 1)
                for i in range(2):
                    eng.wait_ge(rms_root, i + 1)
                    link(V.reciprocal(rstd[:, i, :], rstd[:, i, :]))
                for c in range(MIX):
                    gain = pB[:, PC_GLRU + c:PC_GLRU + c + 1]
                    V.scalar_tensor_tensor(out=y[:, c, :], in0=y[:, c, :], scalar=gain, in1=rstd[:, int(c >= HEADS), :],
                                           op0=ALU.mult, op1=ALU.mult).then_inc(mix_ready, 1)
                eng.wait_ge(h_ready, TB)
                for tb in range(TB):
                    eng.wait_ge(o_done, tb + 1)
                    for i in range(2):
                        blk = h[:, tb, i * HALF_D:(i + 1) * HALF_D]
                        ins = V.scalar_tensor_tensor(out=blk, in0=blk, scalar=ALPHA, in1=bank[4 + 2 * (tb % 2) + i][:, :],
                                                     op0=ALU.mult, op1=ALU.add)
                    link(ins)
                    V.sem_inc(o_used, 1)
                    stats(tb)
                    if tb:
                        normalise(TB + tb, tb - 1)
                normalise(2 * TB, TB - 1)

            @block.tensor
            def _(eng):
                mm = nc.tensor.matmul
                eng.wait_ge(consts_ready, 1)
                eng.wait_ge(p_loaded, 8 * 16)
                nc.tensor.transpose(bank[4][:, 0:P], prow[:, 0, :], ident[:, :])
                nc.tensor.transpose(bank[4][:, P:P + 24], prow[0:24, 1, :], ident[0:24, 0:24]).then_inc(pT_ready, 1)
                for i in range(2 * TB):
                    tb, half = i // 2, i % 2
                    eng.wait_ge(h_ready, tb + 1)
                    after(eng, ht_ready, i - 1)
                    for k in range(4):
                        c = 4 * half + k
                        ins = nc.tensor.transpose(bank[i % 2][:, k * P:(k + 1) * P], h[:, tb, c * P:(c + 1) * P],
                                                  ident[:, :])
                    ins.then_inc(ht_done, 1)
                eng.wait_ge(ht_ready, 2 * TB)

                def z_chunk(n):
                    eng.wait_ge(w_loaded[n % NW], 16 * (n // NW + 1))
                    if n >= 2:
                        if by_dve[n - 2]:
                            eng.wait_ge(z_used_dve, n_dve(n - 2))
                        else:
                            eng.wait_ge(z_used_act, n_act(n - 2))
                    for k in range(KD):
                        ins = mm(bank[n % 2][:, :], wbuf[n % NW][:, k, :], hT[:, k, :], start=(k == 0), stop=(k == KD - 1))
                    ins.then_inc(z_done, 1)

                def head_gates(g):
                    if g == 0:
                        eng.wait_ge(g_loaded, 32)
                    eng.wait_ge(xc_ready, 2 * g + 2)
                    after(eng, decay_ready, 2 * g)
                    for d in range(2):
                        c = d * HEADS + g
                        mm(bank[4 + 2 * d][:, :], wa[:, c, :], xc[:, g % 2, d, :], start=True, stop=True)
                        mm(bank[5 + 2 * d][:, :], wx[:, c, :], xc[:, g % 2, d, :], start=True,
                           stop=True).then_inc(gates_done, 1)

                def sum_squares(i):
                    eng.wait_ge(sq_ready, i + 1)
                    first, last = i in (0, HEADS), i in (HEADS - 1, MIX - 1)
                    mm(bank[2 + int(i >= HEADS)][:, :], ones[:, :], sq[:, i % 2, :], start=first,
                       stop=last).then_inc(sums_done, 1)

                for n in range(HEADS):
                    z_chunk(n)
                for g in range(HEADS):
                    z_chunk(HX + g)
                    if g:
                        head_gates(g - 1)
                    if g > 2:
                        sum_squares(g - 3)
                z_chunk(HC)
                head_gates(HEADS - 1)
                z_chunk(HC + 1)
                sum_squares(HEADS - 3)
                z_chunk(HC + 2)
                sum_squares(HEADS - 2)
                for j in range(1, CONV):
                    for i in range(3):
                        z_chunk(HC + 3 * j + i)
                    sum_squares(HEADS - 2 + j)
                for i in range(HEADS - 2 + CONV, MIX):
                    sum_squares(i)
                eng.wait_ge(wo_loaded, 16)
                for tb in range(TB):
                    after(eng, o_used, tb - 1)
                    for c in range(MIX):
                        if tb == 0:
                            eng.wait_ge(mix_ready, c + 1)
                        for i in range(2):
                            ins = mm(bank[4 + 2 * (tb % 2) + i][:, :], y[:, c, tb * P:(tb + 1) * P],
                                     wo[:, c, i * HALF_D:(i + 1) * HALF_D], start=(c == 0), stop=(c == MIX - 1))
                    ins.then_inc(o_done, 1)


class ActPipeline:

    UB = 4

    def __init__(self, nc, a, sem, sb, bank, ident, xhi, xlo):
        self.nc, self.bank, self.ident, self.xhi, self.xlo = nc, bank, ident, xhi, xlo
        self.rows = a["peer_u"][0]
        self.raw = [sb(f"u_raw{i}", [P, D]) for i in range(self.UB)]
        self.hi = [sb(f"ut_hi{i}", [P, KD, P], F32R) for i in range(2)]
        self.lo = [sb(f"ut_lo{i}", [P, KD, P], F32R) for i in range(2)]
        self.gel = sb("gel", [P, 2, DTOK])
        self.loaded = [sem(f"u_loaded{i}") for i in range(self.UB)]
        self.turned, self.hi_ready, self.lo_ready = sem("u_transposed"), sem("ut_hi_ready"), sem("ut_lo_ready")
        self.done, self.ready = sem("act_done"), sem("gelu_ready")
        self.stored = [sem(f"act_stored{i}") for i in range(2)]

    def load(self, eng, m, r):
        at = slice(m * P, (m + 1) * P) if isinstance(m, int) else bass.ds(m * P, P)
        eng.dma_start(self.raw[r % self.UB][:, :], self.rows[at, :]).then_inc(self.loaded[r % self.UB], 16)

    def load_ahead(self, eng, m, r):
        eng.wait_ge(self.turned, 2 * m + 2)
        self.load(eng, m + self.UB, r)

    def store(self, eng, m, r, act_dram):
        eng.wait_ge(self.ready, m + 1)
        at = slice(m * P, (m + 1) * P) if isinstance(m, int) else bass.ds(m * P, P)
        eng.dma_start(act_dram[at, :], self.gel[:, r % 2, :]).then_inc(self.stored[r % 2], 16)

    def turn(self, eng, m, r, loads):
        for half in range(2):
            self.turn_half(eng, half, m, r, loads, half, 1)

    def turn_half(self, eng, half, m, r, loads, b, spare):
        raw = self.raw[r % self.UB]
        if half == 0:
            eng.wait_ge(self.loaded[r % self.UB], 16 * loads)
        after(eng, self.lo_ready, 2 * m + half - spare)
        for k in range(4):
            j = 4 * half + k
            ins = self.nc.tensor.transpose(self.bank[b][:, k * P:(k + 1) * P], raw[:, j * P:(j + 1) * P],
                                           self.ident[:, :])
        ins.then_inc(self.turned, 1)

    def product(self, eng, m, r, b=2, spare=1):
        eng.wait_ge(self.lo_ready, 2 * m + 2)
        after(eng, self.ready, m - spare)
        i = 0
        for k in range(KD):
            for u, x in ((self.hi, self.xhi), (self.hi, self.xlo), (self.lo, self.xhi)):
                ins = self.nc.tensor.matmul(self.bank[b + (r % 2) * spare][:, 0:DTOK], u[r % 2][:, k, :], x[:, k, 0:DTOK],
                                            start=(i == 0), stop=(i == 3 * KD - 1))
                i += 1
        ins.then_inc(self.done, 1)

    def upper(self, eng, m, r):
        for half in range(2):
            self.upper_half(eng, half, m, r, half, self.whole)

    def upper_half(self, eng, half, m, r, b, whole=None):
        if half == 0:
            after(eng, self.done, m - 1)
        eng.wait_ge(self.turned, 2 * m + half + 1)
        at = (slice(None), slice(4 * half, 4 * half + 4), slice(None))
        turned = self.bank[b].rearrange("p (k e) -> p k e", k=4)
        ins = self.nc.scalar.activation(self.hi[r % 2][at], turned, ACT.Copy)
        if whole is not None:
            after(eng, self.lo_ready, 2 * m + half - 1)
            ins = self.nc.scalar.activation(whole[:, 4 * half:4 * half + 4, :], turned, ACT.Copy)
        ins.then_inc(self.hi_ready, 1)

    def gelu(self, eng, m, r, b=None):
        eng.wait_ge(self.done, m + 1)
        self.nc.scalar.activation(self.gel[:, r % 2, :], self.bank[2 + r % 2 if b is None else b][:, 0:DTOK],
                                  ACT.Gelu).then_inc(self.ready, 1)

    def gelu_to_store(self, eng, m, r, stores):
        after(eng, self.stored[r % 2], 16 * stores)
        self.gelu(eng, m, r)

    def lower(self, eng, m, r):
        for half in range(2):
            at = (slice(None), slice(4 * half, 4 * half + 4), slice(None))
            eng.wait_ge(self.hi_ready, 2 * m + half + 1)
            self.nc.gpsimd.tensor_tensor(out=self.lo[r % 2][at], in0=self.whole[at],
                                         in1=self.hi[r % 2][at].bitcast(F32), op=ALU.subtract).then_inc(self.lo_ready, 1)

    def lower_half(self, eng, half, m, r, b):
        at = (slice(None), slice(4 * half, 4 * half + 4), slice(None))
        eng.wait_ge(self.hi_ready, 2 * m + half + 1)
        self.nc.vector.tensor_tensor(out=self.lo[r % 2][at], in0=self.bank[b].rearrange("p (k e) -> p k e", k=4),
                                     in1=self.hi[r % 2][at].bitcast(F32), op=ALU.subtract).then_inc(self.lo_ready, 1)


class GatherPath:

    FROM = 3

    def __init__(self, nc, a, sem, sb, x):
        self.nc, self.x = nc, x
        self.tables = (a["peer_u"][0], a["peer_v"][0])
        self.tile = [sb(f"gathered{i}", [P, D]) for i in range(RING)]
        self.index = [sb(f"row_index{i}", [P, 1], I32) for i in range(RING)]
        self.rows = sb("expert_rows", [P, SLOTS], I32)
        self.gate = sb("expert_gates", [P, SLOTS])
        self.act = sb("expert_acts", [P, SLOTS])
        self.gel = sb("expert_gelus", [P, SLOTS])
        self.product = sb("gather_product", [P, D])
        self.sum = [sb(f"gather_sum{i}", [P, D]) for i in range(2)]
        self.listed, self.index_ready = sem("rows_listed"), sem("row_index_ready")
        self.loaded = [sem(f"tile_gathered{i}") for i in range(RING)]
        self.used, self.gelu_ready, self.weights_ready = sem("tile_used"), sem("gather_gelu"), sem("gather_weights")

    def start(self, eng, kind, q, j):
        nc, r = self.nc, j % RING
        k = q - kind * SLOTS
        if not (isinstance(q, int) and q < RING):
            eng.wait_ge(self.used, q + (self.FROM + 1 - RING))
        nc.gpsimd.tensor_copy(self.index[r][:, :], self.rows[:, bass.ds(k, 1)]).then_inc(self.index_ready, 1)
        eng.wait_ge(self.index_ready, 2 * q + 1)
        eng.sem_inc(self.index_ready, 1)
        nc.gpsimd.indirect_dma_start(out=self.tile[r][:, :], out_offset=None, in_=self.tables[kind],
                                     in_offset=bass.IndirectOffsetOnAxis(ap=self.index[r][:, 0:1], axis=0),
                                     ).then_inc(self.loaded[r], 16)

    def use(self, eng, kind, q, j, loads):
        V, r = self.nc.vector, j % RING
        k = q - kind * SLOTS
        eng.wait_ge(self.loaded[r], 16 * loads)
        eng.wait_ge(self.used, q + (self.FROM - kind))
        if kind == 0:
            ins = V.scalar_tensor_tensor(out=self.product[:, :], in0=self.tile[r][:, :], scalar=1.0, in1=self.x,
                                         op0=ALU.mult, op1=ALU.mult, accum_out=self.act[:, bass.ds(k, 1)])
        else:
            y = self.sum[j % 2][:, :]
            ins = V.scalar_tensor_tensor(out=y, in0=self.tile[r][:, :], scalar=self.gate[:, bass.ds(k, 1)], in1=y,
                                         op0=ALU.mult, op1=ALU.add)
        ins.then_inc(self.used, 1)

    def weigh(self, eng):
        V = self.nc.vector
        eng.wait_ge(self.gelu_ready, 1)
        V.tensor_tensor(out=self.gate[:, :], in0=self.gate[:, :], in1=self.gel[:, :], op=ALU.mult)
        for y in self.sum:
            ins = V.memset(y[:, :], 0.0)
        ins.then_inc(self.weights_ready, 1)
        eng.wait_ge(self.weights_ready, 1)

    def gelu(self, eng):
        eng.wait_ge(self.used, SLOTS + self.FROM)
        self.nc.scalar.activation(self.gel[:, :], self.act[:, :], ACT.Gelu).then_inc(self.gelu_ready, 1)


def queries(nc, a, sem, bank, h, ident, xhi, xlo, acts, act_dram, top, pos, key):
    V, S, G = nc.vector, nc.scalar, nc.gpsimd
    UB = acts.UB
    with ExitStack() as st:
        sb = lambda name, shape, dt=F32: st.enter_context(nc.sbuf_tensor(name, shape, dt))
        NW = 3
        wq = [sb(f"wq{i}", [P, KD, P]) for i in range(NW)]
        wq_hi = [sb(f"wq_hi{i}", [P, KD, P], F32R) for i in range(2)]
        wq_lo = [sb(f"wq_lo{i}", [P, KD, P], F32R) for i in range(2)]
        keys = sb("keys", [P, 2, P])
        keysT = sb("keysT", [P, 2, P])
        qT = sb("qT", [P, 2, T])
        rep = sb("rep", [P, TB, KEYS])
        best = sb("best", [P, 2, TB, TOPK])
        cand = sb("cand", [P, TB, TOPK, TOPK])
        crep = sb("crep", [P, TB, TOPK * TOPK])

        wq_loaded = [sem(f"wq_loaded{i}") for i in range(NW)]
        keys_loaded, kt_done, kt_ready = sem("keys_loaded"), sem("keys_transposed"), sem("keysT_ready")
        t_done, x_hi_ready, x_lo_ready = (sem(n) for n in ("x1_transposed", "xhi_ready", "xlo_ready"))
        wq_hi_ready, wq_lo_ready = sem("wq_hi_ready"), sem("wq_lo_ready")
        q_done, qT_ready, s_done, s_used = (sem(n) for n in ("q_done", "qT_ready", "scores_done", "scores_used"))
        chain = sem("dve_chain_queries")

        with nc.Block() as block:
            @block.sync
            def _(eng):
                def load_wq(n):
                    after(eng, wq_lo_ready, n - NW + 1)
                    eng.dma_start(wq[n % NW][:, :, :],
                                  a["peer_wq"][0, :, n * P:(n + 1) * P].rearrange("(k p) c -> p k c", p=P)
                                  ).then_inc(wq_loaded[n % NW], 16)

                for n in range(NW):
                    load_wq(n)
                eng.dma_start(keys[:, 0, :], a["peer_k1"][0]).then_inc(keys_loaded, 16)
                eng.dma_start(keys[:, 1, :], a["peer_k2"][0]).then_inc(keys_loaded, 16)
                for m in range(UB):
                    acts.load(eng, m, m)
                for n in range(QC):
                    if n + NW < QC:
                        load_wq(n + NW)
                    acts.load_ahead(eng, n, n)
                    acts.store(eng, n, n, act_dram)

            @block.scalar
            def _(eng):
                def wq_upper(n):
                    eng.wait_ge(wq_loaded[n % NW], 16 * (n // NW + 1))
                    after(eng, q_done, n - 1)
                    S.activation(wq_hi[n % 2][:, :, :], wq[n % NW][:, :, :], ACT.Copy).then_inc(wq_hi_ready, 1)

                wq_upper(0)
                for i in range(2 * TB):
                    tb, half = i // 2, i % 2
                    eng.wait_ge(t_done, i + 1)
                    S.activation(xhi[:, 4 * half:4 * half + 4, tb * P:(tb + 1) * P],
                                 bank[half].rearrange("p (k t) -> p k t", k=4), ACT.Copy).then_inc(x_hi_ready, 1)
                wq_upper(1)
                eng.wait_ge(kt_done, 1)
                S.activation(keysT[:, :, :], bank[6][:, 0:2 * P].rearrange("p (s k) -> p s k", s=2),
                             ACT.Copy).then_inc(kt_ready, 1)
                acts.upper(eng, 0, 0)
                for n in range(QC):
                    eng.wait_ge(q_done, n + 1)
                    after(eng, s_done, n - 1)
                    S.activation(qT[:, n % 2, :], bank[4 + n % 2][:, :], ACT.Copy).then_inc(qT_ready, 1)
                    if n + 2 < QC:
                        wq_upper(n + 2)
                    acts.upper(eng, n + 1, n + 1)
                    acts.gelu_to_store(eng, n, n, n // 2)

            @block.gpsimd
            def _(eng):
                for n in range(QC):
                    if n:
                        acts.lower(eng, n - 1, n - 1)
                    eng.wait_ge(wq_hi_ready, n + 1)
                    G.tensor_tensor(out=wq_lo[n % 2][:, :, :], in0=wq[n % NW][:, :, :],
                                    in1=wq_hi[n % 2][:, :, :].bitcast(F32), op=ALU.subtract).then_inc(wq_lo_ready, 1)
                for m in (QC - 1, QC):
                    acts.lower(eng, m, m)

            @block.tensor
            def _(eng):
                mm, tr = nc.tensor.matmul, nc.tensor.transpose
                for i in range(2 * TB):
                    tb, half = i // 2, i % 2
                    after(eng, x_lo_ready, i - 1)
                    for k in range(4):
                        c = 4 * half + k
                        ins = tr(bank[half][:, k * P:(k + 1) * P], h[:, tb, c * P:(c + 1) * P], ident[:, :])
                    ins.then_inc(t_done, 1)
                eng.wait_ge(keys_loaded, 32)
                tr(bank[6][:, 0:P], keys[:, 0, :], ident[:, :])
                tr(bank[6][:, P:2 * P], keys[:, 1, :], ident[:, :]).then_inc(kt_done, 1)
                eng.wait_ge(x_lo_ready, 2 * TB)
                acts.turn(eng, 0, 0, 1)

                def scores(n):
                    if n == 0:
                        eng.wait_ge(kt_ready, 1)
                    eng.wait_ge(qT_ready, n + 1)
                    after(eng, s_used, n - 1)
                    for tb in range(TB):
                        ins = mm(bank[6 + n % 2][:, tb * P:(tb + 1) * P], qT[:, n % 2, tb * P:(tb + 1) * P],
                                 keysT[:, n % 2, :], start=True, stop=True)
                    ins.then_inc(s_done, 1)

                for n in range(QC):
                    eng.wait_ge(wq_lo_ready, n + 1)
                    after(eng, qT_ready, n - 1)
                    i = 0
                    for k in range(KD):
                        for w, x in ((wq_hi, xhi), (wq_hi, xlo), (wq_lo, xhi)):
                            ins = mm(bank[4 + n % 2][:, :], w[n % 2][:, k, :], x[:, k, :], start=(i == 0),
                                     stop=(i == 3 * KD - 1))
                            i += 1
                    ins.then_inc(q_done, 1)
                    acts.turn(eng, n + 1, n + 1, (n + 1) // UB + 1)
                    acts.product(eng, n, n)
                    scores(n)

            @block.vector
            def _(eng):
                link = Chain(eng, chain)
                for i in range(2 * TB):
                    tb, half = i // 2, i % 2
                    at = (slice(None), slice(4 * half, 4 * half + 4), slice(tb * P, (tb + 1) * P))
                    eng.wait_ge(x_hi_ready, i + 1)
                    V.tensor_tensor(out=xlo[at], in0=bank[half].rearrange("p (k t) -> p k t", k=4),
                                    in1=xhi[at].bitcast(F32), op=ALU.subtract).then_inc(x_lo_ready, 1)

                def top16(src, spare, vals, places):
                    for tb in range(TB):
                        ins = V.max(vals(tb)[:, 0:8], src(tb))
                    link(ins)
                    for tb in range(TB):
                        V.max_index(places(tb)[:, 0:8], vals(tb)[:, 0:8], src(tb))
                        ins = V.match_replace(spare(tb), vals(tb)[:, 0:8], src(tb), NEG)
                    link(ins)
                    for tb in range(TB):
                        ins = V.max(vals(tb)[:, 8:16], spare(tb))
                    link(ins)
                    for tb in range(TB):
                        ins = V.max_index(places(tb)[:, 8:16], vals(tb)[:, 8:16], spare(tb))
                    return ins

                for n in range(QC):
                    q, side = n // 2, n % 2
                    eng.wait_ge(s_done, n + 1)
                    top16(lambda tb: bank[6 + n % 2][:, tb * P:(tb + 1) * P], lambda tb: rep[:, tb, :],
                          lambda tb: best[:, side, tb, :], lambda tb: key[:, tb, q, side, :]).then_inc(s_used, 1)
                    if side == 1:
                        shape = [P, TB, TOPK, TOPK]
                        eng.wait_ge(s_used, n + 1)
                        link(V.tensor_tensor(out=cand[:, :, :, :], in0=best[:, 0, :, :].unsqueeze(3).broadcast_to(shape),
                                             in1=best[:, 1, :, :].unsqueeze(2).broadcast_to(shape), op=ALU.add))
                        link(top16(lambda tb: cand[:, tb, :, :].rearrange("p a b -> p (a b)"), lambda tb: crep[:, tb, :],
                                   lambda tb: top[:, tb, q, :], lambda tb: pos[:, tb, q, :]))


def gates(nc, sem, bank, ident, iota, acts, far, act_dram, top, pos, key, gates_dram):
    V, S = nc.vector, nc.scalar
    NT = 4
    PER = 4
    LOOPS = P // (2 * NT * PER)
    assert LOOPS == GATE_TURNS
    STEPS = P // NT
    UB = acts.UB
    first_of = lambda tb: QC + EXTRA + tb * PER_TB if tb >= 0 else QC
    with ExitStack() as st:
        sb = lambda name, shape, dt=F32: st.enter_context(nc.sbuf_tensor(name, shape, dt))
        stage = sb("stage", [P, KEYS, P])
        place = sb("place", [P, 2, SLOTS], U32)
        placef = sb("placef", [P, 2, SLOTS], BF16)
        keyf = sb("keyf", [P, QH, 2, TOPK], BF16)
        iotab = sb("iotab", [P, TOPK], BF16)
        hit = sb("hit", [P, QH, TOPK, TOPK], BF16)
        sel = sb("sel", [P, 3, SLOTS])
        ex = sb("ex", [P, QH, TOPK])
        total = sb("total", [P, QH])
        selT = sb("selT", [P, 3, P])
        first = sb("first", [P, 2, NT, KEYS])
        second = sb("second", [P, 2, NT, KEYS])

        chain, less_max, exp_ready, sel_ready, selT_done, selT_ready = (sem(n) for n in (
            "dve_chain_gates", "less_max", "exp_ready", "sel_ready", "sel_transposed", "selT_ready"))
        hot_ready, g_done, g_copied, g_stored = (sem(n) for n in (
            "one_hot_ready", "g_done", "g_copied", "g_stored"))

        def beside(eng, tb, step):
            base = first_of(tb)
            for j in range(EXTRA):
                step(base + j, base + j, None, None)
            if tb < 0:
                return
            with eng.Fori(0, LOOPS) as it:
                for j in range(PER):
                    step(base + EXTRA + it * PER + j, base + EXTRA + j, it, j)
            if tb == DT - 1:
                for m in range(MADE - CLOSING, MADE):
                    step(m, m, None, None)

        with nc.Block() as block:
            @block.vector
            def _(eng):
                link = Chain(eng, chain)
                link(V.tensor_copy(iotab[:, :], iota[:, 0:TOPK]))

                def select(tb):
                    p_in = pos[:, tb, :, :].rearrange("p q k -> p (q k)")
                    V.tensor_scalar(out=place[:, 0, :], in0=p_in, scalar1=4, scalar2=None, op0=ALU.logical_shift_right)
                    V.tensor_scalar(out=place[:, 1, :], in0=p_in, scalar1=TOPK - 1, scalar2=None, op0=ALU.bitwise_and)
                    link(V.tensor_copy(keyf[:, :, :, :], key[:, tb, :, :, :]))
                    link(V.tensor_copy(placef[:, :, :], place[:, :, :]))
                    if tb < DT:
                        after(eng, selT_done, tb)
                    for side in range(2):
                        flat = hit[:, :, :, :].rearrange("p q k j -> p (q k) j")
                        shape = [P, SLOTS, TOPK]
                        link(V.tensor_tensor(out=flat, in0=placef[:, side, :].unsqueeze(2).broadcast_to(shape),
                                             in1=iotab[:, :].unsqueeze(1).broadcast_to(shape), op=ALU.is_equal))
                        link(V.tensor_tensor(out=hit[:, :, :, :], in0=hit[:, :, :, :],
                                             in1=keyf[:, :, side, :].unsqueeze(2).broadcast_to([P, QH, TOPK, TOPK]),
                                             op=ALU.mult))
                        link(V.tensor_reduce(sel[:, side, :], flat, AX.X, ALU.add))
                    shape = [P, QH, TOPK]
                    V.tensor_tensor(out=ex[:, :, :], in0=top[:, tb, :, :], in1=top[:, tb, :, 0:1].broadcast_to(shape),
                                    op=ALU.subtract).then_inc(less_max, 1)
                    eng.wait_ge(exp_ready, 1 if tb == DT else tb + 2)
                    link(V.tensor_reduce(total[:, :], ex[:, :, :], AX.X, ALU.add))
                    link(V.reciprocal(total[:, :], total[:, :]))
                    dst = far.gate[:, :] if tb == DT else sel[:, 2, :]
                    ins = V.tensor_tensor(out=dst.rearrange("p (q k) -> p q k", q=QH), in0=ex[:, :, :],
                                          in1=total[:, :].unsqueeze(2).broadcast_to(shape), op=ALU.mult)
                    if tb == DT:
                        link(V.scalar_tensor_tensor(out=far.rows[:, :], in0=sel[:, 0, :], scalar=float(KEYS),
                                                    in1=sel[:, 1, :], op0=ALU.mult, op1=ALU.add))
                        V.sem_inc(far.listed, 1)
                        V.sem_inc(far.used, far.FROM)
                    else:
                        ins.then_inc(sel_ready, 1)

                for tb in range(-1, DT):
                    select(DT if tb < 0 else tb)

                    def step(m, r, it, j):
                        if it is None:
                            return
                        if j == 0:
                            eng.wait_ge(selT_ready, tb + 1)
                        for u in range(2):
                            n = tb * STEPS + it * (2 * PER) + (2 * j + u)
                            t = it * (2 * PER * NT) + (2 * j + u) * NT
                            eng.wait_ge(g_done, n + 1)
                            shape = [P, NT, KEYS]
                            V.tensor_tensor(out=second[:, u, :, :], in0=iota[:, :].unsqueeze(1).broadcast_to(shape),
                                            in1=selT[:, 1, bass.ds(t, NT)].unsqueeze(2).broadcast_to(shape),
                                            op=ALU.is_equal)
                            for q in range(NT):
                                ins = V.tensor_scalar(out=first[:, u, q, :], in0=iota[:, :],
                                                      scalar1=selT[:, 0, bass.ds(t + q, 1)],
                                                      scalar2=selT[:, 2, bass.ds(t + q, 1)], op0=ALU.is_equal, op1=ALU.mult)
                            ins.then_inc(hot_ready, 1)
                        each, q0 = BESIDE[tb] // PER, sum(BESIDE[:tb]) * LOOPS
                        for i in range(j * each, (j + 1) * each):
                            far.use(eng, 0, it * BESIDE[tb] + (q0 + i), i, it * (BESIDE[tb] // RING) + (q0 + i) // RING + 1)

                    beside(eng, tb, step)

            @block.gpsimd
            def _(eng):
                for tb in range(-1, DT):
                    def step(m, r, it, j):
                        if it is None and m == MADE - CLOSING:
                            for q in range(U_FROM + AHEAD, U_FROM + RING):
                                far.start(eng, 0, q, q)
                        acts.lower(eng, m + 1, r + 1)
                        if it is not None:
                            each, q0 = BESIDE[tb] // PER, sum(BESIDE[:tb]) * LOOPS + AHEAD
                            for i in range(j * each, (j + 1) * each):
                                far.start(eng, 0, it * BESIDE[tb] + (q0 + i), q0 + i)

                    beside(eng, tb, step)
                    if tb < 0:
                        eng.wait_ge(far.listed, 1)
                        for q in range(AHEAD):
                            far.start(eng, 0, q, q)

            @block.scalar
            def _(eng):
                eng.sem_inc(g_copied, 2)
                for tb in range(-1, DT):
                    eng.wait_ge(less_max, tb + 2)
                    S.activation(ex[:, :, :], ex[:, :, :], ACT.Exp).then_inc(exp_ready, 1)

                    def step(m, r, it, j):
                        base = first_of(tb) + EXTRA
                        if it is None:
                            stores = m // 2
                        else:
                            stores = it * (PER // 2) + (base + j) // 2
                        acts.upper(eng, m + 1, r + 1)
                        if it is None and tb >= 0 and m == base - 1:
                            eng.wait_ge(selT_done, tb + 1)
                            after(eng, hot_ready, tb * STEPS)
                            S.activation(selT[:, :, :], bank[6][:, 0:3 * P].rearrange("p (a t) -> p a t", a=3),
                                         ACT.Copy).then_inc(selT_ready, 1)
                            after(eng, g_stored, 16 * tb)
                        if it is not None:
                            for u in range(2):
                                n = tb * STEPS + it * (2 * PER) + (2 * j + u)
                                t = it * (2 * PER * NT) + (2 * j + u) * NT
                                eng.wait_ge(g_done, n + 3)
                                S.activation(stage[:, :, bass.ds(t, NT)],
                                             bank[4 + u].rearrange("p (t i) -> p i t", t=NT),
                                             ACT.Copy).then_inc(g_copied, 1)
                        acts.gelu_to_store(eng, m, r, stores)

                    beside(eng, tb, step)

            @block.tensor
            def _(eng):
                eng.sem_inc(g_done, 2)
                for tb in range(-1, DT):
                    def step(m, r, it, j):
                        base = first_of(tb) + EXTRA
                        acts.turn(eng, m + 1, r + 1, (m + 1) // UB + 1 if it is None else it + (r + 1) // UB + 1)
                        acts.product(eng, m, r)
                        if it is None and tb >= 0 and m == base - 1:
                            eng.wait_ge(sel_ready, tb + 1)
                            after(eng, selT_ready, tb)
                            for i in range(3):
                                ins = nc.tensor.transpose(bank[6][:, i * P:(i + 1) * P], sel[:, i, :], ident[:, :])
                            ins.then_inc(selT_done, 1)
                        if it is None:
                            return
                        for u in range(2):
                            n = tb * STEPS + it * (2 * PER) + (2 * j + u)
                            eng.wait_ge(hot_ready, n + 1)
                            eng.wait_ge(g_copied, n + 1)
                            for q in range(NT):
                                ins = nc.tensor.matmul(bank[4 + u][:, q * KEYS:(q + 1) * KEYS], second[:, u, q, :],
                                                       first[:, u, q, :], start=True, stop=True)
                            ins.then_inc(g_done, 1)

                    beside(eng, tb, step)

            @block.sync
            def _(eng):
                for tb in range(-1, DT):
                    def store_gates(i, n):
                        at = slice(i * KEYS // n, (i + 1) * KEYS // n)
                        eng.dma_start(gates_dram[at, :, tb * P:(tb + 1) * P].rearrange("i j t -> j i t"),
                                      stage[:, at, :]).then_inc(g_stored, 16)

                    def step(m, r, it, j):
                        if it is None and m == MADE - CLOSING:
                            eng.wait_ge(g_copied, DT * STEPS + 2)
                        if it is None and MADE - CLOSING <= m < MADE - 1:
                            i = m - (MADE - CLOSING)
                            for part in (0, 1) if i == 0 else (i + 1,):
                                store_gates(part, CLOSING)
                        acts.load_ahead(eng, m, r)
                        acts.store(eng, m, r, act_dram)

                    beside(eng, tb, step)
                    if 0 <= tb < DT - 1:
                        eng.wait_ge(g_copied, (tb + 1) * STEPS + 2)
                        store_gates(0, 1)
                eng.wait_ge(g_stored, 16 * (DT - 1 + CLOSING))
                for i in range(2):
                    eng.wait_ge(acts.stored[i], 16 * (MADE // 2))


def experts(nc, a, sem, bank, h, small, acts, far, act_dram, gates_dram, out):
    V, S, G = nc.vector, nc.scalar, nc.gpsimd
    SLOT = 4
    TURN = 2 * SLOT
    TURNS = (KEYS - MADE) // SLOT
    TAIL = TURNS * TURN
    STEPS = KEYS
    GATHERS = 12
    u_turns = (SLOTS - U_FROM) // GATHERS
    v_turns = TURNS - u_turns
    tail_tiles = SLOTS - v_turns * GATHERS
    assert u_turns * GATHERS == SLOTS - U_FROM and 0 <= tail_tiles <= STEPS - TAIL and 1 < u_turns < TURNS - 1
    LAST = (DT, *range(DT))
    is_live = lambda n, i: i % 2 == 0 and (not isinstance(n, int) or n < TAIL)

    q_of = lambda n: 2 * SLOTS - tail_tiles + n - TAIL

    def block_of(n):
        if n >= TAIL:
            return n - TURNS * SLOT
        return n // TURN * SLOT + n % TURN // 2 + (MADE if n % 2 == 0 else 0)

    with ExitStack() as st:
        sb = lambda name, shape, dt=F32: st.enter_context(nc.sbuf_tensor(name, shape, dt))
        v_raw = [sb(f"v_raw{i}", [P, D]) for i in range(SLOT)]
        g_in = [sb(f"g_in{i}", [P, DTOK]) for i in range(SLOT)]
        a_in = [sb(f"a_in{i}", [P, DTOK]) for i in range(2)]
        v_hi = [sb(f"v_hi{i}", [P, D], F32R) for i in range(SLOT)]
        v_lo = [sb(f"v_lo{i}", [P, D], F32R) for i in range(SLOT)]
        w32 = sb("w32", [P, 2, DTOK])
        w_hi = [sb(f"w_hi{i}", [P, DTOK], F32R) for i in range(SLOT)]
        w_lo = [sb(f"w_lo{i}", [P, DTOK], F32R) for i in range(SLOT)]
        ln = sb("ln2", [P, 2, D])
        bn = sb("bn2", [P, TB, 2, 6])
        mv = sb("mv2", [P, TB, 2])
        rs = sb("rs2", [P, TB, 1])

        v_loaded = [sem(f"v_loaded{i}") for i in range(SLOT)]
        g_loaded = [sem(f"g_loaded{i}") for i in range(SLOT)]
        a_loaded = [sem(f"a_loaded{i}") for i in range(2)]
        w_made, w_hi_ready, w_lo_ready, v_hi_ready, v_lo_ready = (sem(n) for n in (
            "w_made", "w_hi_ready", "w_lo_ready", "v_hi_ready", "v_lo_ready"))
        y_done = sem("y_step_done")
        ln2_loaded, var_ready, rstd_ready, norm_ready, out_ready, stored = (sem(n) for n in (
            "ln2_loaded", "var2_ready", "rstd2_ready", "norm2_ready", "out_ready", "out_stored"))
        chain, pool_chain = sem("dve_chain_experts"), sem("pool_chain_experts")

        def steps(eng, step, between=lambda: None, turn_start=lambda t, tiles: None):
            def turn(t, kind):
                q0 = U_FROM if kind == 0 else SLOTS - u_turns * GATHERS

                def tiles(i):
                    at = i // 2 * 3 + (0, 2)[i % 2]
                    for j in range(at, at + (2, 1)[i % 2]):
                        yield kind, t * GATHERS + (q0 + j), j, t * (GATHERS // RING) + (q0 + j) // RING + 1

                turn_start(t, tiles)
                for i in range(TURN):
                    step(t * TURN + i, i, t, tiles(i), tiles)

            turn(0, 0)
            with eng.Fori(1, u_turns) as t:
                turn(t, 0)
            between()
            with eng.Fori(u_turns, TURNS - 1) as t:
                turn(t, 1)
            turn(TURNS - 1, 1)
            for n in range(TAIL, STEPS):
                q = q_of(n)
                beside = [(1, q, q, q // RING + 1)] if q < 2 * SLOTS else []
                step(n, n % TURN, None, beside, None)

        v_rows = a["peer_v"][0]
        g_rows = gates_dram.rearrange("i j t -> (i j) t")
        rows = lambda b: slice(b * P, (b + 1) * P) if isinstance(b, int) else bass.ds(b * P, P)

        with nc.Block() as block:
            @block.sync
            def _(eng):
                def load_v(i, b):
                    eng.dma_start(v_raw[i % SLOT][:, :], v_rows[rows(b), :]).then_inc(v_loaded[i % SLOT], 16)

                def load_g(i, b):
                    eng.dma_start(g_in[i % SLOT][:, :], g_rows[rows(b), :]).then_inc(g_loaded[i % SLOT], 16)

                def load_a(i, b):
                    eng.dma_start(a_in[i % 2][:, :], act_dram[rows(b), :]).then_inc(a_loaded[i % 2], 16)

                for n in range(SLOT):
                    load_v(n, block_of(n))
                    load_g(n, block_of(n))
                for k in range(2):
                    load_a(k, k)
                eng.dma_start(ln[:, 0, :], a["ln2_g"][0].partition_broadcast(P)).then_inc(ln2_loaded, 16)
                eng.dma_start(ln[:, 1, :], a["ln2_b"][0].partition_broadcast(P)).then_inc(ln2_loaded, 16)

                def step(n, i, t, beside, tiles):
                    live = is_live(n, i)
                    static = isinstance(n, int)
                    if static and n + SLOT >= STEPS:
                        ahead = None
                    elif static:
                        ahead = block_of(n + SLOT)
                    else:
                        ahead = t * SLOT + (i // 2 + 2 + (MADE if live else 0))
                    if live and not (static and MADE + t * SLOT + i // 2 + acts.UB >= KEYS):
                        acts.load_ahead(eng, t * SLOT + (MADE + i // 2), MADE + i // 2)
                    if ahead is not None:
                        eng.wait_ge(v_lo_ready, n + 1)
                        load_v(i, ahead)
                    eng.wait_ge(w_made, n + 1)
                    if ahead is not None:
                        load_g(i, ahead)
                    if not live:
                        k = i // 2 if not (static and n >= TAIL) else block_of(n)
                        if static and block_of(n) + 2 < MADE:
                            load_a(k, block_of(n) + 2)
                        elif not static:
                            load_a(k, t * SLOT + i // 2 + 2)

                steps(eng, step)
                for at, tb in enumerate(LAST):
                    eng.wait_ge(out_ready, at + 1)
                    eng.dma_start(out[0, tb * P:(tb + 1) * P, :], h[:, tb, :]).then_inc(stored, 16)
                eng.wait_ge(stored, 16 * TB)

            @block.tensor
            def _(eng):
                mm = nc.tensor.matmul

                def outputs(n, i):
                    first, last = (isinstance(n, int) and n == e for e in (0, STEPS - 1))
                    r = i % SLOT
                    eng.wait_ge(v_lo_ready, n + 1)
                    eng.wait_ge(w_lo_ready, n + 1)
                    for tb in range(DT):
                        for w, v, begins, ends in ((w_hi, v_hi, first, False), (w_hi, v_lo, False, False),
                                                   (w_lo, v_hi, False, last)):
                            for half in range(2):
                                ins = mm(bank[2 + 2 * tb + half][:, :], w[r][:, tb * P:(tb + 1) * P],
                                         v[r][:, half * HALF_D:(half + 1) * HALF_D], start=begins, stop=ends)
                    ins.then_inc(y_done, 1)

                def step(n, i, t, beside, tiles):
                    if is_live(n, i):
                        m, r = t * SLOT + (MADE + i // 2), MADE + i // 2
                        more = not (isinstance(m, int) and m + 1 == KEYS)
                        if more:
                            acts.turn_half(eng, 0, m + 1, r + 1, (r + 1) // acts.UB + 1 + t, 0, 0)
                        acts.product(eng, m, r, 1, 0)
                        if more:
                            acts.turn_half(eng, 1, m + 1, r + 1, (r + 1) // acts.UB + 1 + t, 0, 0)
                    if not (isinstance(n, int) and n == 0):
                        outputs(n - 1, i - 1)

                steps(eng, step)
                outputs(STEPS - 1, STEPS - 1)

            @block.scalar
            def _(eng):
                def v_upper(n, i, t_loads):
                    r = i % SLOT
                    eng.wait_ge(v_loaded[r], 16 * t_loads)
                    if not (isinstance(n, int) and n < SLOT):
                        eng.wait_ge(y_done, n - SLOT + 1)
                    S.activation(v_hi[r][:, :], v_raw[r][:, :], ACT.Copy).then_inc(v_hi_ready, 1)

                def step(n, i, t, beside, tiles):
                    live = is_live(n, i)
                    m, r = (t * SLOT + (MADE + i // 2), MADE + i // 2) if live else (0, 0)
                    more = live and not (isinstance(m, int) and m + 1 == KEYS)
                    if more:
                        acts.upper_half(eng, 0, m + 1, r + 1, 0)
                    if not (isinstance(n, int) and n + 2 >= STEPS):
                        loads = (n + 2) // SLOT + 1 if isinstance(n, int) else t * (TURN // SLOT) + (i + 2) // SLOT + 1
                        v_upper(n + 2, i + 2, loads)
                    if live:
                        if isinstance(n, int) and n < 4:
                            eng.wait_ge(acts.stored[r % 2], 16 * (MADE // 2))
                        else:
                            eng.wait_ge(w_made, n - 3)
                        acts.gelu(eng, m, r, 1)
                    eng.wait_ge(w_made, n + 1)
                    S.activation(w_hi[i % SLOT][:, :], w32[:, i % 2, :], ACT.Copy).then_inc(w_hi_ready, 1)
                    if more:
                        acts.upper_half(eng, 1, m + 1, r + 1, 0)

                v_upper(0, 0, 1)
                v_upper(1, 1, 1)
                steps(eng, step, between=lambda: far.gelu(eng))

            @block.gpsimd
            def _(eng):
                def v_lower(n, i):
                    r = i % SLOT
                    eng.wait_ge(v_hi_ready, n + 1)
                    G.tensor_tensor(out=v_lo[r][:, :], in0=v_raw[r][:, :], in1=v_hi[r][:, :].bitcast(F32),
                                    op=ALU.subtract).then_inc(v_lo_ready, 1)

                def start(beside):
                    for kind, q, j, _ in beside:
                        if not (isinstance(q, int) and q < U_FROM + RING):
                            far.start(eng, kind, q, j)

                def step(n, i, t, beside, tiles):
                    if tiles is None:
                        ahead = q_of(n) + 2
                        for q in range(q_of(n) if n == TAIL else ahead, min(ahead + 1, 2 * SLOTS)):
                            far.start(eng, 1, q, q)
                    elif i + 1 < TURN:
                        start(tiles(i + 1))
                    if not (isinstance(n, int) and n + 2 >= STEPS):
                        v_lower(n + 2, i + 2)

                v_lower(0, 0)
                v_lower(1, 1)
                steps(eng, step, turn_start=lambda t, tiles: start(tiles(0)))
                eng.wait_ge(far.index_ready, 2 * 2 * SLOTS)
                link = Chain(eng, pool_chain)
                eng.wait_ge(ln2_loaded, 32)
                for at, tb in enumerate(LAST):
                    eng.wait_ge(var_ready, at + 1)
                    link(G.tensor_tensor(out=rs[:, tb, :], in0=mv[:, tb, 1:2], in1=small[:, 2:3], op=ALU.add))
                    G.tensor_tensor(out=rs[:, tb, :], in0=rs[:, tb, :], in1=small[:, 0:1],
                                    op=ALU.pow).then_inc(rstd_ready, 1)
                    eng.wait_ge(norm_ready, at + 1)
                    link(G.tensor_tensor(out=h[:, tb, :], in0=h[:, tb, :], in1=ln[:, 0, :], op=ALU.mult))
                    G.tensor_tensor(out=h[:, tb, :], in0=h[:, tb, :], in1=ln[:, 1, :], op=ALU.add).then_inc(out_ready, 1)

            @block.vector
            def _(eng):
                def step(n, i, t, beside, tiles):
                    live = is_live(n, i)
                    m, r = (t * SLOT + (MADE + i // 2), MADE + i // 2) if live else (0, 0)
                    more = live and not (isinstance(m, int) and m + 1 == KEYS)
                    if more:
                        acts.lower_half(eng, 0, m + 1, r + 1, 0)
                    for kind, q, j, loads in beside:
                        far.use(eng, kind, q, j, loads)
                    if live:
                        eng.wait_ge(acts.ready, m + 1)
                        act = acts.gel[:, r % 2, :]
                    else:
                        k = i // 2 if tiles is not None else block_of(n)
                        loads = block_of(n) // 2 + 1 if isinstance(n, int) else t * (SLOT // 2) + k // 2 + 1
                        eng.wait_ge(a_loaded[k % 2], 16 * loads)
                        act = a_in[k % 2][:, :]
                    loads = n // SLOT + 1 if isinstance(n, int) else t * (TURN // SLOT) + i // SLOT + 1
                    eng.wait_ge(g_loaded[i % SLOT], 16 * loads)
                    V.tensor_tensor(out=w32[:, i % 2, :], in0=act, in1=g_in[i % SLOT][:, :],
                                    op=ALU.mult).then_inc(w_made, 1)
                    eng.wait_ge(w_hi_ready, n + 1)
                    V.tensor_tensor(out=w_lo[i % SLOT][:, :], in0=w32[:, i % 2, :], in1=w_hi[i % SLOT][:, :].bitcast(F32),
                                    op=ALU.subtract).then_inc(w_lo_ready, 1)
                    if more:
                        acts.lower_half(eng, 1, m + 1, r + 1, 0)

                steps(eng, step, between=lambda: far.weigh(eng))
                link = Chain(eng, chain)
                link(V.scalar_tensor_tensor(out=h[:, DT, :], in0=h[:, DT, :], scalar=ALPHA, in1=far.sum[0][:, :],
                                            op0=ALU.mult, op1=ALU.add))
                link(V.tensor_tensor(out=h[:, DT, :], in0=h[:, DT, :], in1=far.sum[1][:, :], op=ALU.add))
                for at in range(TB + 1):
                    if at < TB:
                        tb = LAST[at]
                        if at == 1:
                            eng.wait_ge(y_done, STEPS)
                        if at:
                            for i in range(2):
                                blk = h[:, tb, i * HALF_D:(i + 1) * HALF_D]
                                ins = V.scalar_tensor_tensor(out=blk, in0=blk, scalar=ALPHA, in1=bank[2 + 2 * tb + i][:, :],
                                                             op0=ALU.mult, op1=ALU.add)
                            link(ins)
                        for i in range(2):
                            ins = V.bn_stats(bn[:, tb, i, :], h[:, tb, i * HALF_D:(i + 1) * HALF_D])
                        link(ins)
                        V.bn_aggr(mv[:, tb, :], bn[:, tb, :, :].rearrange("p a b -> p (a b)")).then_inc(var_ready, 1)
                    if at:
                        tb = LAST[at - 1]
                        eng.wait_ge(rstd_ready, at)
                        V.tensor_scalar(out=h[:, tb, :], in0=h[:, tb, :], scalar1=mv[:, tb, 0:1],
                                        scalar2=rs[:, tb, :], op0=ALU.subtract, op1=ALU.mult).then_inc(norm_ready, 1)


_INS = ["x", "ln_emb_g", "ln_emb_b", "w_in", "lru_conv_w", "lru_conv_b", "lru_wa", "lru_ba", "lru_wx", "lru_bx",
        "lru_lambda", "conv_w", "norm_lru_g", "norm_conv_g", "w_out", "ln1_g", "ln1_b",
        "peer_wq", "peer_k1", "peer_k2", "peer_u", "peer_v", "ln2_g", "ln2_b"]


def kernel(**inputs):
    import concourse.bacc as bacc
    from concourse.bass_utils import run_bass_kernel_spmd

    nc = bacc.Bacc("TRN2", target_bir_lowering=False, num_devices=1)
    arrays, args = {}, {}
    for name in _INS:
        v = np.ascontiguousarray(inputs[name])
        arrays[f"in_{name}"] = v
        args[name] = nc.dram_tensor(f"in_{name}", v.shape, F32, kind="ExternalInput").ap()
    out = nc.dram_tensor("out_0", (1, T, D), F32, kind="ExternalOutput").ap()
    gates_dram = nc.dram_tensor("gate_matrix", (KEYS, KEYS, DTOK), F32, kind="Internal").ap()
    act_dram = nc.dram_tensor("activations", (MADE * P, DTOK), F32, kind="Internal").ap()
    build(nc, args, out, gates_dram, act_dram)
    r = run_bass_kernel_spmd(nc, [arrays], core_ids=[0])
    return r.results[0]["out_0"]
```

```python
from contextlib import ExitStack

import numpy as np
import concourse.bass as bass
from concourse import mybir

F32 = mybir.dt.float32
F32R = mybir.dt.float32r
BF16 = mybir.dt.bfloat16
U32 = mybir.dt.uint32
I32 = mybir.dt.int32
ALU = mybir.AluOpType
ACT = mybir.ActivationFunctionType
AX = mybir.AxisListType

P = 128
T, D = 512, 1024
TB, KD = T // P, D // P
HALF_D = D // 2
HEADS = 8
CONV = 4
MIX = HEADS + CONV
LRU_W, SHORT_W = 4, 3
PAD = LRU_W - 1
LRU_C = 8.0
QH, TOPK = 8, 16
KEYS = 128
SLOTS = QH * TOPK
LN_EPS, RMS_EPS = 1e-5, 1e-6
ALPHA = 2.0 ** 0.25
NEG = -3.0e38

DT = TB - 1
DTOK = DT * P
QC = 2 * QH
QUERIES_LAST = 3
FIRST = 3
EXTRA = (3, 7, 7)
BESIDE_TOKENS = 16
CLOSING = 9
BY_QUERIES = QC + QUERIES_LAST
MADE = BY_QUERIES + FIRST + sum(EXTRA) + DT * BESIDE_TOKENS + CLOSING
RING = 4
AHEAD = 2
GATE_TURNS = 4
BESIDE = (4, 8, 8)
U_FROM = sum(BESIDE) * GATE_TURNS

PC_CONVW, PC_CONVB, PC_BA, PC_BX, PC_LAM = 0, 64, 80, 96, 112
PC_SHORT, PC_GAIN, PC_EMB_G, PC_EMB_B, PC_LN1_G, PC_LN1_B, PC_END = 0, 12, 24, 32, 40, 48, 56

COL_X, COL_GATE, COL_CB, COL_CC, COL_CX = 0, HEADS, 2 * HEADS, 2 * HEADS + CONV, 2 * HEADS + 2 * CONV


class Chain:

    def __init__(self, eng, sem):
        self.eng, self.sem, self.n = eng, sem, 0

    def __call__(self, ins):
        self.n += 1
        ins.then_inc(self.sem, 1)
        self.eng.wait_ge(self.sem, self.n)


def after(eng, sem, count):
    if not isinstance(count, int) or count > 0:
        eng.wait_ge(sem, count)


def build(nc, a, out, gates_dram, act_dram):
    ctx = ExitStack()
    with ctx:
        sem = lambda name: ctx.enter_context(nc.semaphore(name))
        sb = lambda name, shape, dt=F32: ctx.enter_context(nc.sbuf_tensor(name, shape, dt))
        bank = [ctx.enter_context(nc.psum_tensor(f"bank{i}", [P, 512], F32)) for i in range(8)]
        h = sb("h", [P, TB, D])
        ident = sb("ident", [P, P])
        ones = sb("ones", [P, P])
        iota = sb("iota", [P, KEYS])
        small = sb("small", [P, 3])
        pB = sb("pB", [P, PC_END])
        mixer(nc, a, sem, bank, h, ident, ones, iota, small, pB)
        xhi = sb("xhi", [P, KD, T], F32R)
        xlo = sb("xlo", [P, KD, T], F32R)
        acts = ActPipeline(nc, a, sem, sb, bank, ident, xhi, xlo)
        far = GatherPath(nc, a, sem, sb, h[:, DT, :])
        acts.whole = far.sum[0].rearrange("p (k e) -> p k e", k=KD)
        with ExitStack() as rs:
            rb = lambda name, shape, dt=F32: rs.enter_context(nc.sbuf_tensor(name, shape, dt))
            top = rb("top", [P, TB, QH, TOPK])
            pos = rb("pos", [P, TB, QH, TOPK], U32)
            key = rb("key", [P, TB, QH, 2, TOPK], U32)
            queries(nc, a, sem, bank, h, ident, pB, xhi, xlo, acts, act_dram, top, pos, key)
            gates(nc, sem, bank, ident, iota, acts, far, act_dram, top, pos, key, gates_dram)
        experts(nc, a, sem, bank, h, small, acts, far, act_dram, gates_dram, out)


class ByChannel:

    def __init__(self, nc, sem, name, h, bank, ident, gain, shift, whole, hi, lo):
        self.nc, self.h, self.bank, self.ident = nc, h, bank, ident
        self.gain, self.shift, self.whole, self.hi, self.lo = gain, shift, whole, hi, lo
        self.turned, self.whole_ready, self.hi_ready, self.ready = (sem(f"{name}_{n}") for n in (
            "turned", "whole_ready", "hi_ready", "split"))

    def turn(self, eng, tb, k):
        ins = self.nc.tensor.transpose(self.bank[k][:, tb * P:(tb + 1) * P], self.h[:, tb, k * P:(k + 1) * P],
                                       self.ident[:, :])
        if tb == TB - 1:
            ins.then_inc(self.turned, 1)

    def shape(self, eng, k):
        eng.wait_ge(self.turned, k + 1)
        after(eng, self.ready, k - 1)
        self.nc.scalar.activation(self.whole[:, k % 2, :], self.bank[k][:, :], ACT.Identity,
                                  scale=self.gain[:, k:k + 1], bias=self.shift[:, k:k + 1]).then_inc(self.whole_ready, 1)

    def split(self, eng, k):
        eng.wait_ge(self.whole_ready, k + 1)
        self.nc.vector.tensor_copy(self.hi[:, k, :], self.whole[:, k % 2, :]).then_inc(self.hi_ready, 1)
        eng.wait_ge(self.hi_ready, k + 1)
        self.nc.vector.tensor_tensor(out=self.lo[:, k, :], in0=self.whole[:, k % 2, :],
                                     in1=self.hi[:, k, :].bitcast(F32), op=ALU.subtract).then_inc(self.ready, 1)


def mixer(nc, a, sem, bank, h, ident, ones, iota, small, pB):
    V, S, G = nc.vector, nc.scalar, nc.gpsimd
    with ExitStack() as st:
        sb = lambda name, shape, dt=F32: st.enter_context(nc.sbuf_tensor(name, shape, dt))
        NW = 3
        hT_hi = sb("hT_hi", [P, KD, T], F32R)
        hT_lo = sb("hT_lo", [P, KD, T], F32R)
        wbuf = [sb(f"w_in{i}", [P, KD, P]) for i in range(NW)]
        w_hi = [sb(f"w_in_hi{i}", [P, KD, P], F32R) for i in range(2)]
        w_lo = [sb(f"w_in_lo{i}", [P, KD, P], F32R) for i in range(2)]
        wg = sb("gate_weights", [P, 2, 2, 2, P])
        wo = sb("wo", [P, MIX, D])
        y = sb("y", [P, MIX, T])
        ln = sb("ln", [P, 2, D])
        prow = sb("prow", [P, 2, P])
        pA = sb("pA", [P, P])
        hb = sb("hb", [P, 32])
        sp = sb("sp", [P, 2, 16])
        t16 = sb("t16", [P, 8, 16])
        xp = sb("xp", [P, 2, T + 2 * PAD])
        xc = sb("xc", [P, 2, 2, T])
        th = sb("th", [P, 2, 2, T])
        da = sb("da", [P, 2, T])
        dw = sb("dw", [P, 2, T])
        dq = sb("dq", [P, 2, T])
        hd = sb("hd", [P, 2, T])
        sq = sb("sq", [P, 2, T])
        rms = sb("rms", [P, 2, TB])
        bn = sb("bn", [P, TB, 2, 6])
        mv = sb("mv", [P, TB, 2])
        rs = sb("rs", [P, TB, 1])
        turner = ByChannel(nc, sem, "hT", h, bank, ident, pB[:, PC_EMB_G:PC_EMB_G + KD],
                           pB[:, PC_EMB_B:PC_EMB_B + KD], dq, hT_hi, hT_lo)

        x_loaded = [sem(f"x_loaded{i}") for i in range(TB)]
        w_loaded = [sem(f"w_loaded{i}") for i in range(NW)]
        g_loaded = [sem(f"gate_weights_loaded{i}") for i in range(2)]
        wo_loaded, ln_loaded, ln_ready, p_loaded = (sem(n) for n in (
            "wo_loaded", "ln_loaded", "ln_ready", "params_loaded"))
        consts_ready, pT_ready, p_ready, sp_ready, exp_lam = (sem(n) for n in (
            "consts_ready", "params_transposed", "params_ready", "softplus_ready", "exp_lambda"))
        var_ready, rstd_ready, norm_ready, h_ready = (sem(n) for n in (
            "var_ready", "rstd_ready", "norm_ready", "h_ready"))
        w_hi_ready, w_lo_ready = sem("w_in_hi_ready"), sem("w_in_lo_ready")
        z_done, z_used_act, z_used_dve = sem("z_done"), sem("z_used_act"), sem("z_used_dve")
        xc_ready, gates_done, factors_ready = (sem(n) for n in ("xc_ready", "gates_done", "factors_ready"))
        q_ready, root_ready, scan_ready, y_ready, sq_ready, sums_done = (sem(n) for n in (
            "q_ready", "root_ready", "scan_ready", "y_ready", "squares_ready", "sums_done"))
        ms_ready, rms_ready, wo_ready, o_done = (sem(n) for n in (
            "mean_squares_ready", "rms_ready", "wo_ready", "out_projection_done"))
        xp_zero, o_used = sem("xp_zero"), sem("out_projection_used")
        dve_chain, pool_chain, act_chain = sem("dve_chain"), sem("pool_chain"), sem("act_chain")

        order = []
        for j in range(CONV):
            order += [COL_CC + j, COL_CX + j, COL_CB + j]
        for g in range(HEADS):
            order += [COL_X + g, COL_GATE + g]
        HX = 3 * CONV
        by_dve = [n < HX and n % 3 > 0 for n in range(len(order))]
        n_act = lambda n: sum(not b for b in by_dve[:n + 1])
        n_dve = lambda n: sum(by_dve[:n + 1])
        rows_with = lambda n: range(2 * (n - 3), 2 * (n - 3) + 2) if 3 <= n < 3 + MIX // 2 else ()
        made = list(range(HEADS, MIX)) + list(range(HEADS))

        last = slice((TB - 1) * P, T)
        out_bank = lambda tb, i, half: bank[(4, 0)[i] + 2 * (tb % 2) + half]

        with nc.Block() as block:
            @block.sync
            def _(eng):
                for tb in range(TB):
                    eng.dma_start(h[:, tb, :], a["x"][0, tb * P:(tb + 1) * P, :]).then_inc(x_loaded[tb], 16)
                for n, c in enumerate(order):
                    after(eng, w_lo_ready, n - NW + 1)
                    eng.dma_start(wbuf[n % NW][:, :, :],
                                  a["w_in"][0, :, c * P:(c + 1) * P].rearrange("(k p) c -> p k c", p=P)
                                  ).then_inc(w_loaded[n % NW], 16)
                    for c in rows_with(n):
                        eng.dma_start(wo[:, c, :], a["w_out"][0, c * P:(c + 1) * P, :]).then_inc(wo_loaded, 16)

            @block.gpsimd
            def _(eng):
                link = Chain(eng, pool_chain)
                G.memset(ones[:, :], 1.0)
                link(G.memset(ident[:, :], 0.0))
                link(G.affine_select(out=ident[:, :], in_=ident[:, :], compare_op=ALU.not_equal, fill=1.0,
                                     base=0, pattern=[[-1, P]], channel_multiplier=1))
                G.iota(iota[:, :], [[1, KEYS]], base=0, channel_multiplier=0,
                       allow_small_or_imprecise_dtypes=True)
                G.memset(small[:, 0:1], -0.5)
                G.memset(small[:, 1:2], -1.0)
                G.memset(small[:, 2:3], LN_EPS).then_inc(consts_ready, 1)
                eng.wait_ge(consts_ready, 1)

                def invert_root(n):
                    tb = n % TB
                    eng.wait_ge(var_ready, n + 1)
                    link(G.tensor_tensor(out=rs[:, tb, :], in0=mv[:, tb, 1:2], in1=small[:, 2:3], op=ALU.add))
                    G.tensor_tensor(out=rs[:, tb, :], in0=rs[:, tb, :], in1=small[:, 0:1],
                                    op=ALU.pow).then_inc(rstd_ready, 1)

                def w_lower(n):
                    eng.wait_ge(w_hi_ready, n + 1)
                    G.tensor_tensor(out=w_lo[n % 2][:, :, :], in0=wbuf[n % NW][:, :, :],
                                    in1=w_hi[n % 2][:, :, :].bitcast(F32), op=ALU.subtract).then_inc(w_lo_ready, 1)

                def head_output(g):
                    eng.wait_ge(scan_ready, g + 1)
                    link(G.tensor_tensor(out=hd[:, 0, :], in0=hd[:, 0, :], in1=hd[:, 1, :], op=ALU.add))
                    eng.wait_ge(z_used_act, n_act(HX + 2 * g + 1))
                    G.tensor_tensor(out=y[:, g, :], in0=y[:, g, :], in1=hd[:, 0, :], op=ALU.mult).then_inc(y_ready, 1)
                    i = CONV + g
                    eng.wait_ge(y_ready, i + 1)
                    eng.wait_ge(sums_done, i - 1)
                    G.tensor_tensor(out=sq[:, i % 2, :], in0=y[:, g, :], in1=y[:, g, :], op=ALU.mult).then_inc(sq_ready, 1)

                for tb in range(TB):
                    invert_root(tb)
                G.memset(xp[:, :, :], 0.0).then_inc(xp_zero, 1)
                w_lower(0)
                w_lower(1)
                eng.wait_ge(ln_ready, 1)
                eng.wait_ge(turner.turned, KD)
                for n in range(2, HX):
                    w_lower(n)
                    if n // 2 <= TB:
                        blk = h[:, n // 2 - 1, :]
                        if n % 2 == 0:
                            link(G.tensor_tensor(out=blk, in0=blk, in1=ln[:, 0, :], op=ALU.mult))
                        else:
                            G.tensor_tensor(out=blk, in0=blk, in1=ln[:, 1, :], op=ALU.add).then_inc(h_ready, 1)
                for n in range(HX, len(order)):
                    w_lower(n)
                    if (n - HX) % 2 == 1 and n > HX + 3:
                        head_output((n - HX - 5) // 2)
                for g in (HEADS - 2, HEADS - 1):
                    head_output(g)
                eng.wait_ge(ms_ready, 1)
                for i in range(2):
                    ins = G.tensor_tensor(out=rms[:, i, :], in0=rms[:, i, :],
                                          in1=small[:, 0:1].broadcast_to([P, TB]), op=ALU.pow)
                ins.then_inc(rms_ready, 1)
                for tb in range(TB):
                    invert_root(TB + tb)

            @block.scalar
            def _(eng):
                rows = lambda r0, n, src: eng.dma_start(prow[r0 % P:r0 % P + n, r0 // P, :], src).then_inc(p_loaded, 16)
                rows(P + PC_EMB_G, 8, a["ln_emb_g"].rearrange("(h p) -> h p", p=P))
                rows(P + PC_EMB_B, 8, a["ln_emb_b"].rearrange("(h p) -> h p", p=P))
                rows(P + PC_SHORT, 12, a["conv_w"][0].rearrange("k (h p) -> (k h) p", p=P))
                rows(P + PC_GAIN, 8, a["norm_lru_g"][0].rearrange("(h p) -> h p", p=P))
                rows(P + PC_GAIN + 8, 4, a["norm_conv_g"][0].rearrange("(h p) -> h p", p=P))
                rows(P + PC_LN1_G, 8, a["ln1_g"][0].rearrange("(h p) -> h p", p=P))
                rows(P + PC_LN1_B, 8, a["ln1_b"][0].rearrange("(h p) -> h p", p=P))
                rows(PC_CONVW, 64, a["lru_conv_w"][0].rearrange("d k (h p) -> (d k h) p", p=P))
                rows(PC_CONVB, 16, a["lru_conv_b"][0].rearrange("d (h p) -> (d h) p", p=P))
                rows(PC_BA, 16, a["lru_ba"][0].rearrange("d (h p) -> (d h) p", p=P))
                rows(PC_BX, 16, a["lru_bx"][0].rearrange("d (h p) -> (d h) p", p=P))
                rows(PC_LAM, 16, a["lru_lambda"][0].rearrange("d (h p) -> (d h) p", p=P))
                for i, name in enumerate(("ln_emb_g", "ln_emb_b")):
                    eng.dma_start(ln[:, i, :], a[name].partition_broadcast(P)).then_inc(ln_loaded, 16)

                def load_gate_weights(g):
                    for i, name in enumerate(("lru_wa", "lru_wx")):
                        eng.dma_start(wg[:, g % 2, i, :, :], a[name][0, :, g].rearrange("d i j -> i d j")
                                      ).then_inc(g_loaded[g % 2], 16)

                def w_upper(n):
                    if n < len(order):
                        eng.wait_ge(w_loaded[n % NW], 16 * (n // NW + 1))
                        S.activation(w_hi[n % 2][:, :, :], wbuf[n % NW][:, :, :], ACT.Copy).then_inc(w_hi_ready, 1)

                load_gate_weights(0)
                load_gate_weights(1)
                link = Chain(eng, act_chain)
                w_upper(0)
                w_upper(1)
                eng.wait_ge(pT_ready, 1)
                S.activation(pB[:, :], bank[7][:, last][:, 0:PC_END], ACT.Copy)
                S.activation(pA[:, :], bank[6][:, last], ACT.Copy).then_inc(p_ready, 1)
                eng.wait_ge(p_ready, 1)
                for k in range(KD):
                    turner.shape(eng, k)
                eng.wait_ge(exp_lam, 1)
                S.activation(t16[:, 2, :], t16[:, 1, :], ACT.Exp, scale=-1.0).then_inc(exp_lam, 1)

                def squares(i):
                    eng.wait_ge(y_ready, i + 1)
                    after(eng, sums_done, i - 1)
                    S.activation(sq[:, i % 2, :], y[:, made[i], :], ACT.Square).then_inc(sq_ready, 1)

                def roots(g):
                    for d in range(2):
                        eng.wait_ge(q_ready, 2 * g + d + 1)
                        S.activation(dq[:, d, :], dq[:, d, :], ACT.Sqrt, scale=0.25).then_inc(root_ready, 1)

                def scale_rows(c):
                    eng.wait_ge(wo_loaded, 16 * (c + 1))
                    S.activation(wo[:, c, :], wo[:, c, :], ACT.Identity, scale=pB[:, PC_GAIN + c:PC_GAIN + c + 1]
                                 ).then_inc(wo_ready, 1)

                for j in range(CONV):
                    for i in range(3):
                        n = 3 * j + i
                        eng.wait_ge(z_done, n + 1)
                        w_upper(n + 2)
                        if i == 0:
                            after(eng, y_ready, j)
                            S.activation(dw[:, 0, :], bank[n % 2][:, :], ACT.Copy).then_inc(z_used_act, 1)
                        for c in rows_with(n - 1):
                            scale_rows(c)
                    if j:
                        squares(j - 1)
                squares(CONV - 1)

                def head_input(g):
                    n = HX + 2 * g
                    eng.wait_ge(z_done, n + 1)
                    w_upper(n + 2)
                    after(eng, xc_ready, 2 * (g - 1))
                    S.activation(xp[:, g % 2, PAD:PAD + T], bank[n % 2][:, :], ACT.Copy).then_inc(z_used_act, 1)

                head_input(0)
                eng.wait_ge(sp_ready, 1)
                for g in range(HEADS):
                    n = HX + 2 * g + 1
                    eng.wait_ge(z_done, n + 1)
                    w_upper(n + 2)
                    S.activation(y[:, g, :], bank[n % 2][:, :], ACT.Gelu_apprx_tanh).then_inc(z_used_act, 1)
                    if g + 1 < HEADS:
                        head_input(g + 1)
                    for d in range(2):
                        c = d * HEADS + g
                        eng.wait_ge(gates_done, 2 * g + d + 1)
                        after(eng, scan_ready, g)
                        S.activation(th[:, d, 0, :], bank[4 + 2 * d][:, :], ACT.Tanh, scale=0.5, bias=hb[:, c:c + 1])
                        link(S.activation(th[:, d, 1, :], bank[5 + 2 * d][:, :], ACT.Tanh, scale=0.5,
                                          bias=hb[:, 16 + c:17 + c]))
                        S.activation(dw[:, d, :], th[:, d, 0, :], ACT.Tanh, scale=sp[:, 0, c:c + 1],
                                     bias=sp[:, 0, c:c + 1])
                        link(S.activation(da[:, d, :], th[:, d, 0, :], ACT.Exp, scale=sp[:, 1, c:c + 1],
                                          bias=sp[:, 1, c:c + 1]))
                        S.activation(th[:, d, 0, :], da[:, d, :], ACT.Square).then_inc(factors_ready, 1)
                    if g + 2 < HEADS:
                        load_gate_weights(g + 2)
                    roots(g)

            @block.vector
            def _(eng):
                link = Chain(eng, dve_chain)

                def stats(tb):
                    for i in range(2):
                        ins = V.bn_stats(bn[:, tb, i, :], h[:, tb, i * HALF_D:(i + 1) * HALF_D])
                    link(ins)
                    V.bn_aggr(mv[:, tb, :], bn[:, tb, :, :].rearrange("p a b -> p (a b)")).then_inc(var_ready, 1)

                def normalise(n, tb):
                    eng.wait_ge(rstd_ready, n)
                    V.tensor_scalar(out=h[:, tb, :], in0=h[:, tb, :], scalar1=mv[:, tb, 0:1], scalar2=rs[:, tb, :],
                                    op0=ALU.subtract, op1=ALU.mult).then_inc(norm_ready, 1)

                for tb in range(TB):
                    eng.wait_ge(x_loaded[tb], 16)
                    stats(tb)
                    if tb:
                        normalise(tb, tb - 1)
                normalise(TB, TB - 1)
                for k in range(KD):
                    turner.split(eng, k)

                eng.wait_ge(ln_loaded, 32)
                V.tensor_scalar(out=ln[:, :, :], in0=ln[:, :, :], scalar1=ALPHA, scalar2=None,
                                op0=ALU.mult).then_inc(ln_ready, 1)

                eng.wait_ge(p_ready, 1)
                neg, mag, e, s, s2, poly = (t16[:, i, :] for i in range(6))
                V.tensor_scalar(out=hb[:, :], in0=pA[:, PC_BA:PC_BA + 32], scalar1=0.5, scalar2=None, op0=ALU.mult)
                link(V.tensor_scalar(out=neg, in0=pA[:, PC_LAM:PC_LAM + 16], scalar1=-1.0, scalar2=None, op0=ALU.mult))
                V.tensor_tensor(out=mag, in0=neg, in1=pA[:, PC_LAM:PC_LAM + 16], op=ALU.max).then_inc(exp_lam, 1)
                eng.wait_ge(exp_lam, 2)
                link(V.tensor_scalar(out=s, in0=e, scalar1=2.0, scalar2=None, op0=ALU.add))
                link(V.reciprocal(s, s))
                link(V.tensor_tensor(out=s, in0=s, in1=e, op=ALU.mult))
                link(V.tensor_tensor(out=s2, in0=s, in1=s, op=ALU.mult))
                link(V.tensor_scalar(out=poly, in0=s2, scalar1=1.0 / 15, scalar2=1.0 / 13, op0=ALU.mult, op1=ALU.add))
                for k in (11, 9, 7, 5, 3, 1):
                    link(V.tensor_tensor(out=poly, in0=poly, in1=s2, op=ALU.mult))
                    link(V.tensor_scalar(out=poly, in0=poly, scalar1=1.0 / k, scalar2=None, op0=ALU.add))
                link(V.tensor_tensor(out=poly, in0=poly, in1=s, op=ALU.mult))
                link(V.tensor_scalar(out=neg, in0=neg, scalar1=0.0, scalar2=LRU_C / 2, op0=ALU.max, op1=ALU.mult))
                link(V.scalar_tensor_tensor(out=sp[:, 0, :], in0=poly, scalar=LRU_C, in1=neg, op0=ALU.mult, op1=ALU.add))
                V.tensor_scalar(out=sp[:, 1, :], in0=sp[:, 0, :], scalar1=-1.0, scalar2=None,
                                op0=ALU.mult).then_inc(sp_ready, 1)

                eng.wait_ge(xp_zero, 1)
                for j in range(CONV):
                    n = 3 * j
                    prod, acc = xp[:, 0, PAD:PAD + T], hd[:, 0, :]
                    eng.wait_ge(z_used_act, n_act(n))
                    eng.wait_ge(z_done, n + 2)
                    link(V.tensor_tensor(out=prod, in0=dw[:, 0, :], in1=bank[(n + 1) % 2][:, :], op=ALU.mult))
                    V.sem_inc(z_used_dve, 1)
                    for k in range(SHORT_W):
                        w = pB[:, PC_SHORT + k * CONV + j:][:, 0:1]
                        src = xp[:, 0, PAD - 1 + k:PAD - 1 + k + T]
                        if k == 0:
                            link(V.tensor_scalar(out=acc, in0=src, scalar1=w, scalar2=None, op0=ALU.mult))
                        else:
                            link(V.scalar_tensor_tensor(out=acc, in0=src, scalar=w, in1=acc, op0=ALU.mult, op1=ALU.add))
                    eng.wait_ge(z_done, n + 3)
                    link(V.tensor_tensor(out=y[:, HEADS + j, :], in0=acc, in1=bank[(n + 2) % 2][:, :], op=ALU.mult))
                    V.sem_inc(z_used_dve, 1)
                    V.sem_inc(y_ready, 1)

                for hd_i in range(HEADS + 1):
                    if hd_i < HEADS:
                        eng.wait_ge(z_used_act, n_act(HX + 2 * hd_i))
                        x0 = xp[:, hd_i % 2, :]
                        after(eng, gates_done, 2 * (hd_i - 1))
                        for k in range(LRU_W):
                            for d in range(2):
                                c = d * HEADS + hd_i
                                w = pA[:, PC_CONVW + (d * LRU_W + k) * HEADS + hd_i:][:, 0:1]
                                o, src = xc[:, hd_i % 2, d, :], x0[:, d * PAD + k:d * PAD + k + T]
                                if k == 0:
                                    ins = V.tensor_scalar(out=o, in0=src, scalar1=w,
                                                          scalar2=pA[:, PC_CONVB + c:PC_CONVB + c + 1],
                                                          op0=ALU.mult, op1=ALU.add)
                                else:
                                    ins = V.scalar_tensor_tensor(out=o, in0=src, scalar=w, in1=o,
                                                                 op0=ALU.mult, op1=ALU.add)
                                if k == LRU_W - 1:
                                    ins.then_inc(xc_ready, 1)
                            if k < LRU_W - 1:
                                link(ins)
                    if hd_i == 0:
                        continue
                    g = hd_i - 1
                    for d in range(2):
                        eng.wait_ge(factors_ready, 2 * g + d + 1)
                        V.scalar_tensor_tensor(out=dq[:, d, :], in0=th[:, d, 0, :], scalar=1.0, in1=dw[:, d, :],
                                               op0=ALU.add, op1=ALU.mult).then_inc(q_ready, 1)
                        link(V.scalar_tensor_tensor(out=th[:, d, 1, :], in0=th[:, d, 1, :], scalar=1.0,
                                                    in1=xc[:, g % 2, d, :], op0=ALU.add, op1=ALU.mult))
                    for d in range(2):
                        eng.wait_ge(root_ready, 2 * g + d + 1)
                        link(V.tensor_tensor(out=dq[:, d, :], in0=dq[:, d, :], in1=th[:, d, 1, :], op=ALU.mult))
                        if d == 0:
                            eng.wait_ge(y_ready, CONV + g)
                        along = slice(None) if d == 0 else slice(None, None, -1)
                        ins = V.tensor_tensor_scan(out=hd[:, d, along], data0=da[:, d, along],
                                                   data1=dq[:, d, along], initial=0.0, op0=ALU.mult, op1=ALU.add)
                    link(ins)
                    V.sem_inc(scan_ready, 1)
                eng.wait_ge(sums_done, MIX)
                for i in range(2):
                    ins = V.tensor_scalar(out=rms[:, i, :], in0=bank[2][:, i * TB:(i + 1) * TB],
                                          scalar1=1.0 / (P * (HEADS, CONV)[i]), scalar2=RMS_EPS, op0=ALU.mult, op1=ALU.add)
                ins.then_inc(ms_ready, 1)
                eng.wait_ge(rms_ready, 1)
                eng.wait_ge(h_ready, TB)
                for tb in range(TB):
                    eng.wait_ge(o_done, tb + 1)
                    for i in (1, 0):
                        for half in range(2):
                            blk = h[:, tb, half * HALF_D:(half + 1) * HALF_D]
                            ins = V.scalar_tensor_tensor(out=blk, in0=out_bank(tb, i, half)[:, :],
                                                         scalar=rms[:, i, tb:tb + 1], in1=blk,
                                                         op0=ALU.mult, op1=ALU.add)
                        link(ins)
                    V.sem_inc(o_used, 1)
                    stats(tb)
                    if tb:
                        normalise(TB + tb, tb - 1)
                normalise(2 * TB, TB - 1)

            @block.tensor
            def _(eng):
                mm = nc.tensor.matmul
                eng.wait_ge(consts_ready, 1)
                for tb in range(TB):
                    if tb == TB - 1:
                        eng.wait_ge(p_loaded, 12 * 16)
                        nc.tensor.transpose(bank[6][:, last], prow[:, 0, :], ident[:, :])
                        nc.tensor.transpose(bank[7][:, last][:, 0:PC_END], prow[0:PC_END, 1, :],
                                            ident[0:PC_END, 0:PC_END]).then_inc(pT_ready, 1)
                    eng.wait_ge(norm_ready, tb + 1)
                    for k in range(KD):
                        if tb == TB - 1 and k == 6:
                            eng.wait_ge(p_ready, 1)
                        turner.turn(eng, tb, k)

                def z_chunk(n):
                    eng.wait_ge(w_lo_ready, n + 1)
                    if n >= 2:
                        if by_dve[n - 2]:
                            eng.wait_ge(z_used_dve, n_dve(n - 2))
                        else:
                            eng.wait_ge(z_used_act, n_act(n - 2))
                    i = 0
                    for k in range(KD):
                        if n == 0:
                            eng.wait_ge(turner.ready, k + 1)
                        for w, x in ((w_hi, hT_hi), (w_hi, hT_lo), (w_lo, hT_hi)):
                            ins = mm(bank[n % 2][:, :], w[n % 2][:, k, :], x[:, k, :], start=(i == 0),
                                     stop=(i == 3 * KD - 1))
                            i += 1
                    ins.then_inc(z_done, 1)

                def head_gates(g):
                    eng.wait_ge(g_loaded[g % 2], 32 * (g // 2 + 1))
                    after(eng, factors_ready, 2 * g)
                    for d in range(2):
                        if d == 0:
                            eng.wait_ge(xc_ready, 2 * g + 2)
                        for i in range(2):
                            ins = mm(bank[4 + 2 * d + i][:, :], wg[:, g % 2, i, d, :], xc[:, g % 2, d, :],
                                     start=True, stop=True)
                        ins.then_inc(gates_done, 1)

                def sum_squares(i):
                    eng.wait_ge(sq_ready, i + 1)
                    conv = made[i] >= HEADS
                    for tb in range(TB):
                        at = int(conv) * TB + tb
                        ins = mm(bank[2][:, at:at + 1], sq[:, i % 2, tb * P:(tb + 1) * P], ones[:, 0:1],
                                 start=(i == 0 and tb == 0), stop=(i == MIX - 1 and tb == TB - 1))
                    ins.then_inc(sums_done, 1)

                for j in range(CONV):
                    for i in range(3):
                        z_chunk(3 * j + i)
                    if j > 1:
                        sum_squares(j - 2)
                z_chunk(HX)
                for g in range(HEADS):
                    z_chunk(HX + 2 * g + 1)
                    if g + 1 < HEADS:
                        z_chunk(HX + 2 * g + 2)
                    sum_squares(CONV - 2 + g)
                    head_gates(g)
                eng.wait_ge(wo_ready, MIX)
                eng.wait_ge(z_used_act, n_act(len(order) - 1))
                for tb in range(TB):
                    after(eng, o_used, tb - 1)
                    for c in range(HEADS, MIX):
                        for half in range(2):
                            mm(out_bank(tb, 1, half)[:, :], y[:, c, tb * P:(tb + 1) * P],
                               wo[:, c, half * HALF_D:(half + 1) * HALF_D], start=(c == HEADS), stop=(c == MIX - 1))
                    if tb == 0:
                        eng.wait_ge(factors_ready, 2 * HEADS)
                    for c in range(HEADS):
                        if tb == 0:
                            eng.wait_ge(y_ready, CONV + c + 1)
                            if c == HEADS - 1:
                                sum_squares(MIX - 2)
                                sum_squares(MIX - 1)
                        for half in range(2):
                            ins = mm(out_bank(tb, 0, half)[:, :], y[:, c, tb * P:(tb + 1) * P],
                                     wo[:, c, half * HALF_D:(half + 1) * HALF_D], start=(c == 0), stop=(c == HEADS - 1))
                    ins.then_inc(o_done, 1)
                    if tb == 0:
                        eng.wait_ge(ms_ready, 1)


class ActPipeline:

    UB = 4

    def __init__(self, nc, a, sem, sb, bank, ident, xhi, xlo):
        self.nc, self.bank, self.ident, self.xhi, self.xlo = nc, bank, ident, xhi, xlo
        self.rows = a["peer_u"][0]
        self.raw = [sb(f"u_raw{i}", [P, D]) for i in range(self.UB)]
        self.hi = [sb(f"ut_hi{i}", [P, KD, P], F32R) for i in range(2)]
        self.lo = [sb(f"ut_lo{i}", [P, KD, P], F32R) for i in range(2)]
        self.gel = sb("gel", [P, 2, DTOK])
        self.loaded = [sem(f"u_loaded{i}") for i in range(self.UB)]
        self.turned, self.hi_ready, self.lo_ready = sem("u_transposed"), sem("ut_hi_ready"), sem("ut_lo_ready")
        self.done, self.ready = sem("act_done"), sem("gelu_ready")
        self.stored = [sem(f"act_stored{i}") for i in range(2)]

    def load(self, eng, m, r):
        at = slice(m * P, (m + 1) * P) if isinstance(m, int) else bass.ds(m * P, P)
        eng.dma_start(self.raw[r % self.UB][:, :], self.rows[at, :]).then_inc(self.loaded[r % self.UB], 16)

    def load_ahead(self, eng, m, r):
        eng.wait_ge(self.turned, 2 * m + 2)
        self.load(eng, m + self.UB, r)

    def store(self, eng, m, r, act_dram):
        eng.wait_ge(self.ready, m + 1)
        at = slice(m * P, (m + 1) * P) if isinstance(m, int) else bass.ds(m * P, P)
        eng.dma_start(act_dram[at, :], self.gel[:, r % 2, :]).then_inc(self.stored[r % 2], 16)

    def turn(self, eng, m, r, loads):
        for half in range(2):
            self.turn_half(eng, half, m, r, loads, half, 1)

    def turn_half(self, eng, half, m, r, loads, b, spare):
        raw = self.raw[r % self.UB]
        if half == 0:
            eng.wait_ge(self.loaded[r % self.UB], 16 * loads)
        after(eng, self.lo_ready, 2 * m + half - spare)
        for k in range(4):
            j = 4 * half + k
            ins = self.nc.tensor.transpose(self.bank[b][:, k * P:(k + 1) * P], raw[:, j * P:(j + 1) * P],
                                           self.ident[:, :])
        ins.then_inc(self.turned, 1)

    def product(self, eng, m, r, b=2, spare=1):
        eng.wait_ge(self.lo_ready, 2 * m + 2)
        after(eng, self.ready, m - spare)
        i = 0
        for k in range(KD):
            for u, x in ((self.hi, self.xhi), (self.hi, self.xlo), (self.lo, self.xhi)):
                ins = self.nc.tensor.matmul(self.bank[b + (r % 2) * spare][:, 0:DTOK], u[r % 2][:, k, :], x[:, k, 0:DTOK],
                                            start=(i == 0), stop=(i == 3 * KD - 1))
                i += 1
        ins.then_inc(self.done, 1)

    def upper(self, eng, m, r):
        for half in range(2):
            self.upper_half(eng, half, m, r, half, self.whole)

    def upper_half(self, eng, half, m, r, b, whole=None):
        if half == 0:
            after(eng, self.done, m - 1)
        eng.wait_ge(self.turned, 2 * m + half + 1)
        at = (slice(None), slice(4 * half, 4 * half + 4), slice(None))
        turned = self.bank[b].rearrange("p (k e) -> p k e", k=4)
        ins = self.nc.scalar.activation(self.hi[r % 2][at], turned, ACT.Copy)
        if whole is not None:
            after(eng, self.lo_ready, 2 * m + half - 1)
            ins = self.nc.scalar.activation(whole[:, 4 * half:4 * half + 4, :], turned, ACT.Copy)
        ins.then_inc(self.hi_ready, 1)

    def gelu(self, eng, m, r, b=None):
        eng.wait_ge(self.done, m + 1)
        self.nc.scalar.activation(self.gel[:, r % 2, :], self.bank[2 + r % 2 if b is None else b][:, 0:DTOK],
                                  ACT.Gelu).then_inc(self.ready, 1)

    def gelu_to_store(self, eng, m, r, stores):
        after(eng, self.stored[r % 2], 16 * stores)
        self.gelu(eng, m, r)

    def lower(self, eng, m, r):
        for half in range(2):
            at = (slice(None), slice(4 * half, 4 * half + 4), slice(None))
            eng.wait_ge(self.hi_ready, 2 * m + half + 1)
            self.nc.gpsimd.tensor_tensor(out=self.lo[r % 2][at], in0=self.whole[at],
                                         in1=self.hi[r % 2][at].bitcast(F32), op=ALU.subtract).then_inc(self.lo_ready, 1)

    def lower_half(self, eng, half, m, r, b):
        at = (slice(None), slice(4 * half, 4 * half + 4), slice(None))
        eng.wait_ge(self.hi_ready, 2 * m + half + 1)
        self.nc.vector.tensor_tensor(out=self.lo[r % 2][at], in0=self.bank[b].rearrange("p (k e) -> p k e", k=4),
                                     in1=self.hi[r % 2][at].bitcast(F32), op=ALU.subtract).then_inc(self.lo_ready, 1)


class GatherPath:

    FROM = 3

    def __init__(self, nc, a, sem, sb, x):
        self.nc, self.x = nc, x
        self.tables = (a["peer_u"][0], a["peer_v"][0])
        self.tile = [sb(f"gathered{i}", [P, D]) for i in range(RING)]
        self.index = [sb(f"row_index{i}", [P, 1], I32) for i in range(RING)]
        self.rows = sb("expert_rows", [P, SLOTS], I32)
        self.gate = sb("expert_gates", [P, SLOTS])
        self.act = sb("expert_acts", [P, SLOTS])
        self.gel = sb("expert_gelus", [P, SLOTS])
        self.product = sb("gather_product", [P, D])
        self.sum = [sb(f"gather_sum{i}", [P, D]) for i in range(2)]
        self.listed, self.index_ready = sem("rows_listed"), sem("row_index_ready")
        self.loaded = [sem(f"tile_gathered{i}") for i in range(RING)]
        self.used, self.gelu_ready, self.weights_ready = sem("tile_used"), sem("gather_gelu"), sem("gather_weights")

    def start(self, eng, kind, q, j):
        nc, r = self.nc, j % RING
        k = q - kind * SLOTS
        if not (isinstance(q, int) and q < RING):
            eng.wait_ge(self.used, q + (self.FROM + 1 - RING))
        nc.gpsimd.tensor_copy(self.index[r][:, :], self.rows[:, bass.ds(k, 1)]).then_inc(self.index_ready, 1)
        eng.wait_ge(self.index_ready, 2 * q + 1)
        eng.sem_inc(self.index_ready, 1)
        nc.gpsimd.indirect_dma_start(out=self.tile[r][:, :], out_offset=None, in_=self.tables[kind],
                                     in_offset=bass.IndirectOffsetOnAxis(ap=self.index[r][:, 0:1], axis=0),
                                     ).then_inc(self.loaded[r], 16)

    def use(self, eng, kind, q, j, loads):
        V, r = self.nc.vector, j % RING
        k = q - kind * SLOTS
        eng.wait_ge(self.loaded[r], 16 * loads)
        eng.wait_ge(self.used, q + (self.FROM - kind))
        if kind == 0:
            ins = V.scalar_tensor_tensor(out=self.product[:, :], in0=self.tile[r][:, :], scalar=1.0, in1=self.x,
                                         op0=ALU.mult, op1=ALU.mult, accum_out=self.act[:, bass.ds(k, 1)])
        else:
            y = self.sum[j % 2][:, :]
            ins = V.scalar_tensor_tensor(out=y, in0=self.tile[r][:, :], scalar=self.gate[:, bass.ds(k, 1)], in1=y,
                                         op0=ALU.mult, op1=ALU.add)
        ins.then_inc(self.used, 1)

    def weigh(self, eng):
        V = self.nc.vector
        eng.wait_ge(self.gelu_ready, 1)
        V.tensor_tensor(out=self.gate[:, :], in0=self.gate[:, :], in1=self.gel[:, :], op=ALU.mult)
        for y in self.sum:
            ins = V.memset(y[:, :], 0.0)
        ins.then_inc(self.weights_ready, 1)
        eng.wait_ge(self.weights_ready, 1)

    def gelu(self, eng):
        eng.wait_ge(self.used, SLOTS + self.FROM)
        self.nc.scalar.activation(self.gel[:, :], self.act[:, :], ACT.Gelu).then_inc(self.gelu_ready, 1)


def queries(nc, a, sem, bank, h, ident, pB, xhi, xlo, acts, act_dram, top, pos, key):
    V, S, G = nc.vector, nc.scalar, nc.gpsimd
    UB = acts.UB
    with ExitStack() as st:
        sb = lambda name, shape, dt=F32: st.enter_context(nc.sbuf_tensor(name, shape, dt))
        NW = 3
        wq = [sb(f"wq{i}", [P, KD, P]) for i in range(NW)]
        wq_hi = [sb(f"wq_hi{i}", [P, KD, P], F32R) for i in range(2)]
        wq_lo = [sb(f"wq_lo{i}", [P, KD, P], F32R) for i in range(2)]
        keys = sb("keys", [P, 2, P])
        keysT = sb("keysT", [P, 2, P])
        qT = sb("qT", [P, 2, T])
        rep = sb("rep", [P, TB, KEYS])
        best = sb("best", [P, 2, TB, TOPK])
        cand = sb("cand", [P, TB, TOPK, TOPK])
        crep = sb("crep", [P, TB, TOPK * TOPK])

        ln = sb("ln1", [P, 2, D])
        turner = ByChannel(nc, sem, "x", h, bank[4:] + bank[:4], ident, pB[:, PC_LN1_G:PC_LN1_G + KD],
                           pB[:, PC_LN1_B:PC_LN1_B + KD], qT, xhi, xlo)

        wq_loaded = [sem(f"wq_loaded{i}") for i in range(NW)]
        keys_loaded, kt_done, kt_ready = sem("keys_loaded"), sem("keys_transposed"), sem("keysT_ready")
        ln_loaded, pool_chain = sem("ln1_loaded"), sem("pool_chain_queries")
        wq_hi_ready, wq_lo_ready = sem("wq_hi_ready"), sem("wq_lo_ready")
        q_done, qT_ready, s_done, s_used = (sem(n) for n in ("q_done", "qT_ready", "scores_done", "scores_used"))
        chain = sem("dve_chain_queries")

        with nc.Block() as block:
            @block.sync
            def _(eng):
                def load_wq(n):
                    after(eng, wq_lo_ready, n - NW + 1)
                    eng.dma_start(wq[n % NW][:, :, :],
                                  a["peer_wq"][0, :, n * P:(n + 1) * P].rearrange("(k p) c -> p k c", p=P)
                                  ).then_inc(wq_loaded[n % NW], 16)

                for n in range(NW):
                    load_wq(n)
                eng.dma_start(keys[:, 0, :], a["peer_k1"][0]).then_inc(keys_loaded, 16)
                eng.dma_start(keys[:, 1, :], a["peer_k2"][0]).then_inc(keys_loaded, 16)
                for i, name in enumerate(("ln1_g", "ln1_b")):
                    eng.dma_start(ln[:, i, :], a[name][0].partition_broadcast(P)).then_inc(ln_loaded, 16)
                for m in range(UB):
                    acts.load(eng, m, m)
                for n in range(QC):
                    if n + NW < QC:
                        load_wq(n + NW)
                    acts.load_ahead(eng, n, n)
                    acts.store(eng, n, n, act_dram)
                for m in range(QC, BY_QUERIES):
                    acts.load_ahead(eng, m, m)
                    acts.store(eng, m, m, act_dram)

            @block.scalar
            def _(eng):
                def wq_upper(n):
                    eng.wait_ge(wq_loaded[n % NW], 16 * (n // NW + 1))
                    after(eng, q_done, n - 1)
                    S.activation(wq_hi[n % 2][:, :, :], wq[n % NW][:, :, :], ACT.Copy).then_inc(wq_hi_ready, 1)

                wq_upper(0)
                for k in range(KD):
                    turner.shape(eng, k)
                wq_upper(1)
                eng.wait_ge(kt_done, 1)
                S.activation(keysT[:, :, :], bank[6][:, 0:2 * P].rearrange("p (s k) -> p s k", s=2),
                             ACT.Copy).then_inc(kt_ready, 1)
                acts.upper(eng, 0, 0)
                for n in range(QC):
                    eng.wait_ge(q_done, n + 1)
                    after(eng, s_done, n - 1)
                    S.activation(qT[:, n % 2, :], bank[4 + n % 2][:, :], ACT.Copy).then_inc(qT_ready, 1)
                    if n + 2 < QC:
                        wq_upper(n + 2)
                    acts.upper(eng, n + 1, n + 1)
                    acts.gelu_to_store(eng, n, n, n // 2)
                for m in range(QC, BY_QUERIES):
                    acts.upper(eng, m + 1, m + 1)
                    acts.gelu_to_store(eng, m, m, m // 2)

            @block.gpsimd
            def _(eng):
                link = Chain(eng, pool_chain)
                for n in range(QC):
                    if n:
                        acts.lower(eng, n - 1, n - 1)
                    eng.wait_ge(wq_hi_ready, n + 1)
                    G.tensor_tensor(out=wq_lo[n % 2][:, :, :], in0=wq[n % NW][:, :, :],
                                    in1=wq_hi[n % 2][:, :, :].bitcast(F32), op=ALU.subtract).then_inc(wq_lo_ready, 1)
                    if n == 0:
                        eng.wait_ge(ln_loaded, 32)
                        eng.wait_ge(turner.turned, KD)
                    if 0 < n <= TB:
                        blk = h[:, n - 1, :]
                        link(G.tensor_tensor(out=blk, in0=blk, in1=ln[:, 0, :], op=ALU.mult))
                        link(G.tensor_tensor(out=blk, in0=blk, in1=ln[:, 1, :], op=ALU.add))
                for m in range(QC - 1, BY_QUERIES + 1):
                    acts.lower(eng, m, m)

            @block.tensor
            def _(eng):
                mm, tr = nc.tensor.matmul, nc.tensor.transpose
                for tb in range(TB):
                    for k in range(KD):
                        turner.turn(eng, tb, k)

                def scores(n):
                    if n == 0:
                        eng.wait_ge(kt_ready, 1)
                    eng.wait_ge(qT_ready, n + 1)
                    after(eng, s_used, n - 1)
                    for tb in range(TB):
                        ins = mm(bank[6 + n % 2][:, tb * P:(tb + 1) * P], qT[:, n % 2, tb * P:(tb + 1) * P],
                                 keysT[:, n % 2, :], start=True, stop=True)
                    ins.then_inc(s_done, 1)

                for n in range(QC):
                    eng.wait_ge(wq_lo_ready, n + 1)
                    after(eng, qT_ready, n - 1)
                    i = 0
                    for k in range(KD):
                        if n == 0:
                            eng.wait_ge(turner.ready, k + 1)
                        for w, x in ((wq_hi, xhi), (wq_hi, xlo), (wq_lo, xhi)):
                            ins = mm(bank[4 + n % 2][:, :], w[n % 2][:, k, :], x[:, k, :], start=(i == 0),
                                     stop=(i == 3 * KD - 1))
                            i += 1
                    ins.then_inc(q_done, 1)
                    if n == 0:
                        eng.wait_ge(keys_loaded, 32)
                        tr(bank[6][:, 0:P], keys[:, 0, :], ident[:, :])
                        tr(bank[6][:, P:2 * P], keys[:, 1, :], ident[:, :]).then_inc(kt_done, 1)
                        acts.turn(eng, 0, 0, 1)
                    acts.turn(eng, n + 1, n + 1, (n + 1) // UB + 1)
                    acts.product(eng, n, n)
                    scores(n)
                for m in range(QC, BY_QUERIES):
                    acts.turn(eng, m + 1, m + 1, (m + 1) // UB + 1)
                    acts.product(eng, m, m)

            @block.vector
            def _(eng):
                link = Chain(eng, chain)
                for k in range(KD):
                    turner.split(eng, k)

                def top16(src, spare, vals, places):
                    for tb in range(TB):
                        ins = V.max(vals(tb)[:, 0:8], src(tb))
                    link(ins)
                    for tb in range(TB):
                        V.max_index(places(tb)[:, 0:8], vals(tb)[:, 0:8], src(tb))
                        ins = V.match_replace(spare(tb), vals(tb)[:, 0:8], src(tb), NEG)
                    link(ins)
                    for tb in range(TB):
                        ins = V.max(vals(tb)[:, 8:16], spare(tb))
                    link(ins)
                    for tb in range(TB):
                        ins = V.max_index(places(tb)[:, 8:16], vals(tb)[:, 8:16], spare(tb))
                    return ins

                for n in range(QC):
                    q, side = n // 2, n % 2
                    eng.wait_ge(s_done, n + 1)
                    top16(lambda tb: bank[6 + n % 2][:, tb * P:(tb + 1) * P], lambda tb: rep[:, tb, :],
                          lambda tb: best[:, side, tb, :], lambda tb: key[:, tb, q, side, :]).then_inc(s_used, 1)
                    if side == 1:
                        shape = [P, TB, TOPK, TOPK]
                        eng.wait_ge(s_used, n + 1)
                        link(V.tensor_tensor(out=cand[:, :, :, :], in0=best[:, 0, :, :].unsqueeze(3).broadcast_to(shape),
                                             in1=best[:, 1, :, :].unsqueeze(2).broadcast_to(shape), op=ALU.add))
                        link(top16(lambda tb: cand[:, tb, :, :].rearrange("p a b -> p (a b)"), lambda tb: crep[:, tb, :],
                                   lambda tb: top[:, tb, q, :], lambda tb: pos[:, tb, q, :]))


def gates(nc, sem, bank, ident, iota, acts, far, act_dram, top, pos, key, gates_dram):
    V, S = nc.vector, nc.scalar
    NT = 4
    PER = 4
    LOOPS = P // (2 * NT * PER)
    assert LOOPS == GATE_TURNS and LOOPS * PER == BESIDE_TOKENS
    STEPS = P // NT
    PARTS = 7
    assert min(EXTRA[1:] + (CLOSING,)) >= PARTS - 1
    UB = acts.UB
    extra = lambda tb: EXTRA[tb] if tb >= 0 else FIRST
    first_of = lambda tb: BY_QUERIES + FIRST + sum(EXTRA[:tb]) + tb * BESIDE_TOKENS if tb >= 0 else BY_QUERIES
    with ExitStack() as st:
        sb = lambda name, shape, dt=F32: st.enter_context(nc.sbuf_tensor(name, shape, dt))
        stage = sb("stage", [P, KEYS, P])
        place = sb("place", [P, 2, SLOTS], U32)
        placef = sb("placef", [P, 2, SLOTS], BF16)
        keyf = sb("keyf", [P, QH, 2, TOPK], BF16)
        iotab = sb("iotab", [P, TOPK], BF16)
        hit = sb("hit", [P, QH, TOPK, TOPK], BF16)
        sel = sb("sel", [P, 3, SLOTS])
        ex = sb("ex", [P, QH, TOPK])
        total = sb("total", [P, QH])
        selT = sb("selT", [P, 3, P])
        first = sb("first", [P, 2, NT, KEYS])
        second = sb("second", [P, 2, NT, KEYS])

        chain, less_max, exp_ready, sel_ready, selT_done, selT_ready = (sem(n) for n in (
            "dve_chain_gates", "less_max", "exp_ready", "sel_ready", "sel_transposed", "selT_ready"))
        hot_ready, g_done, g_copied, g_stored = (sem(n) for n in (
            "one_hot_ready", "g_done", "g_copied", "g_stored"))

        def beside(eng, tb, step):
            base = first_of(tb)
            for j in range(extra(tb)):
                step(base + j, base + j, None, None)
            if tb < 0:
                return
            with eng.Fori(0, LOOPS) as it:
                for j in range(PER):
                    step(base + extra(tb) + it * PER + j, base + extra(tb) + j, it, j)
            if tb == DT - 1:
                for m in range(MADE - CLOSING, MADE):
                    step(m, m, None, None)

        with nc.Block() as block:
            @block.vector
            def _(eng):
                link = Chain(eng, chain)
                link(V.tensor_copy(iotab[:, :], iota[:, 0:TOPK]))

                def select(tb):
                    heads = [P, QH, TOPK]
                    V.tensor_tensor(out=ex[:, :, :], in0=top[:, tb, :, :], in1=top[:, tb, :, 0:1].broadcast_to(heads),
                                    op=ALU.subtract).then_inc(less_max, 1)
                    p_in = pos[:, tb, :, :].rearrange("p q k -> p (q k)")
                    V.tensor_scalar(out=place[:, 0, :], in0=p_in, scalar1=4, scalar2=None, op0=ALU.logical_shift_right)
                    V.tensor_scalar(out=place[:, 1, :], in0=p_in, scalar1=TOPK - 1, scalar2=None, op0=ALU.bitwise_and)
                    link(V.tensor_copy(keyf[:, :, :, :], key[:, tb, :, :, :]))
                    link(V.tensor_copy(placef[:, :, :], place[:, :, :]))
                    if tb < DT:
                        after(eng, selT_done, tb)
                    for side in range(2):
                        flat = hit[:, :, :, :].rearrange("p q k j -> p (q k) j")
                        shape = [P, SLOTS, TOPK]
                        link(V.tensor_tensor(out=flat, in0=placef[:, side, :].unsqueeze(2).broadcast_to(shape),
                                             in1=iotab[:, :].unsqueeze(1).broadcast_to(shape), op=ALU.is_equal))
                        link(V.tensor_tensor(out=hit[:, :, :, :], in0=hit[:, :, :, :],
                                             in1=keyf[:, :, side, :].unsqueeze(2).broadcast_to([P, QH, TOPK, TOPK]),
                                             op=ALU.mult))
                        link(V.tensor_reduce(sel[:, side, :], flat, AX.X, ALU.add))
                    eng.wait_ge(exp_ready, 1 if tb == DT else tb + 2)
                    link(V.tensor_reduce(total[:, :], ex[:, :, :], AX.X, ALU.add))
                    link(V.reciprocal(total[:, :], total[:, :]))
                    dst = far.gate[:, :] if tb == DT else sel[:, 2, :]
                    ins = V.tensor_tensor(out=dst.rearrange("p (q k) -> p q k", q=QH), in0=ex[:, :, :],
                                          in1=total[:, :].unsqueeze(2).broadcast_to(heads), op=ALU.mult)
                    if tb == DT:
                        link(V.scalar_tensor_tensor(out=far.rows[:, :], in0=sel[:, 0, :], scalar=float(KEYS),
                                                    in1=sel[:, 1, :], op0=ALU.mult, op1=ALU.add))
                        V.sem_inc(far.listed, 1)
                        V.sem_inc(far.used, far.FROM)
                    else:
                        ins.then_inc(sel_ready, 1)

                for tb in range(-1, DT):
                    select(DT if tb < 0 else tb)

                    def step(m, r, it, j):
                        if it is None:
                            return
                        if j == 0:
                            eng.wait_ge(selT_ready, tb + 1)
                        for u in range(2):
                            n = tb * STEPS + it * (2 * PER) + (2 * j + u)
                            t = it * (2 * PER * NT) + (2 * j + u) * NT
                            eng.wait_ge(g_done, n + 1)
                            shape = [P, NT, KEYS]
                            V.tensor_tensor(out=second[:, u, :, :], in0=iota[:, :].unsqueeze(1).broadcast_to(shape),
                                            in1=selT[:, 1, bass.ds(t, NT)].unsqueeze(2).broadcast_to(shape),
                                            op=ALU.is_equal)
                            for q in range(NT):
                                ins = V.tensor_scalar(out=first[:, u, q, :], in0=iota[:, :],
                                                      scalar1=selT[:, 0, bass.ds(t + q, 1)],
                                                      scalar2=selT[:, 2, bass.ds(t + q, 1)], op0=ALU.is_equal, op1=ALU.mult)
                            ins.then_inc(hot_ready, 1)
                        each, q0 = BESIDE[tb] // PER, sum(BESIDE[:tb]) * LOOPS
                        for i in range(j * each, (j + 1) * each):
                            far.use(eng, 0, it * BESIDE[tb] + (q0 + i), i, it * (BESIDE[tb] // RING) + (q0 + i) // RING + 1)

                    beside(eng, tb, step)

            @block.gpsimd
            def _(eng):
                for tb in range(-1, DT):
                    def step(m, r, it, j):
                        if it is None and m == MADE - CLOSING:
                            for q in range(U_FROM + AHEAD, U_FROM + RING):
                                far.start(eng, 0, q, q)
                        acts.lower(eng, m + 1, r + 1)
                        if it is not None:
                            each, q0 = BESIDE[tb] // PER, sum(BESIDE[:tb]) * LOOPS + AHEAD
                            for i in range(j * each, (j + 1) * each):
                                far.start(eng, 0, it * BESIDE[tb] + (q0 + i), q0 + i)

                    beside(eng, tb, step)
                    if tb < 0:
                        eng.wait_ge(far.listed, 1)
                        for q in range(AHEAD):
                            far.start(eng, 0, q, q)

            @block.scalar
            def _(eng):
                eng.sem_inc(g_copied, 2)
                for tb in range(-1, DT):
                    eng.wait_ge(less_max, tb + 2)
                    S.activation(ex[:, :, :], ex[:, :, :], ACT.Exp).then_inc(exp_ready, 1)

                    def step(m, r, it, j):
                        base = first_of(tb) + extra(tb)
                        if it is None:
                            stores = m // 2
                        else:
                            stores = it * (PER // 2) + (base + j) // 2
                        acts.upper(eng, m + 1, r + 1)
                        if it is None and tb >= 0 and m == base - 1:
                            eng.wait_ge(selT_done, tb + 1)
                            after(eng, hot_ready, tb * STEPS)
                            S.activation(selT[:, :, :], bank[6][:, 0:3 * P].rearrange("p (a t) -> p a t", a=3),
                                         ACT.Copy).then_inc(selT_ready, 1)
                            after(eng, g_stored, 16 * PARTS * tb)
                        if it is not None:
                            for u in range(2):
                                n = tb * STEPS + it * (2 * PER) + (2 * j + u)
                                t = it * (2 * PER * NT) + (2 * j + u) * NT
                                eng.wait_ge(g_done, n + 3)
                                S.activation(stage[:, :, bass.ds(t, NT)],
                                             bank[4 + u].rearrange("p (t i) -> p i t", t=NT),
                                             ACT.Copy).then_inc(g_copied, 1)
                        acts.gelu_to_store(eng, m, r, stores)

                    beside(eng, tb, step)

            @block.tensor
            def _(eng):
                eng.sem_inc(g_done, 2)
                for tb in range(-1, DT):
                    def step(m, r, it, j):
                        base = first_of(tb) + extra(tb)
                        acts.turn(eng, m + 1, r + 1, (m + 1) // UB + 1 if it is None else it + (r + 1) // UB + 1)
                        acts.product(eng, m, r)
                        if it is None and tb >= 0 and m == base - 1:
                            eng.wait_ge(sel_ready, tb + 1)
                            after(eng, selT_ready, tb)
                            for i in range(3):
                                ins = nc.tensor.transpose(bank[6][:, i * P:(i + 1) * P], sel[:, i, :], ident[:, :])
                            ins.then_inc(selT_done, 1)
                        if it is None:
                            return
                        for u in range(2):
                            n = tb * STEPS + it * (2 * PER) + (2 * j + u)
                            eng.wait_ge(hot_ready, n + 1)
                            eng.wait_ge(g_copied, n + 1)
                            for q in range(NT):
                                ins = nc.tensor.matmul(bank[4 + u][:, q * KEYS:(q + 1) * KEYS], second[:, u, q, :],
                                                       first[:, u, q, :], start=True, stop=True)
                            ins.then_inc(g_done, 1)

                    beside(eng, tb, step)

            @block.sync
            def _(eng):
                def store_gates(tb, i):
                    if i == 0:
                        eng.wait_ge(g_copied, (tb + 1) * STEPS + 2)
                    for part in (0, 1) if i == 0 else (i + 1,) if i + 1 < PARTS else ():
                        at = slice(part * KEYS // PARTS, (part + 1) * KEYS // PARTS)
                        eng.dma_start(gates_dram[at, :, tb * P:(tb + 1) * P].rearrange("i j t -> j i t"),
                                      stage[:, at, :]).then_inc(g_stored, 16)

                for tb in range(-1, DT):
                    def step(m, r, it, j):
                        if it is None and m >= MADE - CLOSING:
                            store_gates(DT - 1, m - (MADE - CLOSING))
                        elif it is None and tb > 0:
                            store_gates(tb - 1, m - first_of(tb))
                        acts.load_ahead(eng, m, r)
                        acts.store(eng, m, r, act_dram)

                    beside(eng, tb, step)
                eng.wait_ge(g_stored, 16 * PARTS * DT)
                for i in range(2):
                    eng.wait_ge(acts.stored[i], 16 * (MADE // 2))


def experts(nc, a, sem, bank, h, small, acts, far, act_dram, gates_dram, out):
    V, S, G = nc.vector, nc.scalar, nc.gpsimd
    SLOT = 4
    TURN = 2 * SLOT
    TURNS = (KEYS - MADE) // SLOT
    TAIL = TURNS * TURN
    STEPS = KEYS
    GATHERS = 2 * TURN
    u_turns = (SLOTS - U_FROM) // GATHERS
    v_turns = TURNS - u_turns
    tail_tiles = SLOTS - v_turns * GATHERS
    assert TURNS * SLOT == KEYS - MADE and GATHERS % RING == 0 and 2 < u_turns < TURNS - 1
    assert u_turns * GATHERS == SLOTS - U_FROM and 0 <= tail_tiles <= STEPS - TAIL
    LAST = (DT, *range(DT))
    LEFT, RIGHT = slice(0, 6 * P), slice(6 * P, D)
    is_live = lambda n, i: i % 2 == 0 and (not isinstance(n, int) or n < TAIL)

    q_of = lambda n: 2 * SLOTS - tail_tiles + n - TAIL

    def block_of(n):
        if n >= TAIL:
            return n - TURNS * SLOT
        return n // TURN * SLOT + n % TURN // 2 + (MADE if n % 2 == 0 else 0)

    with ExitStack() as st:
        sb = lambda name, shape, dt=F32: st.enter_context(nc.sbuf_tensor(name, shape, dt))
        v_raw = [sb(f"v_raw{i}", [P, D]) for i in range(SLOT)]
        g_in = [sb(f"g_in{i}", [P, DTOK]) for i in range(SLOT)]
        a_in = [sb(f"a_in{i}", [P, DTOK]) for i in range(2)]
        v_hi = [sb(f"v_hi{i}", [P, D], F32R) for i in range(SLOT)]
        v_lo = [sb(f"v_lo{i}", [P, D], F32R) for i in range(SLOT)]
        w32 = sb("w32", [P, 2, DTOK])
        w_hi = [sb(f"w_hi{i}", [P, DTOK], F32R) for i in range(SLOT)]
        w_lo = [sb(f"w_lo{i}", [P, DTOK], F32R) for i in range(SLOT)]
        ln = sb("ln2", [P, 2, D])
        bn = sb("bn2", [P, TB, 2, 6])
        mv = sb("mv2", [P, TB, 2])
        rs = sb("rs2", [P, TB, 1])
        shift = sb("shift2", [P, TB, 1])

        v_loaded = [sem(f"v_loaded{i}") for i in range(SLOT)]
        g_loaded = [sem(f"g_loaded{i}") for i in range(SLOT)]
        a_loaded = [sem(f"a_loaded{i}") for i in range(2)]
        w_made, w_hi_ready, w_lo_ready, v_hi_ready, v_lo_ready = (sem(n) for n in (
            "w_made", "w_hi_ready", "w_lo_ready", "v_hi_ready", "v_lo_ready"))
        y_done = sem("y_step_done")
        ln2_loaded, var_ready, rstd_ready, norm_ready, stored = (sem(n) for n in (
            "ln2_loaded", "var2_ready", "rstd2_ready", "norm2_ready", "out_stored"))
        y_ready, left_ready, right_ready = sem("y_block_ready"), sem("out_left_ready"), sem("out_right_ready")
        chain, pool_chain = sem("dve_chain_experts"), sem("pool_chain_experts")

        def steps(eng, step, between=lambda: None):
            def turn(t, kind, then):
                def tiles(i):
                    for j in range(2 * i, 2 * i + 2):
                        yield (kind if i < TURN else then, t * GATHERS + (U_FROM + j), j,
                               t * (GATHERS // RING) + (U_FROM + j) // RING + 1)

                for i in range(TURN):
                    step(t * TURN + i, i, t, tiles)

            turn(0, 0, 0)
            with eng.Fori(1, u_turns - 1) as t:
                turn(t, 0, 0)
            turn(u_turns - 1, 0, 1)
            between()
            with eng.Fori(u_turns, TURNS - 1) as t:
                turn(t, 1, 1)
            turn(TURNS - 1, 1, None)
            for n in range(TAIL, STEPS):
                q = q_of(n)
                step(n, n % TURN, None, lambda i: [(1, q, q, q // RING + 1)] if q < 2 * SLOTS else [])

        def affine(eng, engine, link, at, cols, ready):
            blk = h[:, LAST[at], cols]
            eng.wait_ge(norm_ready, at + 1)
            link(engine.tensor_tensor(out=blk, in0=blk, in1=ln[:, 0, cols], op=ALU.mult))
            engine.tensor_tensor(out=blk, in0=blk, in1=ln[:, 1, cols], op=ALU.add).then_inc(ready, 1)

        v_rows = a["peer_v"][0]
        g_rows = gates_dram.rearrange("i j t -> (i j) t")
        rows = lambda b: slice(b * P, (b + 1) * P) if isinstance(b, int) else bass.ds(b * P, P)

        with nc.Block() as block:
            @block.sync
            def _(eng):
                def load_v(i, b):
                    eng.dma_start(v_raw[i % SLOT][:, :], v_rows[rows(b), :]).then_inc(v_loaded[i % SLOT], 16)

                def load_g(i, b):
                    eng.dma_start(g_in[i % SLOT][:, :], g_rows[rows(b), :]).then_inc(g_loaded[i % SLOT], 16)

                def load_a(i, b):
                    eng.dma_start(a_in[i % 2][:, :], act_dram[rows(b), :]).then_inc(a_loaded[i % 2], 16)

                for n in range(SLOT):
                    load_v(n, block_of(n))
                    load_g(n, block_of(n))
                for k in range(2):
                    load_a(k, k)
                eng.dma_start(ln[:, 0, :], a["ln2_g"][0].partition_broadcast(P)).then_inc(ln2_loaded, 16)
                eng.dma_start(ln[:, 1, :], a["ln2_b"][0].partition_broadcast(P)).then_inc(ln2_loaded, 16)

                def step(n, i, t, tiles):
                    live = is_live(n, i)
                    static = isinstance(n, int)
                    if static and n + SLOT >= STEPS:
                        ahead = None
                    elif static:
                        ahead = block_of(n + SLOT)
                    else:
                        ahead = t * SLOT + (i // 2 + 2 + (MADE if live else 0))
                    if live and not (static and MADE + t * SLOT + i // 2 + acts.UB >= KEYS):
                        acts.load_ahead(eng, t * SLOT + (MADE + i // 2), MADE + i // 2)
                    if ahead is not None:
                        eng.wait_ge(v_lo_ready, n + 1)
                        load_v(i, ahead)
                    eng.wait_ge(w_made, n + 1)
                    if ahead is not None:
                        load_g(i, ahead)
                    if not live:
                        k = i // 2 if not (static and n >= TAIL) else block_of(n)
                        if static and block_of(n) + 2 < MADE:
                            load_a(k, block_of(n) + 2)
                        elif not static:
                            load_a(k, t * SLOT + i // 2 + 2)

                steps(eng, step)
                for at, tb in enumerate(LAST):
                    for cols, ready in ((RIGHT, right_ready), (LEFT, left_ready)):
                        eng.wait_ge(ready, at + 1)
                        eng.dma_start(out[0, tb * P:(tb + 1) * P, cols], h[:, tb, cols]).then_inc(stored, 16)
                eng.wait_ge(stored, 2 * 16 * TB)

            @block.tensor
            def _(eng):
                mm = nc.tensor.matmul

                def outputs(n, i):
                    first, last = (isinstance(n, int) and n == e for e in (0, STEPS - 1))
                    r = i % SLOT
                    eng.wait_ge(v_lo_ready, n + 1)
                    eng.wait_ge(w_lo_ready, n + 1)
                    for tb in range(DT):
                        for w, v, begins, ends in ((w_hi, v_hi, first, False), (w_hi, v_lo, False, False),
                                                   (w_lo, v_hi, False, last)):
                            for half in range(2):
                                ins = mm(bank[2 + 2 * tb + half][:, :], w[r][:, tb * P:(tb + 1) * P],
                                         v[r][:, half * HALF_D:(half + 1) * HALF_D], start=begins, stop=ends)
                        if last:
                            ins.then_inc(y_ready, 1)
                    if not last:
                        ins.then_inc(y_done, 1)

                def step(n, i, t, tiles):
                    if is_live(n, i):
                        m, r = t * SLOT + (MADE + i // 2), MADE + i // 2
                        more = not (isinstance(m, int) and m + 1 == KEYS)
                        if more:
                            acts.turn_half(eng, 0, m + 1, r + 1, (r + 1) // acts.UB + 1 + t, 0, 0)
                        acts.product(eng, m, r, 1, 0)
                        if more:
                            acts.turn_half(eng, 1, m + 1, r + 1, (r + 1) // acts.UB + 1 + t, 0, 0)
                    if not (isinstance(n, int) and n == 0):
                        outputs(n - 1, i - 1)

                steps(eng, step)
                outputs(STEPS - 1, STEPS - 1)

            @block.scalar
            def _(eng):
                def v_upper(n, i, t_loads):
                    r = i % SLOT
                    eng.wait_ge(v_loaded[r], 16 * t_loads)
                    if not (isinstance(n, int) and n < SLOT):
                        eng.wait_ge(y_done, n - SLOT + 1)
                    S.activation(v_hi[r][:, :], v_raw[r][:, :], ACT.Copy).then_inc(v_hi_ready, 1)

                def step(n, i, t, tiles):
                    live = is_live(n, i)
                    m, r = (t * SLOT + (MADE + i // 2), MADE + i // 2) if live else (0, 0)
                    more = live and not (isinstance(m, int) and m + 1 == KEYS)
                    if more:
                        acts.upper_half(eng, 0, m + 1, r + 1, 0)
                    if not (isinstance(n, int) and n + 2 >= STEPS):
                        loads = (n + 2) // SLOT + 1 if isinstance(n, int) else t * (TURN // SLOT) + (i + 2) // SLOT + 1
                        v_upper(n + 2, i + 2, loads)
                    if live:
                        if isinstance(n, int) and n < 4:
                            eng.wait_ge(acts.stored[r % 2], 16 * (MADE // 2))
                        else:
                            eng.wait_ge(w_made, n - 3)
                        acts.gelu(eng, m, r, 1)
                    eng.wait_ge(w_made, n + 1)
                    S.activation(w_hi[i % SLOT][:, :], w32[:, i % 2, :], ACT.Copy).then_inc(w_hi_ready, 1)
                    if more:
                        acts.upper_half(eng, 1, m + 1, r + 1, 0)

                v_upper(0, 0, 1)
                v_upper(1, 1, 1)
                steps(eng, step, between=lambda: far.gelu(eng))
                for at, tb in enumerate(LAST):
                    eng.wait_ge(rstd_ready, at + 1)
                    S.activation(h[:, tb, :], h[:, tb, :], ACT.Identity, scale=rs[:, tb, :],
                                 bias=shift[:, tb, :]).then_inc(norm_ready, 1)

            @block.gpsimd
            def _(eng):
                def v_lower(n, i):
                    r = i % SLOT
                    eng.wait_ge(v_hi_ready, n + 1)
                    G.tensor_tensor(out=v_lo[r][:, :], in0=v_raw[r][:, :], in1=v_hi[r][:, :].bitcast(F32),
                                    op=ALU.subtract).then_inc(v_lo_ready, 1)

                def start(tiles):
                    for kind, q, j, _ in tiles:
                        if not (isinstance(q, int) and q < U_FROM + RING):
                            far.start(eng, kind, q, j)

                def step(n, i, t, tiles):
                    if t is None:
                        ahead = q_of(n) + 2
                        for q in range(q_of(n) if n == TAIL else ahead, min(ahead + 1, 2 * SLOTS)):
                            far.start(eng, 1, q, q)
                    elif not (isinstance(n, int) and n + 1 == TAIL):
                        start(tiles(i + 1))
                    if not (isinstance(n, int) and n + 2 >= STEPS):
                        v_lower(n + 2, i + 2)

                v_lower(0, 0)
                v_lower(1, 1)
                steps(eng, step)
                eng.wait_ge(far.index_ready, 2 * 2 * SLOTS)
                link = Chain(eng, pool_chain)
                eng.wait_ge(ln2_loaded, 32)
                for at in range(TB + 1):
                    if at < TB:
                        tb = LAST[at]
                        eng.wait_ge(var_ready, at + 1)
                        link(G.tensor_tensor(out=rs[:, tb, :], in0=mv[:, tb, 1:2], in1=small[:, 2:3], op=ALU.add))
                        link(G.tensor_tensor(out=rs[:, tb, :], in0=rs[:, tb, :], in1=small[:, 0:1], op=ALU.pow))
                        link(G.tensor_tensor(out=shift[:, tb, :], in0=mv[:, tb, 0:1], in1=rs[:, tb, :], op=ALU.mult))
                        G.tensor_tensor(out=shift[:, tb, :], in0=shift[:, tb, :], in1=small[:, 1:2],
                                        op=ALU.mult).then_inc(rstd_ready, 1)
                    if at:
                        affine(eng, G, link, at - 1, RIGHT, right_ready)

            @block.vector
            def _(eng):
                def step(n, i, t, tiles):
                    live = is_live(n, i)
                    m, r = (t * SLOT + (MADE + i // 2), MADE + i // 2) if live else (0, 0)
                    more = live and not (isinstance(m, int) and m + 1 == KEYS)
                    if more:
                        acts.lower_half(eng, 0, m + 1, r + 1, 0)
                    for kind, q, j, loads in tiles(i):
                        far.use(eng, kind, q, j, loads)
                    if live:
                        eng.wait_ge(acts.ready, m + 1)
                        act = acts.gel[:, r % 2, :]
                    else:
                        k = i // 2 if t is not None else block_of(n)
                        loads = block_of(n) // 2 + 1 if isinstance(n, int) else t * (SLOT // 2) + k // 2 + 1
                        eng.wait_ge(a_loaded[k % 2], 16 * loads)
                        act = a_in[k % 2][:, :]
                    loads = n // SLOT + 1 if isinstance(n, int) else t * (TURN // SLOT) + i // SLOT + 1
                    eng.wait_ge(g_loaded[i % SLOT], 16 * loads)
                    V.tensor_tensor(out=w32[:, i % 2, :], in0=act, in1=g_in[i % SLOT][:, :],
                                    op=ALU.mult).then_inc(w_made, 1)
                    eng.wait_ge(w_hi_ready, n + 1)
                    V.tensor_tensor(out=w_lo[i % SLOT][:, :], in0=w32[:, i % 2, :], in1=w_hi[i % SLOT][:, :].bitcast(F32),
                                    op=ALU.subtract).then_inc(w_lo_ready, 1)
                    if more:
                        acts.lower_half(eng, 1, m + 1, r + 1, 0)

                steps(eng, step, between=lambda: far.weigh(eng))
                link = Chain(eng, chain)
                eng.wait_ge(ln2_loaded, 32)
                link(V.scalar_tensor_tensor(out=h[:, DT, :], in0=h[:, DT, :], scalar=ALPHA, in1=far.sum[0][:, :],
                                            op0=ALU.mult, op1=ALU.add))
                link(V.tensor_tensor(out=h[:, DT, :], in0=h[:, DT, :], in1=far.sum[1][:, :], op=ALU.add))
                for at in range(TB + 1):
                    if at < TB:
                        tb = LAST[at]
                        if at:
                            eng.wait_ge(y_ready, at)
                            for i in range(2):
                                blk = h[:, tb, i * HALF_D:(i + 1) * HALF_D]
                                ins = V.scalar_tensor_tensor(out=blk, in0=blk, scalar=ALPHA, in1=bank[2 + 2 * tb + i][:, :],
                                                             op0=ALU.mult, op1=ALU.add)
                            link(ins)
                        for i in range(2):
                            ins = V.bn_stats(bn[:, tb, i, :], h[:, tb, i * HALF_D:(i + 1) * HALF_D])
                        link(ins)
                        V.bn_aggr(mv[:, tb, :], bn[:, tb, :, :].rearrange("p a b -> p (a b)")).then_inc(var_ready, 1)
                    if at:
                        affine(eng, V, link, at - 1, LEFT, left_ready)


_INS = ["x", "ln_emb_g", "ln_emb_b", "w_in", "lru_conv_w", "lru_conv_b", "lru_wa", "lru_ba", "lru_wx", "lru_bx",
        "lru_lambda", "conv_w", "norm_lru_g", "norm_conv_g", "w_out", "ln1_g", "ln1_b",
        "peer_wq", "peer_k1", "peer_k2", "peer_u", "peer_v", "ln2_g", "ln2_b"]


def kernel(**inputs):
    import concourse.bacc as bacc
    from concourse.bass_utils import run_bass_kernel_spmd

    nc = bacc.Bacc("TRN2", target_bir_lowering=False, num_devices=1)
    arrays, args = {}, {}
    for name in _INS:
        v = np.ascontiguousarray(inputs[name])
        arrays[f"in_{name}"] = v
        args[name] = nc.dram_tensor(f"in_{name}", v.shape, F32, kind="ExternalInput").ap()
    out = nc.dram_tensor("out_0", (1, T, D), F32, kind="ExternalOutput").ap()
    gates_dram = nc.dram_tensor("gate_matrix", (KEYS, KEYS, DTOK), F32, kind="Internal").ap()
    act_dram = nc.dram_tensor("activations", (MADE * P, DTOK), F32, kind="Internal").ap()
    build(nc, args, out, gates_dram, act_dram)
    r = run_bass_kernel_spmd(nc, [arrays], core_ids=[0])
    return r.results[0]["out_0"]
```
